# Optimizing a Trainium2 kernel written in Bass

```python
import math
import jax, jax.numpy as jnp
from jax import lax
import numpy as np

D_MODEL = 1024
BATCH = 1
SEQ = 1024
DEPTH = 2
DEC_BATCH = 1
DEC_SEQ = 32
PAST_LEN = 512

CHUNK = 64
QBLK = 128
PLE_DIM = 256
ROPE_THETA = 500000.0
EPS = 1e-6
NEG_INF = -1e30
A_HEADS = 8
A_DH = 64
A_WIDTH = A_HEADS * 2 * A_DH
A_ROT = A_DH // 4
B_HEADS = 16
B_DH = 64
B_WIDTH = B_HEADS * B_DH
N_A = (DEPTH + 1) // 2
N_B = DEPTH // 2

kernel_name = 'hybrid_diffattn_stickbreak_stream_step'

def _rmsnorm(x, g):
    xf = x.astype(jnp.float32)
    y = xf * lax.rsqrt(jnp.mean(xf * xf, axis=-1, keepdims=True) + EPS)
    return (y * g.astype(jnp.float32)).astype(x.dtype)

def _rope(x, pos):
    half = A_ROT // 2
    inv = ROPE_THETA ** (-jnp.arange(half, dtype=jnp.float32) * 2.0 / A_ROT)
    ang = pos.astype(jnp.float32)[:, None] * inv[None, :]
    shape = (1, x.shape[1]) + (1,) * (x.ndim - 3) + (half,)
    c = jnp.cos(ang).reshape(shape)
    s = jnp.sin(ang).reshape(shape)
    xf = x.astype(jnp.float32)
    x1 = xf[..., :half]
    x2 = xf[..., half:A_ROT]
    out = jnp.concatenate([x1 * c - x2 * s, x2 * c + x1 * s, xf[..., A_ROT:]], axis=-1)
    return out.astype(x.dtype)

def _sweep(block_fn, q, q_pos):
    b, t = q.shape[:2]
    if t <= QBLK:
        return block_fn(q, q_pos)
    nb = t // QBLK
    qb = jnp.moveaxis(q.reshape((b, nb, QBLK) + q.shape[2:]), 1, 0)
    pb = q_pos.reshape(nb, QBLK)
    ob = lax.map(lambda a: block_fn(a[0], a[1]), (qb, pb))
    return jnp.moveaxis(ob, 0, 1).reshape((b, t) + ob.shape[3:])

def _with_past(new, past, pos):
    if past is None:
        return new, pos
    k_pos = jnp.concatenate([jnp.arange(past.shape[1], dtype=jnp.int32), pos])
    return jnp.concatenate([past.astype(new.dtype), new], axis=1), k_pos

def _diff_attn(h, pos, w_in, lq1, lk1, lq2, lk2, sub_g, w_out, lam_init, k_past, v_past):
    b, t, _ = h.shape
    q, k, v, g = jnp.split(h @ w_in, 4, axis=-1)
    q = _rope(q.reshape(b, t, A_HEADS, 2, A_DH), pos)
    k = _rope(k.reshape(b, t, A_HEADS, 2, A_DH), pos)
    v = v.reshape(b, t, A_HEADS, 2 * A_DH)
    k_all, k_pos = _with_past(k, k_past, pos)
    v_all, _ = _with_past(v, v_past, pos)
    f32 = jnp.float32
    lam = (jnp.exp(jnp.sum(lq1.astype(f32) * lk1.astype(f32)))
           - jnp.exp(jnp.sum(lq2.astype(f32) * lk2.astype(f32))) + lam_init)
    kf = k_all.astype(f32)
    vf = v_all.astype(f32)
    k_chunk = k_pos // CHUNK

    def block(qb, qpb):
        s = jnp.einsum('bqhcd,bkhcd->bhcqk', qb.astype(f32), kf) * (A_DH ** -0.5)
        mask = k_chunk[None, :] <= (qpb // CHUNK)[:, None]
        pr = jax.nn.softmax(jnp.where(mask, s, NEG_INF), axis=-1)
        w = pr[:, :, 0] - lam * pr[:, :, 1]
        return jnp.einsum('bhqk,bkhe->bqhe', w, vf)

    o = _sweep(block, q, pos)
    o = _rmsnorm(o, sub_g) * (1.0 - lam_init)
    o = o.reshape(b, t, A_WIDTH).astype(h.dtype) * jax.nn.silu(g)
    return o @ w_out, k, v

def _stick_breaking(h, pos, w_in, w_out, k_past, v_past):
    b, t, _ = h.shape
    q, k, v, g = jnp.split(h @ w_in, 4, axis=-1)
    q = q.reshape(b, t, B_HEADS, B_DH)
    k = k.reshape(b, t, B_HEADS, B_DH)
    v = v.reshape(b, t, B_HEADS, B_DH)
    k_all, k_pos = _with_past(k, k_past, pos)
    v_all, _ = _with_past(v, v_past, pos)
    f32 = jnp.float32
    kf = k_all.astype(f32)
    vf = v_all.astype(f32)

    def block(qb, qpb):
        z = jnp.einsum('bqhd,bkhd->bhqk', qb.astype(f32), kf) * (B_DH ** -0.5)
        valid = k_pos[None, :] < qpb[:, None]
        log_keep = jnp.where(valid, jax.nn.log_sigmoid(-z), 0.0)
        after = lax.cumsum(log_keep, axis=3, reverse=True) - log_keep
        a = jnp.where(valid, jnp.exp(jax.nn.log_sigmoid(z) + after), 0.0)
        return jnp.einsum('bhqk,bkhd->bqhd', a, vf)

    o = _sweep(block, q, pos)
    o = o.reshape(b, t, B_WIDTH).astype(h.dtype) * jax.nn.silu(g)
    return o @ w_out, k, v

def _trunk(x, p, pos, a_norm_g, a_w_in, a_lam_q1, a_lam_k1, a_lam_q2, a_lam_k2, a_subln_g, a_w_out,
           b_norm_g, b_w_in, b_w_out, ple_w_proj, ple_w_gate, final_norm_g,
           a_k_past, a_v_past, b_k_past, b_v_past):
    ak, av, bk, bv = [], [], [], []
    for i in range(DEPTH):
        j = i // 2
        if i % 2 == 0:
            lam_init = 0.8 - 0.6 * math.exp(-0.3 * i)
            y, k, v = _diff_attn(_rmsnorm(x, a_norm_g[j]), pos, a_w_in[j], a_lam_q1[j], a_lam_k1[j],
                                 a_lam_q2[j], a_lam_k2[j], a_subln_g[j], a_w_out[j], lam_init,
                                 None if a_k_past is None else a_k_past[j],
                                 None if a_v_past is None else a_v_past[j])
            ak.append(k)
            av.append(v)
        else:
            y, k, v = _stick_breaking(_rmsnorm(x, b_norm_g[j]), pos, b_w_in[j], b_w_out[j],
                                      None if b_k_past is None else b_k_past[j],
                                      None if b_v_past is None else b_v_past[j])
            bk.append(k)
            bv.append(v)
        x = x + y
        x = x + jax.nn.sigmoid(x @ ple_w_gate[i]) * (p[i] @ ple_w_proj[i])
    return _rmsnorm(x, final_norm_g), jnp.stack(ak), jnp.stack(av), jnp.stack(bk), jnp.stack(bv)

def setup_inputs(seed: int = 0) -> dict:
    key = jax.random.key(seed)
    ks = jax.random.split(key, 24)
    f32 = jnp.float32

    def nrm(k, shape, scale=1.0):
        return jax.random.normal(k, shape, f32) * scale

    return {
        'x_prompt': nrm(ks[0], (BATCH, SEQ, D_MODEL)),
        'x_sample': nrm(ks[1], (DEC_BATCH, DEC_SEQ, D_MODEL)),
        'cache_a_k': nrm(ks[2], (N_A, DEC_BATCH, PAST_LEN, A_HEADS, 2, A_DH)),
        'cache_a_v': nrm(ks[3], (N_A, DEC_BATCH, PAST_LEN, A_HEADS, 2 * A_DH)),
        'cache_b_k': nrm(ks[4], (N_B, DEC_BATCH, PAST_LEN, B_HEADS, B_DH)),
        'cache_b_v': nrm(ks[5], (N_B, DEC_BATCH, PAST_LEN, B_HEADS, B_DH)),
        'p_prompt': nrm(ks[6], (DEPTH, BATCH, SEQ, PLE_DIM)),
        'p_sample': nrm(ks[7], (DEPTH, DEC_BATCH, DEC_SEQ, PLE_DIM)),
        'a_norm_g': 1.0 + nrm(ks[8], (N_A, D_MODEL), 0.02),
        'a_w_in': nrm(ks[9], (N_A, D_MODEL, 4 * A_WIDTH), D_MODEL ** -0.5),
        'a_lam_q1': nrm(ks[10], (N_A, A_DH), 0.1),
        'a_lam_k1': nrm(ks[11], (N_A, A_DH), 0.1),
        'a_lam_q2': nrm(ks[12], (N_A, A_DH), 0.1),
        'a_lam_k2': nrm(ks[13], (N_A, A_DH), 0.1),
        'a_subln_g': 1.0 + nrm(ks[14], (N_A, 2 * A_DH), 0.02),
        'a_w_out': nrm(ks[15], (N_A, A_WIDTH, D_MODEL), A_WIDTH ** -0.5),
        'b_norm_g': 1.0 + nrm(ks[16], (N_B, D_MODEL), 0.02),
        'b_w_in': nrm(ks[17], (N_B, D_MODEL, 4 * B_WIDTH), D_MODEL ** -0.5),
        'b_w_out': nrm(ks[18], (N_B, B_WIDTH, D_MODEL), B_WIDTH ** -0.5),
        'ple_w_proj': nrm(ks[19], (DEPTH, PLE_DIM, D_MODEL), PLE_DIM ** -0.5),
        'ple_w_gate': nrm(ks[20], (DEPTH, D_MODEL, D_MODEL), D_MODEL ** -0.5),
        'final_norm_g': 1.0 + nrm(ks[21], (D_MODEL,), 0.02),
    }

def reference(x_prompt, x_sample, cache_a_k, cache_a_v, cache_b_k, cache_b_v, p_prompt, p_sample,
              a_norm_g, a_w_in, a_lam_q1, a_lam_k1, a_lam_q2, a_lam_k2, a_subln_g, a_w_out,
              b_norm_g, b_w_in, b_w_out, ple_w_proj, ple_w_gate, final_norm_g):
    pos_p = jnp.arange(x_prompt.shape[1], dtype=jnp.int32)
    pos_s = cache_a_k.shape[2] + jnp.arange(x_sample.shape[1], dtype=jnp.int32)
    y_prompt, ak_p, av_p, bk_p, bv_p = _trunk(
        x_prompt, p_prompt, pos_p, a_norm_g, a_w_in, a_lam_q1, a_lam_k1, a_lam_q2, a_lam_k2,
        a_subln_g, a_w_out, b_norm_g, b_w_in, b_w_out, ple_w_proj, ple_w_gate, final_norm_g,
        None, None, None, None)
    y_sample, ak_s, av_s, bk_s, bv_s = _trunk(
        x_sample, p_sample, pos_s, a_norm_g, a_w_in, a_lam_q1, a_lam_k1, a_lam_q2, a_lam_k2,
        a_subln_g, a_w_out, b_norm_g, b_w_in, b_w_out, ple_w_proj, ple_w_gate, final_norm_g,
        cache_a_k, cache_a_v, cache_b_k, cache_b_v)
    return (y_prompt, y_sample, ak_p, av_p, bk_p, bv_p, ak_s, av_s, bk_s, bv_s)


_drawn_inputs = setup_inputs


def setup_inputs(seed=0):
    import zlib

    import numpy as np

    out = dict(_drawn_inputs(seed))
    spreads = {}
    factors = {'a_norm_g': 2.985,
     'a_lam_q1': 8.0,
     'a_subln_g': 7.198,
     'b_norm_g': 8.066,
     'final_norm_g': 7.545,
     'cache_a_v': 2.882,
     'cache_b_k': 2.742,
     'a_lam_q2': 3.006}
    for name, (base, spread) in spreads.items():
        noise = np.random.default_rng([zlib.crc32(name.encode()), seed]).standard_normal(out[name].shape)
        drawn = base * np.exp(spread * noise) if base else spread * noise
        out[name] = __import__('jax').numpy.asarray(drawn.astype(out[name].dtype))
    for name, factor in factors.items():
        out[name] = (out[name] * factor).astype(out[name].dtype)
    return out
```

```python
import math
from contextlib import ExitStack

import numpy as np

import concourse.bass as bass
from concourse import mybir

F32 = mybir.dt.float32
F32R = mybir.dt.float32r
ACT = mybir.ActivationFunctionType
ALU = mybir.AluOpType
AX = mybir.AxisListType

P = 128
D = 1024
KT = D // P
SEQ, DEC, PAST = 1024, 32, 512
ROWS = SEQ + DEC
NT = SEQ // P
PADDED = SEQ + P
GROUPS = D // P
DH = 64
STAGES = 4
PB = PAST // P
PLE = 256
PT = PLE // P
CHUNK = 64
EPS = 1e-6
QC = 512
NEG = -1e30
CLAMP = 80.0
SOFT_MAX = 40.0
CHUNKS = [(0, QC), (QC, QC), (SEQ, DEC)]
TILES = [(t, P) for t in range(NT)] + [(NT, DEC)]


CREDIT = 1


class Count:

    def __init__(self, per, r):
        self.per, self.r, self.seen = per, r, {}

    def nth(self, x, k):
        return self.r * self.per[x] + k + CREDIT

    def before(self, x):
        return self.nth(x, 0)

    def all(self, x):
        return self.nth(x, self.per[x])

    def next(self, x):
        self.seen[x] = self.seen.get(x, 0) + 1
        return self.nth(x, self.seen[x])


def semaphores(nc, ctx, name, per):
    made = {x: nc.alloc_semaphore(f"{name}_{x}") for x in per}
    sems = list(made.values())

    def give_back():
        nc.clear_and_free_semaphores(sems)
        nc.all_engine_barrier()
    ctx.callback(give_back)
    return made


def start_credits(eng, S):
    for sem in S.values():
        eng.sem_inc(sem, CREDIT)


def three(pe, out, a, b, start, stop, **kw):
    pairs = [(a[0], b[0]), (a[1], b[0]), (a[0], b[1])]
    for n, (x, y) in enumerate(pairs):
        last = pe.matmul(out, x, y, start=start and n == 0, stop=stop and n == 2, **kw)
    return last


def norm_phase(nc, top, name, x_in, gain, ident, h, y_out=None):
    with ExitStack() as ctx:
        sb = lambda n, s, dt=F32: ctx.enter_context(nc.sbuf_tensor(f"{name}_{n}", s, dt))
        xt = sb("xt", [P, 2, D])
        hn = sb("hn", [P, 2, D])
        sq = sb("sq", [P, D])
        ss = sb("ss", [P, 2])
        rstd = sb("rstd", [P, 2])
        gb = sb("gb", [P, D])
        ps = ctx.enter_context(nc.psum_tensor(f"{name}_ps", [P, 2, KT, P], F32))
        per = {"gain": 16, "x_even": 16, "x_odd": 16, "sum": 2, "mean": 2, "log": 2, "rstd": 2, "h": 2,
            "turned": 2, "high": 2, "low": 2, "stored_even": 16, "stored_odd": 16, "fill": 1}
        S = semaphores(nc, ctx, name, per)
        loaded, stored = ("x_even", "x_odd"), ("stored_even", "stored_odd")
        block = ctx.enter_context(nc.Block())

        def rounds(eng, tile):
            with eng.Fori(0, NT // 2) as i:
                for u in range(2):
                    tile(Count(per, i), 2 * i + u, u, P)
            tile(Count(per, NT // 2), NT, 0, DEC)

        @block.sync
        def _(sp):
            sp.dma_start(gb[:, :], gain.to_broadcast([P, D])).then_inc(S["gain"], 16)

            def load(at, t, u, n):
                sp.wait_ge(S["h"], at.nth("h", u - 1))
                sp.dma_start(xt[0:n, u, :], x_in[bass.ds(t * P, n), :]).then_inc(S[loaded[u]], 16)
            rounds(sp, load)
            if y_out is not None:
                sp.wait_ge(S["stored_even"], 16 * (NT // 2 + 1) + CREDIT)
                sp.wait_ge(S["stored_odd"], 16 * (NT // 2) + CREDIT)

        @block.scalar
        def _(act):
            act.preload_act_table_set("natural_log_exp_and_others")
            act.wait_ge(S["fill"], 1 + 1)

            def tile(at, t, u, n):
                act.wait_ge(S[loaded[u]], at.nth(loaded[u], 16))
                act.activation(sq[0:n, :], xt[0:n, u, :], ACT.Square,
                               accum_out=ss[0:n, u:u + 1]).then_inc(S["sum"], 1)
                act.wait_ge(S["mean"], at.nth("mean", u + 1))
                act.activation(ss[0:n, u:u + 1], ss[0:n, u:u + 1], ACT.Ln).then_inc(S["log"], 1)
                act.wait_ge(S["log"], at.nth("log", u + 1))
                act.activation(rstd[0:n, u:u + 1], ss[0:n, u:u + 1], ACT.Exp,
                               scale=-0.5).then_inc(S["rstd"], 1)
                if y_out is None:
                    act.wait_ge(S["turned"], at.nth("turned", u + 1))
                    act.activation(h[0][:, :, bass.ds(t * P, n)], ps[:, u, :, 0:n],
                                   ACT.Copy).then_inc(S["high"], 1)
                else:
                    act.wait_ge(S["h"], at.nth("h", u + 1))
                    act.dma_start(y_out[bass.ds(t * P, n), :], hn[0:n, u, :]).then_inc(S[stored[u]], 16)
            rounds(act, tile)

        @block.vector
        def _(dve):
            start_credits(dve, S)
            dve.drain().then_inc(S["fill"], 1)
            dve.wait_ge(S["gain"], 16 + 1)

            def tile(at, t, u, n):
                dve.wait_ge(S["sum"], at.nth("sum", u + 1))
                dve.tensor_scalar(ss[0:n, u:u + 1], ss[0:n, u:u + 1], 1.0 / D, EPS, ALU.mult,
                                  ALU.add).then_inc(S["mean"], 1)
                dve.wait_ge(S["rstd"], at.nth("rstd", u + 1))
                if y_out is None:
                    dve.wait_ge(S["low"], at.nth("low", u - 1))
                else:
                    dve.wait_ge(S[stored[u]], at.before(stored[u]))
                dve.scalar_tensor_tensor(out=hn[0:n, u, :], in0=xt[0:n, u, :], scalar=rstd[0:n, u:u + 1],
                                         in1=gb[0:n, :], op0=ALU.mult, op1=ALU.mult).then_inc(S["h"], 1)
                if y_out is None:
                    dve.wait_ge(S["high"], at.nth("high", u + 1))
                    cols = bass.ds(t * P, n)
                    dve.tensor_tensor(h[1][:, :, cols], ps[:, u, :, 0:n], h[0][:, :, cols].bitcast(F32),
                                      ALU.subtract).then_inc(S["low"], 1)
            rounds(dve, tile)

        if y_out is None:
            @block.tensor
            def _(pe):
                def tile(at, t, u, n):
                    pe.wait_ge(S["h"], at.nth("h", u + 1))
                    pe.wait_ge(S["low"], at.nth("low", u - 1))
                    for k in range(KT):
                        last = pe.transpose(ps[:, u, k, 0:n], hn[0:n, u, k * P:(k + 1) * P], ident[0:n, 0:n])
                    last.then_inc(S["turned"], 1)
                rounds(pe, tile)


def attention_layer(nc, top, name, h, w_in, k_past, v_past, k_out, v_out, o_dram, consts, core):
    ident = consts["ident"]
    with ExitStack() as ctx:
        sb = lambda n, s, dt=F32: ctx.enter_context(nc.sbuf_tensor(f"{name}_{n}", s, dt))
        pb = lambda n, s: ctx.enter_context(nc.psum_tensor(f"{name}_{n}", s, F32))
        w = [sb("w_high", [P, KT, QC], F32R), sb("w_low", [P, KT, QC], F32R)]
        stage = sb("stage", [P, STAGES, QC])
        tok = sb("tok", [P, NT + 1, 3 * P])
        qk = [sb("qk_high", [P, 2, PADDED], F32R), sb("qk_low", [P, 2, PADDED], F32R)]
        kp = sb("kp", [P, PB, P])
        vp = sb("vp", [P, PB, P])
        kpt = [sb("kpt_high", [P, PAST], F32R), sb("kpt_low", [P, PAST], F32R)]
        gate = sb("gate", [P, ROWS])
        gtmp = sb("gtmp", [P, QC])
        o = sb("o", [P, ROWS])
        pj = pb("pj", [P, 3, 512])
        acc = pb("acc", [P, 512])
        sc = pb("sc", [P, 4, 512])
        table = dict(past=32, w_high=KT, w_low=KT, tok_ready=9, pj_tok=9, turned=10, turned_high=10,
                     turned_low=10, tok_stored=64, g_ready=3, g_clamped=3, g_exp=3, g_done=3, pv=3,
                     o_ready=3, pe_tick=0, fill=1)
        table.update({f"w_loaded{s}": 16 * KT // STAGES for s in range(STAGES)})
        table.update({f"o_stored{c}": 16 for c in range(3)})
        table.update(core.TABLE)
        S = semaphores(nc, ctx, name, table)
        rows_ready = core.ROWS
        B = dict(tok=tok, qk=qk, kpt=kpt, vp=vp, gate=gate, gtmp=gtmp, o=o, pj=pj, acc=acc, sc=sc,
                 ident=ident, **core.memory(sb))
        block = ctx.enter_context(nc.Block())

        def groups(eng, body):
            with eng.Fori(0, GROUPS - 1) as r:
                body(r, True)
            body(GROUPS - 1, False)

        def load_w(sp, g, k):
            sp.dma_start(stage[:, k % STAGES, :], w_in[bass.ds(g, 1), k * P:(k + 1) * P, :]
                         .rearrange("o p n -> p (o n)")).then_inc(S[f"w_loaded{k % STAGES}"], 16)

        def split_w_high(act, g, k):
            act.wait_ge(S[f"w_loaded{k % STAGES}"], Count(table, g).nth(f"w_loaded{k % STAGES}", 16 * (k // STAGES + 1)))
            act.activation(w[0][:, k, :], stage[:, k % STAGES, :], ACT.Copy).then_inc(S["w_high"], 1)

        def split_w_low(dve, g, k):
            dve.wait_ge(S["w_high"], Count(table, g).nth("w_high", k + 1))
            dve.tensor_tensor(w[1][:, k, :], stage[:, k % STAGES, :], w[0][:, k, :].bitcast(F32),
                              ALU.subtract).then_inc(S["w_low"], 1)

        @block.sync
        def _(sp):
            sp.wait_ge(S["fill"], 1 + 1)
            for k in range(KT):
                if k >= STAGES:
                    sp.wait_ge(S["w_low"], k - STAGES + 1 + 1)
                load_w(sp, 0, k)

            def body(r, more):
                at = Count(table, r)
                sp.wait_ge(S["pv"], at.before("pv"))
                sp.wait_ge(S["turned_high"], at.before("turned_high"))
                for buf, past in ((kp, k_past), (vp, v_past)):
                    sp.dma_start(buf[:, :, :], past[:, bass.ds(r * P, P)].rearrange("(b p) f -> p b f", p=P)
                                 ).then_inc(S["past"], 16)
                if more:
                    for k in range(KT):
                        sp.wait_ge(S["w_low"], Count(table, r + 1).nth("w_low", k - STAGES + 1))
                        if k == STAGES:
                            send_rows(r, at)
                        load_w(sp, r + 1, k)
                else:
                    send_rows(r, at)
                for c, (c0, cn) in enumerate(CHUNKS):
                    sp.wait_ge(S["o_ready"], at.next("o_ready"))
                    sp.dma_start(o_dram[bass.ds(r, 1), :, c0:c0 + cn].rearrange("o p n -> p (o n)"),
                                 o[:, c0:c0 + cn]).then_inc(S[f"o_stored{c}"], 16)

            def send_rows(r, at):
                sp.wait_ge(S[rows_ready], at.nth(rows_ready, 9))
                for n, out in ((1, k_out), (2, v_out)):
                    cols = slice(n * P, (n + 1) * P)
                    sp.dma_start(out[0:SEQ, bass.ds(r * P, P)].rearrange("(t p) f -> p t f", p=P),
                                 tok[:, 0:NT, cols]).then_inc(S["tok_stored"], 16)
                    sp.dma_start(out[SEQ:ROWS, bass.ds(r * P, P)],
                                 tok[0:DEC, NT, cols]).then_inc(S["tok_stored"], 16)
            groups(sp, body)
            sp.wait_ge(S["tok_stored"], 64 * GROUPS + 1)
            for c in range(3):
                sp.wait_ge(S[f"o_stored{c}"], 16 * GROUPS + 1)

        two = acc[:, 0:2 * P].rearrange("p (a n) -> p a n", a=2)

        @block.scalar
        def _(act):
            act.preload_act_table_set("natural_log_exp_and_others")
            act.wait_ge(S["fill"], 1 + 1)
            for k in range(KT):
                split_w_high(act, 0, k)

            def body(r, more):
                at = Count(table, r)
                act.wait_ge(S["tok_stored"], at.before("tok_stored"))
                act.wait_ge(S["pv"], at.before("pv"))

                def turned_high(n):
                    act.wait_ge(S["turned"], at.next("turned"))
                    if n <= NT:
                        t, m = TILES[n]
                        out, src = qk[0][:, :, t * P:t * P + m], two[:, :, 0:m]
                    else:
                        out, src = kpt[0][:, :], acc[:, :]
                    act.activation(out, src, ACT.Copy).then_inc(S["turned_high"], 1)

                def g_exp(c):
                    c0, cn = CHUNKS[c]
                    act.wait_ge(S["g_clamped"], at.next("g_clamped"))
                    act.activation(gate[:, c0:c0 + cn], gtmp[:, 0:cn], ACT.Exp, scale=-1.0).then_inc(S["g_exp"], 1)

                for t, n in TILES:
                    act.wait_ge(S["pj_tok"], at.next("pj_tok"))
                    act.activation(tok[0:n, t, 0:P], pj[0:n, t % 2, 0:P], ACT.Copy, scale=DH ** -0.5)
                    act.activation(tok[0:n, t, P:], pj[0:n, t % 2, P:3 * P], ACT.Copy).then_inc(S["tok_ready"], 1)
                    if t >= 2:
                        turned_high(t - 2)
                g_exp(0)
                turned_high(NT - 1)
                g_exp(1)
                turned_high(NT)
                turned_high(NT + 1)
                g_exp(2)

                def next_weights(k):
                    if more:
                        if k == 0:
                            act.wait_ge(S["g_ready"], at.all("g_ready"))
                        split_w_high(act, r + 1, k)
                core.scalar(act, at, S, B, next_weights)
            groups(act, body)

        @block.vector
        def _(dve):
            start_credits(dve, S)
            dve.memset(qk[0][:, :, ROWS:].bitcast(F32), 0.0)
            dve.memset(qk[1][:, :, ROWS:].bitcast(F32), 0.0)
            for q in range(DEC, P, DEC):
                dve.memset(tok[q:q + DEC, NT, :], 0.0)
            core.prepare(dve, B)
            dve.drain().then_inc(S["fill"], 1)
            for k in range(KT):
                split_w_low(dve, 0, k)

            def body(r, more):
                at = Count(table, r)

                def turned_low(n):
                    dve.wait_ge(S["turned_high"], at.next("turned_high"))
                    if n <= NT:
                        t, m = TILES[n]
                        cols = slice(t * P, t * P + m)
                        out, sub, src = qk[1][:, :, cols], qk[0][:, :, cols], two[:, :, 0:m]
                    else:
                        out, sub, src = kpt[1][:, :], kpt[0][:, :], acc[:, :]
                    dve.tensor_tensor(out, src, sub.bitcast(F32), ALU.subtract).then_inc(S["turned_low"], 1)

                def clamp_gate(c):
                    c0, cn = CHUNKS[c]
                    dve.wait_ge(S["g_ready"], at.next("g_ready"))
                    dve.tensor_scalar(gtmp[:, 0:cn], pj[:, 2, 0:cn], -CLAMP, None, ALU.max).then_inc(S["g_clamped"], 1)

                def finish_gate(c):
                    c0, cn = CHUNKS[c]
                    g = gate[:, c0:c0 + cn]
                    dve.wait_ge(S["g_exp"], at.next("g_exp"))
                    dve.tensor_scalar(g, g, 1.0, None, ALU.add).then_inc(S["dve_link"], 1)
                    dve.wait_ge(S["dve_link"], at.next("dve_link"))
                    dve.reciprocal(g, g).then_inc(S["dve_link"], 1)
                    dve.wait_ge(S["dve_link"], at.next("dve_link"))
                    dve.tensor_tensor(g, pj[:, 2, 0:cn], g, ALU.mult).then_inc(S["g_done"], 1)

                for n in range(NT - 1):
                    turned_low(n)
                clamp_gate(0)
                finish_gate(0)
                turned_low(NT - 1)
                clamp_gate(1)
                finish_gate(1)
                turned_low(NT)
                turned_low(NT + 1)
                clamp_gate(2)
                finish_gate(2)

                def next_weights(k):
                    if more:
                        split_w_low(dve, r + 1, k)
                core.vector(dve, at, S, B, next_weights)
            groups(dve, body)

        @block.gpsimd
        def _(pool):
            pool.wait_ge(S["fill"], 1 + 1)

            def body(r, more):
                at = Count(table, r)
                core.gpsimd(pool, at, S, B)
            groups(pool, body)

        @block.tensor
        def _(pe):
            pe.wait_ge(S["fill"], 1 + 1)

            def body(r, more):
                at = Count(table, r)
                pe.wait_ge(S["w_low"], at.all("w_low"))
                pe.wait_ge(S[core.PJ_LEFT], at.before(core.PJ_LEFT))

                def project(t, n):
                    pe.wait_ge(S["tok_ready"], at.nth("tok_ready", t - 1))
                    rows = slice(t * P, t * P + n)
                    for k in range(KT):
                        last = three(pe, pj[0:n, t % 2, 0:3 * P], [x[:, k, rows] for x in h],
                                     [x[:, k, 0:3 * P] for x in w], k == 0, k == KT - 1)
                    last.then_inc(S["pj_tok"], 1)

                def turn(n):
                    if n == 0:
                        pe.wait_ge(S["o_ready"], at.before("o_ready"))
                    pe.wait_ge(S["turned_low"], at.nth("turned_low", n))
                    if n <= NT:
                        pe.wait_ge(S[rows_ready], at.nth(rows_ready, n + 1))
                        t, m = TILES[n]
                        if m < P:
                            pe.sem_inc(S["pe_tick"], 1)
                        for a in range(2):
                            last = pe.transpose(acc[:, a * P:a * P + m], tok[0:m, t, a * P:(a + 1) * P],
                                                ident[0:m, 0:m])
                    else:
                        pe.wait_ge(S["past"], at.nth("past", 32))
                        for b in range(PB):
                            last = pe.transpose(acc[:, b * P:(b + 1) * P], kp[:, b, :], ident[:, :])
                    last.then_inc(S["turned"], 1)

                for t, n in TILES:
                    project(t, n)
                    if t >= 2:
                        turn(t - 2)
                for c, (c0, cn) in enumerate(CHUNKS):
                    pe.wait_ge(S["g_done"], at.nth("g_done", c))
                    if c == 0:
                        pe.wait_ge(S[core.G_LEFT], at.before(core.G_LEFT))
                    for k in range(KT):
                        last = three(pe, pj[:, 2, 0:cn], [x[:, k, 3 * P:] for x in w],
                                     [x[:, k, c0:c0 + cn] for x in h], k == 0, k == KT - 1)
                    last.then_inc(S["g_ready"], 1)
                    if c < 2:
                        turn(NT - 1 + c)
                    if c == 1:
                        turn(NT + 1)
                pe.wait_ge(S["turned_low"], at.all("turned_low"))
                pe.wait_ge(S["tok_ready"], at.all("tok_ready"))
                core.tensor(pe, at, S, B)
            groups(pe, body)


class DifferentialAttention:

    UNITS = [(qb * P, P, (qb + 1) * P) for qb in range(NT)] + [(SEQ, DEC, PAST + DEC)]
    CHUNK_END = {3: 0, 7: 1, 8: 2}
    ROWS, PJ_LEFT, G_LEFT = "rope", "moved", "rstd"
    TABLE = dict(rope=9, pool_link=9, scores=18, neg_max=18, probs=18, weights=9, w_turned=14, moved=14,
                 squared=3, var=3, log=3, rstd=3, dve_link=6 + 34 + 27 + 3)

    def __init__(self, lam, gain, cos, sin):
        self.neg_lam, self.gain, self.cos, self.sin = lam, gain, cos, sin

    def memory(self, sb):
        return dict(p=[[sb(f"p{u}{c}", [P, SEQ]) for c in range(2)] for u in range(2)],
                    wt=sb("wt", [P, NT, QC]), mean=sb("mean", [P, P]), eps=sb("eps", [P, 1]),
                    mx=sb("mx", [P, 2, 2]), nm=sb("nm", [P, 2, 2]), sums=sb("sums", [P, 2, 2]),
                    ra=sb("ra", [P, 2, 4, 16]))

    def prepare(self, dve, B):
        dve.memset(B["mean"][:, :], 1.0 / P)
        dve.memset(B["eps"][:, :], EPS)

    def groups_of(self, u):
        if u == NT:
            return [(0, PB, P), (PB, 1, DEC)]
        return [(k, min(4, u + 1 - k), P) for k in range(0, u + 1, 4)]

    def gpsimd(self, pool, at, S, B):
        tok, ra = B["tok"], B["ra"]
        for t, n in TILES:
            pool.wait_ge(S["tok_ready"], at.next("tok_ready"))
            pool.wait_ge(S["rope"], at.nth("rope", t))
            x = tok[0:n, t, 0:2 * P].rearrange("p (c d) -> p c d", d=DH)
            xc, xs = ra[0:n, 0], ra[0:n, 1]
            pool.tensor_tensor(xc, x[:, :, 0:16], self.cos[0:n, t], ALU.mult)
            pool.tensor_tensor(xs, x[:, :, 0:16], self.sin[0:n, t], ALU.mult).then_inc(S["pool_link"], 1)
            pool.wait_ge(S["pool_link"], at.next("pool_link"))
            pool.tensor_tensor(x[:, :, 0:8], xc[:, :, 0:8], xs[:, :, 8:16], ALU.subtract)
            pool.tensor_tensor(x[:, :, 8:16], xc[:, :, 8:16], xs[:, :, 0:8], ALU.add).then_inc(S["rope"], 1)

    def tensor(self, pe, at, S, B):
        sc, pj, acc, wt, p = B["sc"], B["pj"], B["acc"], B["wt"], B["p"]
        ring = [0]

        def score(u, c):
            q0, n, nk = self.UNITS[u]
            if u:
                pe.wait_ge(S["probs"], at.nth("probs", 2 * u + c - 1))
            else:
                pe.wait_ge(S["probs"], at.before("probs"))
            if n < P:
                pe.sem_inc(S["pe_tick"], 1)
            f = slice(c * DH, (c + 1) * DH)
            keys = [([x[f, 0:PAST] for x in B["kpt"]], 0, PAST), ([x[f, 1, SEQ:ROWS] for x in B["qk"]], PAST, DEC)
                    ] if u == NT else [([x[f, 1, k:min(k + 512, nk)] for x in B["qk"]], k, min(512, nk - k))
                                       for k in range(0, nk, 512)]
            for rhs, k, kn in keys:
                last = three(pe, sc[0:n, 2 * c + k // 512, k % 512:k % 512 + kn],
                             [x[f, 0, q0:q0 + n] for x in B["qk"]], rhs, True, True)
            last.then_inc(S["scores"], 1)

        def turn_weights(u):
            q0, n, nk = self.UNITS[u]
            pe.wait_ge(S["weights"], at.nth("weights", u + 1))
            for k0, nb, rows in self.groups_of(u):
                if ring[0] >= 2:
                    pe.wait_ge(S["moved"], at.nth("moved", ring[0] - 1))
                if n < P:
                    pe.sem_inc(S["pe_tick"], 1)
                bank = pj[0:rows, ring[0] % 2, 0:nb * n].rearrange("p (b n) -> p b n", n=n)
                for b in range(nb):
                    k = (k0 + b) * P
                    last = pe.transpose(bank[:, b, :], p[u % 2][0][0:n, k:k + rows], B["ident"][0:n, 0:n])
                last.then_inc(S["w_turned"], 1)
                ring[0] += 1

        def values(c):
            c0, cn = CHUNKS[c]
            if c == 0:
                pe.wait_ge(S["o_ready"], at.before("o_ready"))
            else:
                pe.wait_ge(S["o_ready"], at.nth("o_ready", c))
            pe.wait_ge(S["moved"], at.nth("moved", sum(len(self.groups_of(u)) for u in range({0: 4, 1: 8, 2: 9}[c]))))
            if c == 2:
                for b in range(PB):
                    pe.matmul(acc[:, 0:cn], B["vp"][:, b, :], wt[:, b, 0:cn], start=b == 0, stop=False)
                last = pe.matmul(acc[:, 0:cn], B["tok"][0:DEC, NT, 2 * P:], wt[0:DEC, PB, 0:cn],
                                 start=False, stop=True)
            else:
                blocks = 4 * (c + 1)
                for b in range(blocks):
                    q = max(0, b * P - c0)
                    last = pe.matmul(acc[:, q:], B["tok"][:, b, 2 * P:], wt[:, b, q:],
                                     start=b == 0, stop=b == blocks - 1)
            last.then_inc(S["pv"], 1)

        def variance(c):
            cn = CHUNKS[c][1]
            pe.wait_ge(S["squared"], at.next("squared"))
            if c == 0:
                pe.wait_ge(S["g_done"], at.all("g_done"))
            else:
                pe.wait_ge(S["rstd"], at.nth("rstd", c))
            pe.matmul(pj[:, 2, 0:cn], B["mean"][:, :], B["gtmp"][:, 0:cn], start=True, stop=True).then_inc(S["var"], 1)

        for u in range(NT + 1):
            for c in range(2):
                score(u, c)
            if u >= 1:
                turn_weights(u - 1)
                if u - 1 in self.CHUNK_END:
                    values(self.CHUNK_END[u - 1])
            if u == 5:
                variance(0)
        variance(1)
        turn_weights(NT)
        values(2)
        variance(2)

    def scalar(self, act, at, S, B, next_weights):
        p, sc, wt = B["p"], B["sc"], B["wt"]
        ring = [0]

        def probs(u, c):
            q0, n, nk = self.UNITS[u]
            if u >= 2:
                act.wait_ge(S["w_turned"], at.nth("w_turned", sum(len(self.groups_of(x)) for x in range(u - 1))))
            act.wait_ge(S["neg_max"], at.next("neg_max"))
            act.activation(p[u % 2][c][0:n, 0:nk],
                                  sc[0:n, 2 * c:2 * c + 2, :].rearrange("p a n -> p (a n)")[:, 0:nk],
                                  ACT.Exp, bias=B["nm"][0:n, u % 2, c:c + 1],
                                  accum_out=B["sums"][0:n, u % 2, c:c + 1]).then_inc(S["probs"], 1)

        def move(u):
            q0, n, nk = self.UNITS[u]
            if u in (4, 8):
                act.wait_ge(S["pv"], at.nth("pv", u // 4))
            off = q0 % QC
            for k0, nb, rows in self.groups_of(u):
                act.wait_ge(S["w_turned"], at.next("w_turned"))
                bank = B["pj"][0:rows, ring[0] % 2, 0:nb * n].rearrange("p (b n) -> p b n", n=n)
                act.activation(wt[0:rows, k0:k0 + nb, off:off + n], bank, ACT.Copy).then_inc(S["moved"], 1)
                ring[0] += 1

        def norm(c):
            c0, cn = CHUNKS[c]
            act.wait_ge(S["pv"], at.next("pv"))
            act.wait_ge(S["g_exp"], at.all("g_exp"))
            act.activation(B["gtmp"][:, 0:cn], B["acc"][:, 0:cn], ACT.Square).then_inc(S["squared"], 1)
            act.wait_ge(S["var"], at.next("var"))
            act.wait_ge(S[f"o_stored{c}"], at.before(f"o_stored{c}"))
            r = B["o"][:, c0:c0 + cn]
            act.activation(r, B["pj"][:, 2, 0:cn], ACT.Ln, bias=B["eps"][:, 0:1]).then_inc(S["log"], 1)
            act.wait_ge(S["log"], at.next("log"))
            act.activation(r, r, ACT.Exp, scale=-0.5).then_inc(S["rstd"], 1)

        for u in range(NT + 1):
            for c in range(2):
                probs(u, c)
            if u == 5:
                norm(0)
            if u >= 1:
                move(u - 1)
                next_weights(u - 1)
        norm(1)
        move(NT)
        norm(2)

    def vector(self, dve, at, S, B, next_weights):
        sc, p, mx, nm, sums = B["sc"], B["p"], B["mx"], B["nm"], B["sums"]

        def maxima(u, c):
            q0, n, nk = self.UNITS[u]
            dve.wait_ge(S["scores"], at.next("scores"))
            s = sc[0:n, 2 * c:2 * c + 2, :].rearrange("p a n -> p (a n)")[:, 0:nk]
            if u < NT:
                dve.memset(s[0:CHUNK, nk - CHUNK:nk], NEG).then_inc(S["dve_link"], 1)
                dve.wait_ge(S["dve_link"], at.next("dve_link"))
            dve.reduce_max(mx[0:n, u % 2, c:c + 1], s, AX.X).then_inc(S["dve_link"], 1)
            dve.wait_ge(S["dve_link"], at.next("dve_link"))
            dve.tensor_scalar(nm[0:n, u % 2, c:c + 1], mx[0:n, u % 2, c:c + 1], -1.0, None, ALU.mult).then_inc(S["neg_max"], 1)

        def combine(u):
            q0, n, nk = self.UNITS[u]
            dve.wait_ge(S["probs"], at.next("probs"))
            dve.wait_ge(S["probs"], at.next("probs"))
            s, a, b = sums[0:n, u % 2], p[u % 2][0][0:n, 0:nk], p[u % 2][1][0:n, 0:nk]
            dve.reciprocal(s, s).then_inc(S["dve_link"], 1)
            dve.wait_ge(S["dve_link"], at.next("dve_link"))
            dve.tensor_scalar(s[:, 1:2], s[:, 1:2], self.neg_lam[0:n, 0:1], None, ALU.mult).then_inc(S["dve_link"], 1)
            dve.wait_ge(S["dve_link"], at.next("dve_link"))
            dve.tensor_scalar(b, b, s[:, 1:2], None, ALU.mult).then_inc(S["dve_link"], 1)
            dve.wait_ge(S["dve_link"], at.next("dve_link"))
            dve.scalar_tensor_tensor(out=a, in0=a, scalar=s[:, 0:1], in1=b, op0=ALU.mult, op1=ALU.add).then_inc(S["weights"], 1)

        def finish(c):
            c0, cn = CHUNKS[c]
            out = B["o"][:, c0:c0 + cn]
            dve.wait_ge(S["rstd"], at.next("rstd"))
            dve.tensor_tensor(out, B["acc"][:, 0:cn], out, ALU.mult).then_inc(S["dve_link"], 1)
            dve.wait_ge(S["dve_link"], at.next("dve_link"))
            dve.scalar_tensor_tensor(out=out, in0=out, scalar=self.gain[:, 0:1],
                                            in1=B["gate"][:, c0:c0 + cn], op0=ALU.mult, op1=ALU.mult).then_inc(S["o_ready"], 1)

        for u in range(NT + 1):
            for c in range(2):
                maxima(u, c)
            if u >= 1:
                combine(u - 1)
                next_weights(u - 1)
            if u == 5:
                finish(0)
        combine(NT)
        finish(1)
        finish(2)


class StickBreaking:

    UNITS = [(c, b, hd) for c in range(2) for b in reversed(range(4 * (c + 1))) for hd in range(2)] + [(2, 0, 0)]
    N = len(UNITS)
    SLOTS = 4
    SB = PB + 1
    SN = SB * DEC
    ROWS, PJ_LEFT, G_LEFT = "tok_ready", "pv", "g_done"
    DIAG = sum(c < 2 and b >= 4 * c for c, b, _ in UNITS)
    TABLE = dict(z=N, clamped=N, exp=N, log=N, soft=N, after=N, a=N, running=24 - 4, r_zero=2, dve_link=6 + DIAG + 5)

    def __init__(self, masks):
        self.masks = masks

    def memory(self, sb):
        return dict(m=[sb(f"m{i}", [P, QC]) for i in range(3)], s=[sb(f"s{i}", [P, QC]) for i in range(4)],
                    a=[sb(f"a{i}", [P, QC]) for i in range(4)], r=sb("r", [P, 2, 2, QC]),
                    rs=sb("rs", [P, 2, PB, DEC]), hide=sb("hide", [P, P], F32R),
                    unit=sb("unit", [P, P], F32R))

    def prepare(self, dve, B):
        dve.tensor_scalar(B["hide"][:, :], self.masks["strict"][:, :], -1.0, -NEG, ALU.add, ALU.mult)
        dve.tensor_copy(B["unit"][:, :], B["ident"][:, :])

    def span(self, s):
        c, b, hd = self.UNITS[s]
        q = max(0, b * P - c * QC)
        return q, QC - q, b >= 4 * c

    def views(self, s, B):
        if self.UNITS[s][0] == 2:
            first = s % self.SLOTS
            assert first + 1 < self.SLOTS
            wide = lambda x: x[:, 0:2 * self.SN].rearrange("p (h n) -> p h n", h=2)
            return B["sc"][:, first:first + 2, 0:self.SN], wide(B["m"][s % 3]), wide(B["s"][s % 4]), wide(B["a"][s % 4])
        q, n, _ = self.span(s)
        return tuple(x[:, q:q + n] for x in (B["sc"][:, s % self.SLOTS, :], B["m"][s % 3], B["s"][s % 4], B["a"][s % 4]))

    def last_of(self, c):
        return max(s for s, x in enumerate(self.UNITS) if x[0] == c)

    def running_before(self, s):
        return sum(self.UNITS[x][0] < 2 and self.UNITS[x][1] > 0 for x in range(s))

    def tensor(self, pe, at, S, B):
        sc, acc, qk = B["sc"], B["acc"], B["qk"]
        tri, ones = self.masks["neg_tri"], self.masks["neg_ones"]

        def scores(s):
            c, b, hd = self.UNITS[s]
            slot = sc[:, s % self.SLOTS, :]
            if s >= self.SLOTS:
                pe.wait_ge(S["a"], at.nth("a", s - self.SLOTS + 1 + (c == 2)))
            else:
                pe.wait_ge(S["a"], at.before("a"))
            if c == 2:
                for b in range(self.SB):
                    for hd in range(2):
                        f = slice(hd * DH, (hd + 1) * DH)
                        keys = [x[f, b * P:(b + 1) * P] for x in B["kpt"]] if b < PB else [x[f, 1, SEQ:] for x in qk]
                        last = three(pe, self.views(s, B)[0][:, hd, b * DEC:(b + 1) * DEC], keys,
                                     [x[f, 0, SEQ:ROWS] for x in qk], b == 0, True, skip_group_check=True)
            else:
                q, n, _ = self.span(s)
                f = slice(hd * DH, (hd + 1) * DH)
                c0 = c * QC
                last = three(pe, slot[:, q:], [x[f, 1, b * P:(b + 1) * P] for x in qk],
                             [x[f, 0, c0 + q:c0 + QC] for x in qk], True, True, skip_group_check=True)
            last.then_inc(S["z"], 1)

        def after(s):
            c, b, hd = self.UNITS[s]
            slot, _, sp, _ = self.views(s, B)
            add = dict(start=False, stop=True, skip_group_check=True)
            pe.wait_ge(S["soft"], at.nth("soft", s + 1))
            if c == 2:
                for hd in range(2):
                    pe.matmul(slot[:, hd, PB * DEC:], B["unit"][:, :], B["hide"][:, 0:DEC], **add)
                    pe.matmul(slot[:, hd, 0:PB * DEC], ones[:, :], B["rs"][:, hd].rearrange("p b n -> p (b n)"), **add)
                    last = pe.matmul(slot[:, hd, :], tri[:, :], sp[:, hd, :], **add)
            else:
                q, n, masked = self.span(s)
                if masked:
                    pe.matmul(slot[:, 0:P], B["unit"][:, :], B["hide"][:, :], **add)
                if b < 4 * c + 3:
                    pe.wait_ge(S["running"], at.nth("running", self.running_before(s - 1)))
                    pe.matmul(slot, ones[:, :], B["r"][:, c, hd, q:], **add)
                last = pe.matmul(slot, tri[:, :], sp, **add)
            last.then_inc(S["after"], 1)

        def values(s):
            c, b, hd = self.UNITS[s]
            a = B["a"][s % 4]
            pe.wait_ge(S["a"], at.nth("a", s + 1))
            if s in (0, self.last_of(0) + 1, self.last_of(1) + 1):
                if c == 0:
                    pe.wait_ge(S["o_ready"], at.before("o_ready"))
                else:
                    pe.wait_ge(S["o_ready"], at.nth("o_ready", c))
            if c == 2:
                for b in range(self.SB):
                    for hd in range(2):
                        f = slice(hd * DH, (hd + 1) * DH)
                        v = B["vp"][:, b, f] if b < PB else B["tok"][:, NT, 2 * P + hd * DH:2 * P + (hd + 1) * DH]
                        col = hd * self.SN + b * DEC
                        last = pe.matmul(acc[f, 0:DEC], v, a[:, col:col + DEC], start=b == 0,
                                         stop=b == PB, skip_group_check=True)
            else:
                q = self.span(s)[0]
                f = slice(hd * DH, (hd + 1) * DH)
                last = pe.matmul(acc[f, q:], B["tok"][:, b, 2 * P + hd * DH:2 * P + (hd + 1) * DH], a[:, q:],
                                 start=b == 4 * c + 3, stop=b == 0, skip_group_check=True)
            if s == self.last_of(c):
                last.then_inc(S["pv"], 1)

        for s in range(self.N + 3):
            if s < self.N:
                scores(s)
            if 2 <= s < self.N + 2:
                after(s - 2)
            if s >= 3:
                values(s - 3)

    def scalar(self, act, at, S, B, next_weights):
        for s in range(self.N + 2):
            if s < self.N:
                m = self.views(s, B)[1]
                act.wait_ge(S["clamped"], at.next("clamped"))
                act.activation(m, m, ACT.Exp).then_inc(S["exp"], 1)
                act.wait_ge(S["exp"], at.next("exp"))
                act.activation(m, m, ACT.Ln, bias=1.0).then_inc(S["log"], 1)
            if s >= 2:
                j = s - 2
                slot, _, _, a = self.views(j, B)
                act.wait_ge(S["after"], at.next("after"))
                act.activation(a, slot, ACT.Exp).then_inc(S["a"], 1)
            if 3 <= s < 3 + 2 * KT and s % 2:
                next_weights((s - 3) // 2)

    def vector(self, dve, at, S, B, next_weights):
        strict, strict_sample = self.masks["strict"], self.masks["strict_sample"]
        dve.wait_ge(S["running"], at.before("running"))
        dve.wait_ge(S["after"], at.before("after"))
        for c in range(2):
            dve.memset(B["r"][:, c, :, :], 0.0).then_inc(S["r_zero"], 1)

        def softplus(s):
            c = self.UNITS[s][0]
            masked = c == 2 or self.span(s)[2]
            slot, m, sp, _ = self.views(s, B)
            dve.wait_ge(S["log"], at.next("log"))
            if s >= 4:
                dve.wait_ge(S["after"], at.nth("after", s - 3))
                dve.wait_ge(S["running"], at.nth("running", self.running_before(s - 3)))
            ins = dve.tensor_tensor(sp, slot, m, ALU.max)
            if not masked:
                ins.then_inc(S["soft"], 1)
            elif c < 2:
                ins.then_inc(S["dve_link"], 1)
                dve.wait_ge(S["dve_link"], at.next("dve_link"))
                dve.tensor_tensor(sp[:, 0:P], sp[:, 0:P], strict[:, :], ALU.mult).then_inc(S["soft"], 1)
            else:
                ins.then_inc(S["dve_link"], 1)
                dve.wait_ge(S["dve_link"], at.next("dve_link"))
                new = sp[:, :, PB * DEC:]
                dve.tensor_tensor(new, new, strict_sample[:, :, :], ALU.mult).then_inc(S["dve_link"], 1)
                dve.wait_ge(S["dve_link"], at.next("dve_link"))
                rs = B["rs"]
                dve.tensor_copy(rs[:, :, PB - 1, :], new).then_inc(S["dve_link"], 1)
                dve.wait_ge(S["dve_link"], at.next("dve_link"))
                for b in reversed(range(PB - 1)):
                    ins = dve.tensor_tensor(rs[:, :, b, :], rs[:, :, b + 1, :], sp[:, :, (b + 1) * DEC:(b + 2) * DEC],
                                            ALU.add)
                    if b:
                        ins.then_inc(S["dve_link"], 1)
                        dve.wait_ge(S["dve_link"], at.next("dve_link"))
                    else:
                        ins.then_inc(S["soft"], 1)

        def finish(c):
            c0, cn = CHUNKS[c]
            dve.wait_ge(S["pv"], at.next("pv"))
            dve.wait_ge(S[f"o_stored{c}"], at.before(f"o_stored{c}"))
            dve.tensor_tensor(B["o"][:, c0:c0 + cn], B["acc"][:, 0:cn], B["gate"][:, c0:c0 + cn], ALU.mult).then_inc(S["o_ready"], 1)

        for s in range(self.N + 4):
            if s < self.N:
                slot, m, _, _ = self.views(s, B)
                dve.wait_ge(S["z"], at.next("z"))
                if s >= 3:
                    dve.wait_ge(S["soft"], at.nth("soft", s - 2))
                else:
                    dve.wait_ge(S["soft"], at.before("soft"))
                dve.tensor_scalar(m, slot, SOFT_MAX, None, ALU.min).then_inc(S["clamped"], 1)
            if 1 <= s <= self.N:
                softplus(s - 1)
            for c in range(3):
                if s - 3 == self.last_of(c):
                    finish(c)
            if 3 <= s < 3 + 2 * KT and s % 2:
                next_weights((s - 3) // 2)

    def gpsimd(self, pool, at, S, B):
        pool.wait_ge(S["r_zero"], at.all("r_zero"))
        for s, (c, b, hd) in enumerate(self.UNITS):
            if c < 2 and b > 0:
                q = self.span(s)[0]
                pool.wait_ge(S["soft"], at.nth("soft", s + 1))
                pool.wait_ge(S["after"], at.nth("after", s + 1))
                r = B["r"][:, c, hd, q:]
                pool.tensor_tensor(r, r, B["s"][s % 4][:, q:], ALU.add).then_inc(S["running"], 1)


def mix_phase(nc, top, name, x_in, x_out, o_dram, p_in, w_out, w_gate, w_proj, ident):
    with ExitStack() as ctx:
        sb = lambda n, s, dt=F32: ctx.enter_context(nc.sbuf_tensor(f"{name}_{n}", s, dt))
        pb = lambda n, s: ctx.enter_context(nc.psum_tensor(f"{name}_{n}", s, F32))
        NW = 2 * KT + PT
        w = [sb("w_high", [P, NW, D], F32R), sb("w_low", [P, NW, D], F32R)]
        stage = sb("stage", [P, 2, D])
        xt, x1, xo, sig = sb("xt", [P, D]), sb("x1", [P, D]), sb("xo", [P, D]), sb("sig", [P, D])
        pt = sb("pt", [P, PLE])
        ot = sb("ot", [P, KT, P])
        os_ = [sb("o_high", [P, KT, P], F32R), sb("o_low", [P, KT, P], F32R)]
        xs = [sb("x_high", [P, KT, P], F32R), sb("x_low", [P, KT, P], F32R)]
        ps_ = [sb("p_high", [P, PT, P], F32R), sb("p_low", [P, PT, P], F32R)]
        y, xtr, gt, pp = (pb(n, [P, 2, 512]) for n in ("y", "xtr", "gt", "pp"))
        flat = lambda b, n: b[0:n, :, :].rearrange("p a n -> p (a n)")
        per = dict(
            w_even=16, w_odd=16, w_high=NW, w_low=NW, o_loaded=16, x_loaded=16, p_loaded=16, o_high=1,
            o_low=1, y=1, x1=1, turned=1, x_high=1, x_low=1, mixed=1, clamped=1, sig_exp=1, copied=1,
            x_out=1, stored=16, link=3, fill=1)
        S = semaphores(nc, ctx, name, per)
        block = ctx.enter_context(nc.Block())

        def rounds(eng, tile):
            tile(0, P)
            with eng.Fori(1, NT) as t:
                tile(t, P)
            tile(NT, DEC)

        def done(x, t):
            return (t + 1) * per[x] + CREDIT

        @block.sync
        def _(sp):
            sp.wait_ge(S["fill"], 1 + 1)

            def load_tile(t, n):
                sp.wait_ge(S["o_low"], done("o_low", t - 1))
                rows = bass.ds(t * P, n)
                sp.dma_start(ot[:, :, 0:n], o_dram[:, :, rows].rearrange("k p n -> p k n")).then_inc(S["o_loaded"], 16)
                sp.wait_ge(S["turned"], done("turned", t - 1))
                sp.dma_start(pt[0:n, :], p_in[rows, :]).then_inc(S["p_loaded"], 16)
                sp.dma_start(xt[0:n, :], x_in[rows, :]).then_inc(S["x_loaded"], 16)

            blocks = [m[k * P:(k + 1) * P, :] for m, count in ((w_out, KT), (w_gate, KT), (w_proj, PT))
                      for k in range(count)]
            load_tile(0, P)
            for k, src in enumerate(blocks):
                if k >= 2:
                    sp.wait_ge(S["w_low"], k - 1 + 1)
                sp.dma_start(stage[:, k % 2, :], src).then_inc(S["w_odd" if k % 2 else "w_even"], 16)
            with sp.Fori(1, NT) as t:
                load_tile(t, P)
            load_tile(NT, DEC)

        @block.scalar
        def _(act):
            act.preload_act_table_set("natural_log_exp_and_others")
            act.wait_ge(S["fill"], 1 + 1)

            def o_high(t, n):
                act.wait_ge(S["o_loaded"], done("o_loaded", t))
                act.wait_ge(S["y"], done("y", t - 1))
                act.activation(os_[0][:, :, 0:n], ot[:, :, 0:n], ACT.Copy).then_inc(S["o_high"], 1)

            def sigmoid_exp(t, n):
                act.wait_ge(S["clamped"], done("clamped", t))
                act.activation(sig[0:n, :], sig[0:n, :], ACT.Exp, scale=-1.0).then_inc(S["sig_exp"], 1)

            def send(t, n):
                act.wait_ge(S["x_out"], done("x_out", t))
                act.dma_start(x_out[bass.ds(t * P, n), :], xo[0:n, :]).then_inc(S["stored"], 16)

            def tile(t, n, first=False, last=False):
                if not first:
                    sigmoid_exp(t - 1, P)
                    send(t - 1, P)
                act.wait_ge(S["turned"], done("turned", t))
                act.activation(xs[0][:, :, 0:n], xtr[:, :, :].rearrange("p a (k n) -> p (a k) n", n=P)[:, :, 0:n],
                               ACT.Copy)
                act.activation(ps_[0][:, :, 0:n], y[:, 0, 0:2 * P].rearrange("p (k n) -> p k n", n=P)[:, :, 0:n],
                               ACT.Copy).then_inc(S["x_high"], 1)
                if not last:
                    o_high(t + 1, DEC if isinstance(t, int) and t == NT - 1 else P)
                act.wait_ge(S["x1"], done("x1", t))
                act.wait_ge(S["stored"], done("stored", t - 1))
                act.activation(xo[0:n, :], x1[0:n, :], ACT.Copy).then_inc(S["copied"], 1)

            o_high(0, P)
            for k in range(NW):
                act.wait_ge(S["w_odd" if k % 2 else "w_even"], 16 * (k // 2 + 1) + 1)
                act.activation(w[0][:, k, :], stage[:, k % 2, :], ACT.Copy).then_inc(S["w_high"], 1)
            tile(0, P, first=True)
            with act.Fori(1, NT - 1) as t:
                tile(t, P)
            tile(NT - 1, P)
            tile(NT, DEC, last=True)
            sigmoid_exp(NT, DEC)
            send(NT, DEC)
            act.wait_ge(S["stored"], done("stored", NT))

        @block.vector
        def _(dve):
            start_credits(dve, S)
            dve.drain().then_inc(S["fill"], 1)

            def o_low(t, n):
                dve.wait_ge(S["o_high"], done("o_high", t))
                dve.tensor_tensor(os_[1][:, :, 0:n], ot[:, :, 0:n], os_[0][:, :, 0:n].bitcast(F32),
                                  ALU.subtract).then_inc(S["o_low"], 1)

            def residual(t, n):
                dve.wait_ge(S["y"], done("y", t))
                dve.wait_ge(S["x_loaded"], done("x_loaded", t))
                dve.wait_ge(S["copied"], done("copied", t - 1))
                dve.tensor_tensor(x1[0:n, :], xt[0:n, :], flat(y, n), ALU.add).then_inc(S["x1"], 1)

            def finish(t, n):
                at = Count(per, t)
                s = sig[0:n, :]
                dve.wait_ge(S["mixed"], done("mixed", t))
                dve.wait_ge(S["x_out"], done("x_out", t - 1))
                dve.tensor_scalar(s, flat(gt, n), -CLAMP, None, ALU.max).then_inc(S["clamped"], 1)
                dve.wait_ge(S["sig_exp"], done("sig_exp", t))
                dve.tensor_scalar(s, s, 1.0, None, ALU.add).then_inc(S["link"], 1)
                dve.wait_ge(S["link"], at.next("link"))
                dve.reciprocal(s, s).then_inc(S["link"], 1)
                dve.wait_ge(S["link"], at.next("link"))
                dve.tensor_tensor(s, flat(pp, n), s, ALU.mult).then_inc(S["link"], 1)
                dve.wait_ge(S["link"], at.next("link"))
                dve.wait_ge(S["copied"], done("copied", t))
                dve.tensor_tensor(xo[0:n, :], xo[0:n, :], s, ALU.add).then_inc(S["x_out"], 1)

            def x_low(t, n):
                dve.wait_ge(S["x_high"], done("x_high", t))
                dve.tensor_tensor(xs[1][:, :, 0:n], xtr[:, :, :].rearrange("p a (k n) -> p (a k) n", n=P)[:, :, 0:n],
                                  xs[0][:, :, 0:n].bitcast(F32), ALU.subtract)
                dve.tensor_tensor(ps_[1][:, :, 0:n], y[:, 0, 0:2 * P].rearrange("p (k n) -> p k n", n=P)[:, :, 0:n],
                                  ps_[0][:, :, 0:n].bitcast(F32), ALU.subtract).then_inc(S["x_low"], 1)

            def tile(t, n, first=False, last=False):
                residual(t, n)
                if not first:
                    finish(t - 1, P)
                x_low(t, n)
                if not last:
                    o_low(t + 1, DEC if isinstance(t, int) and t == NT - 1 else P)

            o_low(0, P)
            for k in range(NW):
                dve.wait_ge(S["w_high"], k + 1 + 1)
                dve.tensor_tensor(w[1][:, k, :], stage[:, k % 2, :], w[0][:, k, :].bitcast(F32),
                                  ALU.subtract).then_inc(S["w_low"], 1)
            tile(0, P, first=True)
            with dve.Fori(1, NT - 1) as t:
                tile(t, P)
            tile(NT - 1, P)
            tile(NT, DEC, last=True)
            finish(NT, DEC)

        @block.tensor
        def _(pe):
            def product(out, n, parts, first_block, blocks):
                for half in range(2):
                    for k in range(blocks):
                        last = three(pe, out[0:n, half, :], [x[:, k, 0:n] for x in parts],
                                     [x[:, first_block + k, half * 512:(half + 1) * 512] for x in w],
                                     k == 0, k == blocks - 1)
                return last

            def out_product(t, n):
                pe.wait_ge(S["o_low"], done("o_low", t))
                pe.wait_ge(S["x_low"], done("x_low", t - 1))
                product(y, n, os_, 0, KT).then_inc(S["y"], 1)

            def mix(t, n):
                pe.wait_ge(S["x_low"], done("x_low", t))
                pe.wait_ge(S["x_out"], done("x_out", t - 1))
                product(pp, n, ps_, 2 * KT, PT)
                product(gt, n, xs, KT, KT).then_inc(S["mixed"], 1)

            def turn(t, n):
                pe.wait_ge(S["x1"], done("x1", t))
                pe.wait_ge(S["p_loaded"], done("p_loaded", t))
                for k in range(KT):
                    pe.transpose(xtr[:, k // 4, k % 4 * P:k % 4 * P + n], x1[0:n, k * P:(k + 1) * P], ident[0:n, 0:n])
                for k in range(PT):
                    last = pe.transpose(y[:, 0, k * P:k * P + n], pt[0:n, k * P:(k + 1) * P], ident[0:n, 0:n])
                last.then_inc(S["turned"], 1)

            pe.wait_ge(S["w_low"], KT + 1)
            out_product(0, P)
            turn(0, P)
            pe.wait_ge(S["w_low"], NW + 1)
            with pe.Fori(1, NT) as t:
                out_product(t, P)
                mix(t - 1, P)
                turn(t, P)
            out_product(NT, DEC)
            mix(NT - 1, P)
            turn(NT, DEC)
            mix(NT, DEC)


def head_constants(nc, top, lams, sub_gain, neg_lam, gain):
    lam_init = 0.8 - 0.6 * math.exp(-0.3 * 0)
    with ExitStack() as ctx:
        sb = lambda n, s: ctx.enter_context(nc.sbuf_tensor(f"lam_{n}", s, F32))
        rows, prod, dots = sb("rows", [P, 4, DH]), sb("prod", [P, 2, DH]), sb("dots", [P, 2])
        loaded, step, es = (top.enter_context(nc.semaphore(f"lam_{n}")) for n in ("loaded", "step", "exp"))
        block = ctx.enter_context(nc.Block())

        @block.sync
        def _(sp):
            for n, row in enumerate(lams):
                sp.dma_start(rows[:, n, :], row.to_broadcast([P, DH])).then_inc(loaded, 16)
            sp.dma_start(gain[:, :], sub_gain.rearrange("o p -> p o")).then_inc(loaded, 16)

        @block.scalar
        def _(act):
            act.preload_act_table_set("natural_log_exp_and_others")
            act.wait_ge(step, 2)
            act.activation(dots[:, :], dots[:, :], ACT.Exp).then_inc(es, 1)

        @block.vector
        def _(dve):
            dve.wait_ge(loaded, 80)
            dve.tensor_scalar(gain[:, :], gain[:, :], 1.0 - lam_init, None, ALU.mult)
            dve.tensor_tensor(prod[:, :, :], rows[:, 0::2, :], rows[:, 1::2, :], ALU.mult).then_inc(step, 1)
            dve.wait_ge(step, 1)
            dve.reduce_sum(dots[:, :], prod[:, :, :], AX.X).then_inc(step, 1)
            dve.wait_ge(es, 1)
            dve.tensor_scalar(neg_lam[:, :], dots[:, 1:2], dots[:, 0:1], -lam_init, ALU.subtract, ALU.add)


def load_constants(nc, top, name, pairs):
    with ExitStack() as ctx:
        loaded = top.enter_context(nc.semaphore(f"{name}_loaded"))
        block = ctx.enter_context(nc.Block())

        @block.sync
        def _(sp):
            for dst, src in pairs:
                sp.dma_start(dst, src).then_inc(loaded, 16)
            sp.wait_ge(loaded, 16 * len(pairs))


def build(nc, A, out):
    y, ak, av, bk, bv = out
    top = ExitStack()
    with top:
        internal = lambda n, s: nc.dram_tensor(n, s, F32, kind="Internal").ap()
        x_mid, x_last = internal("x_mid", (ROWS, D)), internal("x_last", (ROWS, D))
        o_dram = internal("o_t", (GROUPS, P, ROWS))
        ident = top.enter_context(nc.sbuf_tensor("ident", [P, P], F32))
        load_constants(nc, top, "ident", [(ident[:, :], A["c_ident"])])

        with ExitStack() as a:
            sb = lambda n, s: a.enter_context(nc.sbuf_tensor(n, s, F32))
            cos, sin = sb("cos", [P, NT + 1, 4, 16]), sb("sin", [P, NT + 1, 4, 16])
            neg_lam, gain = sb("neg_lam", [P, 1]), sb("sub_gain", [P, 1])
            h = [a.enter_context(nc.sbuf_tensor(f"ha_{n}", [P, KT, ROWS], F32R)) for n in ("high", "low")]
            load_constants(nc, top, "rope", [(cos[:, :, :, :], A["c_cos"]), (sin[:, :, :, :], A["c_sin"])])
            head_constants(nc, top, [A[f"a_lam_{n}"] for n in ("q1", "k1", "q2", "k2")], A["a_subln_g"], neg_lam, gain)
            norm_phase(nc, top, "norm_a", A["x"], A["a_norm_g"], ident, h)
            attention_layer(nc, top, "la", h, A["a_w_in"], A["cache_a_k"], A["cache_a_v"], ak, av, o_dram,
                            dict(ident=ident), DifferentialAttention(neg_lam, gain, cos, sin))
        mix_phase(nc, top, "mix_a", A["x"], x_mid, o_dram, A["p"][0], A["a_w_out"], A["ple_w_gate"][0],
                  A["ple_w_proj"][0], ident)
        with ExitStack() as b:
            masks = {n: b.enter_context(nc.sbuf_tensor(n, s, F32)) for n, s in
                     (("neg_tri", [P, P]), ("neg_ones", [P, P]), ("strict", [P, P]), ("strict_sample", [P, 2, DEC]))}
            h = [b.enter_context(nc.sbuf_tensor(f"hb_{n}", [P, KT, ROWS], F32R)) for n in ("high", "low")]
            load_constants(nc, top, "mask", [(m[:], A[f"c_{n}"]) for n, m in masks.items()])
            norm_phase(nc, top, "norm_b", x_mid, A["b_norm_g"], ident, h)
            attention_layer(nc, top, "lb", h, A["b_w_in"], A["cache_b_k"], A["cache_b_v"], bk, bv, o_dram,
                            dict(ident=ident), StickBreaking(masks))
        mix_phase(nc, top, "mix_b", x_mid, x_last, o_dram, A["p"][1], A["b_w_out"], A["ple_w_gate"][1],
                  A["ple_w_proj"][1], ident)
        norm_phase(nc, top, "norm_y", x_last, A["final_norm_g"], ident, None, y_out=y)


def constants():
    half, theta = DH // 8, 500000.0
    inv = np.float32(theta) ** (-np.arange(half, dtype=np.float32) * np.float32(2.0) / np.float32(DH // 4))
    pos = np.zeros(PADDED, np.float32)
    pos[:SEQ] = np.arange(SEQ)
    pos[SEQ:ROWS] = PAST + np.arange(DEC)
    ang = (pos[:, None] * inv[None, :]).astype(np.float32)
    wide = lambda a: np.ascontiguousarray(
        np.tile(a.astype(np.float32), (1, 8)).reshape(NT + 1, P, 4, 16).transpose(1, 0, 2, 3))
    i = np.arange(P)
    strict = (i[:, None] < i[None, :]).astype(np.float32)
    return {"c_cos": wide(np.cos(ang)), "c_sin": wide(np.sin(ang)), "c_ident": np.eye(P, dtype=np.float32),
            "c_neg_tri": -(i[:, None] >= i[None, :]).astype(np.float32),
            "c_neg_ones": np.full((P, P), -1.0, np.float32), "c_strict": strict,
            "c_strict_sample": np.ascontiguousarray(np.tile(strict[:, None, :DEC], (1, 2, 1)))}


def kernel(**inputs):
    import concourse.bacc as bacc
    from concourse.bass_utils import run_bass_kernel_spmd

    a = {k: np.asarray(v) for k, v in inputs.items()}
    by_group = lambda w: w.reshape(D, 4, GROUPS, P).transpose(2, 0, 1, 3).reshape(GROUPS, D, 4 * P)
    arrays = {
        "x": np.concatenate([a["x_prompt"][0], a["x_sample"][0]]),
        "p": np.concatenate([a["p_prompt"][:, 0], a["p_sample"][:, 0]], axis=1),
        "a_w_in": by_group(a["a_w_in"][0]), "b_w_in": by_group(a["b_w_in"][0]),
        "a_w_out": a["a_w_out"][0], "b_w_out": a["b_w_out"][0],
        "ple_w_gate": a["ple_w_gate"], "ple_w_proj": a["ple_w_proj"],
        "a_norm_g": a["a_norm_g"], "b_norm_g": a["b_norm_g"], "a_subln_g": a["a_subln_g"],
        "final_norm_g": a["final_norm_g"].reshape(1, D),
        **{f"a_lam_{n}": a[f"a_lam_{n}"] for n in ("q1", "k1", "q2", "k2")},
        **{n: a[n].reshape(PAST, D) for n in ("cache_a_k", "cache_a_v", "cache_b_k", "cache_b_v")},
        **constants(),
    }
    nc = bacc.Bacc("TRN2", target_bir_lowering=False, num_devices=1)
    arrays = {k: np.ascontiguousarray(v) for k, v in arrays.items()}
    A = {k: nc.dram_tensor(f"in_{k}", v.shape, F32, kind="ExternalInput").ap() for k, v in arrays.items()}
    names = ["y", "ak", "av", "bk", "bv"]
    out = [nc.dram_tensor(f"out_{n}", (ROWS, D), F32, kind="ExternalOutput").ap() for n in names]
    build(nc, A, out)
    r = run_bass_kernel_spmd(nc, [{f"in_{k}": v for k, v in arrays.items()}], core_ids=[0]).results[0]
    y, ak, av, bk, bv = (r[f"out_{n}"] for n in names)
    p_, s_ = slice(0, SEQ), slice(SEQ, ROWS)
    shape = {"ak": (8, 2, DH), "av": (8, 2 * DH), "bk": (16, DH), "bv": (16, DH)}
    cut = lambda arr, n, rows: arr[rows].reshape(1, 1, -1, *shape[n])
    return (y[p_].reshape(1, SEQ, D), y[s_].reshape(1, DEC, D),
            cut(ak, "ak", p_), cut(av, "av", p_), cut(bk, "bk", p_), cut(bv, "bv", p_),
            cut(ak, "ak", s_), cut(av, "av", s_), cut(bk, "bk", s_), cut(bv, "bv", s_))
```

```python
import math
from contextlib import ExitStack

import numpy as np

import concourse.bass as bass
from concourse import mybir

F32 = mybir.dt.float32
F32R = mybir.dt.float32r
ACT = mybir.ActivationFunctionType
ALU = mybir.AluOpType
AX = mybir.AxisListType

P = 128
D = 1024
KT = D // P
SEQ, DEC, PAST = 1024, 32, 512
ROWS = SEQ + DEC
NT = SEQ // P
PADDED = SEQ + P
GROUPS = D // P
DH = 64
STAGES = 4
PB = PAST // P
PLE = 256
PT = PLE // P
CHUNK = 64
EPS = 1e-6
QC = 512
NEG = -1e30
SOFT_MAX = 40.0
CHUNKS = [(0, QC), (QC, QC), (SEQ, DEC)]
TILES = [(t, P) for t in range(NT)] + [(NT, DEC)]


CREDIT = 1


class Count:

    def __init__(self, per, r):
        self.per, self.r, self.seen = per, r, {}

    def nth(self, x, k):
        return self.r * self.per[x] + k + CREDIT

    def before(self, x):
        return self.nth(x, 0)

    def all(self, x):
        return self.nth(x, self.per[x])

    def next(self, x):
        self.seen[x] = self.seen.get(x, 0) + 1
        return self.nth(x, self.seen[x])


def semaphores(nc, ctx, name, per):
    made = {x: nc.alloc_semaphore(f"{name}_{x}") for x in per}
    sems = list(made.values())

    def give_back():
        nc.clear_and_free_semaphores(sems)
        nc.all_engine_barrier()
    ctx.callback(give_back)
    return made


def start_credits(eng, S):
    for sem in S.values():
        eng.sem_inc(sem, CREDIT)


def three(pe, out, a, b, start, stop, **kw):
    pairs = [(a[0], b[0]), (a[1], b[0]), (a[0], b[1])]
    for n, (x, y) in enumerate(pairs):
        last = pe.matmul(out, x, y, start=start and n == 0, stop=stop and n == 2, **kw)
    return last


def out_weights(h, part, k):
    return h[part][:, :, :].rearrange("p k n -> p (k n)")[:, k * D:(k + 1) * D]


def norm_phase(nc, top, name, x_in, gain, ident, h):
    with ExitStack() as ctx:
        sb = lambda n, s, dt=F32: ctx.enter_context(nc.sbuf_tensor(f"{name}_{n}", s, dt))
        xt = sb("xt", [P, 2, D])
        hn = sb("hn", [P, 2, D])
        sq = sb("sq", [P, D])
        ss = sb("ss", [P, 2])
        rstd = sb("rstd", [P, 2])
        eps = sb("eps", [P, 1])
        gb = sb("gb", [P, D])
        ps = ctx.enter_context(nc.psum_tensor(f"{name}_ps", [P, 2, KT, P], F32))
        per = {"gain": 16, "x_even": 16, "x_odd": 16, "sum": 2, "log": 2, "rstd": 2, "h": 2,
            "turned": 2, "high": 2, "low": 2, "fill": 1}
        S = semaphores(nc, ctx, name, per)
        loaded = ("x_even", "x_odd")
        block = ctx.enter_context(nc.Block())

        def rounds(eng, front, back=None):
            def pair(i, last):
                for u in range(2):
                    front(Count(per, i + u), 2 * i + u + 1, 1 - u, DEC if last and u else P)
                    if back:
                        back(Count(per, i), 2 * i + u, u, P)
            front(Count(per, 0), 0, 0, P)
            with eng.Fori(0, NT // 2 - 1) as i:
                pair(i, False)
            pair(NT // 2 - 1, True)
            if back:
                back(Count(per, NT // 2), NT, 0, DEC)

        @block.sync
        def _(sp):
            sp.dma_start(gb[:, :], gain.to_broadcast([P, D])).then_inc(S["gain"], 16)

            def load(at, t, u, n):
                sp.wait_ge(S["h"], at.nth("h", u - 1))
                sp.dma_start(xt[0:n, u, :], x_in[bass.ds(t * P, n), :]).then_inc(S[loaded[u]], 16)
            rounds(sp, load)

        @block.scalar
        def _(act):
            act.preload_act_table_set("natural_log_exp_and_others")
            act.wait_ge(S["fill"], 1 + 1)

            def statistics(at, t, u, n):
                act.wait_ge(S[loaded[u]], at.nth(loaded[u], 16))
                act.activation(sq[0:n, :], xt[0:n, u, :], ACT.Square,
                               accum_out=ss[0:n, u:u + 1]).then_inc(S["sum"], 1)
                act.wait_ge(S["sum"], at.nth("sum", u + 1))
                act.activation(ss[0:n, u:u + 1], ss[0:n, u:u + 1], ACT.Ln, scale=1.0 / D,
                               bias=eps[0:n, 0:1]).then_inc(S["log"], 1)
                act.wait_ge(S["log"], at.nth("log", u + 1))
                act.activation(rstd[0:n, u:u + 1], ss[0:n, u:u + 1], ACT.Exp,
                               scale=-0.5).then_inc(S["rstd"], 1)

            def high(at, t, u, n):
                act.wait_ge(S["turned"], at.nth("turned", u + 1))
                act.activation(h[0][:, :, bass.ds(t * P, n)], ps[:, u, :, 0:n], ACT.Copy).then_inc(S["high"], 1)
            rounds(act, statistics, high)

        @block.vector
        def _(dve):
            start_credits(dve, S)
            dve.memset(eps[:, :], EPS)
            dve.drain().then_inc(S["fill"], 1)

            def scale(at, t, u, n):
                dve.wait_ge(S["rstd"], at.nth("rstd", u + 1))
                dve.wait_ge(S["low"], at.nth("low", u - 1))
                dve.scalar_tensor_tensor(out=hn[0:n, u, :], in0=xt[0:n, u, :], scalar=rstd[0:n, u:u + 1],
                                         in1=gb[0:n, :], op0=ALU.mult, op1=ALU.mult).then_inc(S["h"], 1)

            def low(at, t, u, n):
                dve.wait_ge(S["high"], at.nth("high", u + 1))
                cols = bass.ds(t * P, n)
                dve.tensor_tensor(h[1][:, :, cols], ps[:, u, :, 0:n], h[0][:, :, cols].bitcast(F32),
                                  ALU.subtract).then_inc(S["low"], 1)
            dve.wait_ge(S["gain"], 16 + 1)
            rounds(dve, scale, low)

        @block.tensor
        def _(pe):
            def turn(at, t, u, n):
                pe.wait_ge(S["h"], at.nth("h", u + 1))
                pe.wait_ge(S["low"], at.nth("low", u - 1))
                for k in range(KT):
                    last = pe.transpose(ps[:, u, k, 0:n], hn[0:n, u, k * P:(k + 1) * P], ident[0:n, 0:n])
                last.then_inc(S["turned"], 1)
            rounds(pe, turn)


def attention_layer(nc, top, name, h, w_in, k_past, v_past, k_out, v_out, o_dram, consts, core):
    ident = consts["ident"]
    with ExitStack() as ctx:
        sb = lambda n, s, dt=F32: ctx.enter_context(nc.sbuf_tensor(f"{name}_{n}", s, dt))
        pb = lambda n, s: ctx.enter_context(nc.psum_tensor(f"{name}_{n}", s, F32))
        w = [sb("w_high", [P, KT, QC], F32R), sb("w_low", [P, KT, QC], F32R)]
        stage = sb("stage", [P, STAGES, QC])
        tok = sb("tok", [P, NT + 1, 3 * P])
        qk = [sb("qk_high", [P, 2, PADDED], F32R), sb("qk_low", [P, 2, PADDED], F32R)]
        kp = sb("kp", [P, PB, P])
        vp = sb("vp", [P, PB, P])
        kpt = [sb("kpt_high", [P, PAST], F32R), sb("kpt_low", [P, PAST], F32R)]
        gate = sb("gate", [P, ROWS])
        gtmp = sb("gtmp", [P, 2, QC])
        o = sb("o", [P, ROWS])
        pj = pb("pj", [P, 3, 512])
        acc = pb("acc", [P, 512])
        sc = pb("sc", [P, 4, 512])
        table = dict(past=32, w_high=KT, w_low=KT, tok_ready=9, pj_tok=9, turned=10, turned_high=10,
                     turned_low=10, tok_stored=64, g_ready=3, g_raw=3, g_clamped=3, g_exp=3, g_log=3,
                     g_soft=3, g_sig=3, g_done=3, pv=3,
                     o_ready=3, pe_tick=0, fill=1)
        table.update({f"w_loaded{s}": 16 * KT // STAGES for s in range(STAGES)})
        table.update({f"o_stored{c}": 16 for c in range(3)})
        table.update(core.TABLE)
        S = semaphores(nc, ctx, name, table)
        rows_ready = core.ROWS
        B = dict(tok=tok, qk=qk, kpt=kpt, vp=vp, gate=gate, gtmp=gtmp, o=o, pj=pj, acc=acc, sc=sc,
                 ident=ident, **core.memory(sb))
        block = ctx.enter_context(nc.Block())

        def groups(eng, body):
            with eng.Fori(0, GROUPS - 1) as r:
                body(r, True)
            body(GROUPS - 1, False)

        def load_w(sp, g, k):
            sp.dma_start(stage[:, k % STAGES, :], w_in[bass.ds(g, 1), k * P:(k + 1) * P, :]
                         .rearrange("o p n -> p (o n)")).then_inc(S[f"w_loaded{k % STAGES}"], 16)

        def split_w_high(act, g, k):
            act.wait_ge(S[f"w_loaded{k % STAGES}"], Count(table, g).nth(f"w_loaded{k % STAGES}", 16 * (k // STAGES + 1)))
            act.activation(w[0][:, k, :], stage[:, k % STAGES, :], ACT.Copy).then_inc(S["w_high"], 1)

        def split_w_low(dve, g, k):
            dve.wait_ge(S["w_high"], Count(table, g).nth("w_high", k + 1))
            dve.tensor_tensor(w[1][:, k, :], stage[:, k % STAGES, :], w[0][:, k, :].bitcast(F32),
                              ALU.subtract).then_inc(S["w_low"], 1)

        @block.sync
        def _(sp):
            sp.wait_ge(S["fill"], 1 + 1)
            for k in range(KT):
                if k >= STAGES:
                    sp.wait_ge(S["w_low"], k - STAGES + 1 + 1)
                load_w(sp, 0, k)

            def body(r, more):
                at = Count(table, r)
                sp.wait_ge(S["pv"], at.before("pv"))
                sp.wait_ge(S["turned_high"], at.before("turned_high"))
                for buf, past in ((kp, k_past), (vp, v_past)):
                    sp.dma_start(buf[:, :, :], past[:, bass.ds(r * P, P)].rearrange("(b p) f -> p b f", p=P)
                                 ).then_inc(S["past"], 16)
                if more:
                    for k in range(KT):
                        sp.wait_ge(S["w_low"], Count(table, r + 1).nth("w_low", k - STAGES + 1))
                        if k == STAGES:
                            send_rows(r, at)
                        load_w(sp, r + 1, k)
                else:
                    send_rows(r, at)
                for c, (c0, cn) in enumerate(CHUNKS):
                    sp.wait_ge(S["o_ready"], at.next("o_ready"))
                    sp.dma_start(o_dram[bass.ds(r, 1), :, c0:c0 + cn].rearrange("o p n -> p (o n)"),
                                 o[:, c0:c0 + cn]).then_inc(S[f"o_stored{c}"], 16)

            def send_rows(r, at):
                sp.wait_ge(S[rows_ready], at.nth(rows_ready, 9))
                for n, out in ((1, k_out), (2, v_out)):
                    cols = slice(n * P, (n + 1) * P)
                    sp.dma_start(out[0:SEQ, bass.ds(r * P, P)].rearrange("(t p) f -> p t f", p=P),
                                 tok[:, 0:NT, cols]).then_inc(S["tok_stored"], 16)
                    sp.dma_start(out[SEQ:ROWS, bass.ds(r * P, P)],
                                 tok[0:DEC, NT, cols]).then_inc(S["tok_stored"], 16)
            groups(sp, body)
            sp.wait_ge(S["tok_stored"], 64 * GROUPS + 1)
            for c in range(3):
                sp.wait_ge(S[f"o_stored{c}"], 16 * GROUPS + 1)

        two = acc[:, 0:2 * P].rearrange("p (a n) -> p a n", a=2)

        @block.scalar
        def _(act):
            act.preload_act_table_set("natural_log_exp_and_others")
            act.wait_ge(S["fill"], 1 + 1)
            for k in range(KT):
                split_w_high(act, 0, k)

            def body(r, more):
                at = Count(table, r)
                act.wait_ge(S["tok_stored"], at.before("tok_stored"))
                act.wait_ge(S["pv"], at.before("pv"))

                def turned_high(n):
                    act.wait_ge(S["turned"], at.next("turned"))
                    if n <= NT:
                        t, m = TILES[n]
                        out, src = qk[0][:, :, t * P:t * P + m], two[:, :, 0:m]
                    else:
                        out, src = kpt[0][:, :], acc[:, :]
                    act.activation(out, src, ACT.Copy).then_inc(S["turned_high"], 1)

                def gate_raw(c):
                    c0, cn = CHUNKS[c]
                    act.wait_ge(S["g_ready"], at.next("g_ready"))
                    act.wait_ge(S["o_ready"], at.before("o_ready"))
                    act.activation(gate[:, c0:c0 + cn], pj[:, 2, 0:cn], ACT.Copy).then_inc(S["g_raw"], 1)

                def gate_log(c):
                    g = gtmp[:, c % 2, 0:CHUNKS[c][1]]
                    act.wait_ge(S["g_clamped"], at.next("g_clamped"))
                    act.activation(g, g, ACT.Exp, scale=-1.0).then_inc(S["g_exp"], 1)
                    act.wait_ge(S["g_exp"], at.next("g_exp"))
                    act.activation(g, g, ACT.Ln, bias=1.0).then_inc(S["g_log"], 1)

                def gate_sigmoid(c):
                    g = gtmp[:, c % 2, 0:CHUNKS[c][1]]
                    act.wait_ge(S["g_soft"], at.next("g_soft"))
                    act.activation(g, g, ACT.Exp, scale=-1.0).then_inc(S["g_sig"], 1)

                for t, n in TILES:
                    act.wait_ge(S["pj_tok"], at.next("pj_tok"))
                    act.activation(tok[0:n, t, 0:P], pj[0:n, t % 2, 0:P], ACT.Copy, scale=DH ** -0.5)
                    act.activation(tok[0:n, t, P:], pj[0:n, t % 2, P:3 * P], ACT.Copy).then_inc(S["tok_ready"], 1)
                    if t >= 2:
                        turned_high(t - 2)
                for k in range(NT - 1, NT + 2):
                    turned_high(k)

                def next_weights(k):
                    if more:
                        if k == 0:
                            act.wait_ge(S["g_ready"], at.all("g_ready"))
                        split_w_high(act, r + 1, k)
                core.scalar(act, at, S, B, next_weights, (gate_raw, gate_log, gate_sigmoid))
            groups(act, body)

        @block.vector
        def _(dve):
            start_credits(dve, S)
            dve.memset(qk[0][:, :, ROWS:].bitcast(F32), 0.0)
            dve.memset(qk[1][:, :, ROWS:].bitcast(F32), 0.0)
            for q in range(DEC, P, DEC):
                dve.memset(tok[q:q + DEC, NT, :], 0.0)
            core.prepare(dve, B)
            dve.drain().then_inc(S["fill"], 1)
            for k in range(KT):
                split_w_low(dve, 0, k)

            def body(r, more):
                at = Count(table, r)

                def turned_low(n):
                    dve.wait_ge(S["turned_high"], at.next("turned_high"))
                    if n <= NT:
                        t, m = TILES[n]
                        cols = slice(t * P, t * P + m)
                        out, sub, src = qk[1][:, :, cols], qk[0][:, :, cols], two[:, :, 0:m]
                    else:
                        out, sub, src = kpt[1][:, :], kpt[0][:, :], acc[:, :]
                    dve.tensor_tensor(out, src, sub.bitcast(F32), ALU.subtract).then_inc(S["turned_low"], 1)

                def gate_clamp(c):
                    c0, cn = CHUNKS[c]
                    dve.wait_ge(S["g_raw"], at.next("g_raw"))
                    if c == 2:
                        dve.wait_ge(S["g_done"], at.nth("g_done", 1))
                    dve.tensor_scalar(gtmp[:, c % 2, 0:cn], gate[:, c0:c0 + cn], -SOFT_MAX, None,
                                      ALU.max).then_inc(S["g_clamped"], 1)

                def gate_soft(c):
                    c0, cn = CHUNKS[c]
                    g = gtmp[:, c % 2, 0:cn]
                    dve.wait_ge(S["g_log"], at.next("g_log"))
                    dve.scalar_tensor_tensor(out=g, in0=gate[:, c0:c0 + cn], scalar=-1.0, in1=g, op0=ALU.mult,
                                             op1=ALU.max).then_inc(S["g_soft"], 1)

                for k in range(NT + 2):
                    turned_low(k)

                def next_weights(k):
                    if more:
                        split_w_low(dve, r + 1, k)
                core.vector(dve, at, S, B, next_weights, (gate_clamp, gate_soft))
            groups(dve, body)

        @block.gpsimd
        def _(pool):
            pool.wait_ge(S["fill"], 1 + 1)

            def body(r, more):
                at = Count(table, r)

                def gate_product(c):
                    c0, cn = CHUNKS[c]
                    g = gate[:, c0:c0 + cn]
                    pool.wait_ge(S["g_sig"], at.next("g_sig"))
                    pool.tensor_tensor(g, g, gtmp[:, c % 2, 0:cn], ALU.mult).then_inc(S["g_done"], 1)
                core.gpsimd(pool, at, S, B, gate_product)
            groups(pool, body)

        @block.tensor
        def _(pe):
            pe.wait_ge(S["fill"], 1 + 1)

            def body(r, more):
                at = Count(table, r)
                pe.wait_ge(S["w_low"], at.all("w_low"))
                pe.wait_ge(S[core.PJ_LEFT], at.before(core.PJ_LEFT))

                def project(t, n):
                    pe.wait_ge(S["tok_ready"], at.nth("tok_ready", t - 1))
                    rows = slice(t * P, t * P + n)
                    for k in range(KT):
                        last = three(pe, pj[0:n, t % 2, 0:3 * P], [x[:, k, rows] for x in h],
                                     [x[:, k, 0:3 * P] for x in w], k == 0, k == KT - 1)
                    last.then_inc(S["pj_tok"], 1)

                def turn(n):
                    if n == 0:
                        pe.wait_ge(S["o_ready"], at.before("o_ready"))
                    pe.wait_ge(S["turned_low"], at.nth("turned_low", n))
                    if n <= NT:
                        pe.wait_ge(S[rows_ready], at.nth(rows_ready, n + 1))
                        t, m = TILES[n]
                        if m < P:
                            pe.sem_inc(S["pe_tick"], 1)
                        for a in range(2):
                            last = pe.transpose(acc[:, a * P:a * P + m], tok[0:m, t, a * P:(a + 1) * P],
                                                ident[0:m, 0:m])
                    else:
                        pe.wait_ge(S["past"], at.nth("past", 32))
                        for b in range(PB):
                            last = pe.transpose(acc[:, b * P:(b + 1) * P], kp[:, b, :], ident[:, :])
                    last.then_inc(S["turned"], 1)

                for t, n in TILES:
                    project(t, n)
                    if t >= 2:
                        turn(t - 2)
                for k in range(NT - 1, NT + 2):
                    turn(k)

                def gate_project(c):
                    c0, cn = CHUNKS[c]
                    if c == 0:
                        pe.wait_ge(S[core.G_LEFT], at.before(core.G_LEFT))
                    else:
                        pe.wait_ge(S["g_raw"], at.nth("g_raw", c))
                    for k in range(KT):
                        last = three(pe, pj[:, 2, 0:cn], [x[:, k, 3 * P:] for x in w],
                                     [x[:, k, c0:c0 + cn] for x in h], k == 0, k == KT - 1)
                    last.then_inc(S["g_ready"], 1)
                pe.wait_ge(S["turned_low"], at.all("turned_low"))
                pe.wait_ge(S["tok_ready"], at.all("tok_ready"))
                core.tensor(pe, at, S, B, gate_project)
            groups(pe, body)


class DifferentialAttention:

    UNITS = [(qb * P, P, (qb + 1) * P) for qb in range(NT)] + [(SEQ, DEC, PAST + DEC)]
    CHUNK_END = {3: 0, 7: 1, 8: 2}
    GATE_AT = (2, 3, 4)
    ROWS, PJ_LEFT, G_LEFT = "rope", "moved", "rstd"
    TABLE = dict(rope=9, pool_link=9, scores=18, neg_max=18, probs=18, weights=9, w_turned=14, moved=14,
                 squared=3, var=3, log=3, rstd=3, dve_link=34 + 27 + 3)

    def __init__(self, lam, gain, cos, sin):
        self.neg_lam, self.gain, self.cos, self.sin = lam, gain, cos, sin

    def memory(self, sb):
        return dict(p=[[sb(f"p{u}{c}", [P, SEQ]) for c in range(2)] for u in range(2)],
                    wt=sb("wt", [P, NT, QC]), mean=sb("mean", [P, P]), eps=sb("eps", [P, 1]),
                    mx=sb("mx", [P, 2, 2]), nm=sb("nm", [P, 2, 2]), sums=sb("sums", [P, 2, 2]),
                    ra=sb("ra", [P, 2, 4, 16]))

    def prepare(self, dve, B):
        dve.memset(B["mean"][:, :], 1.0 / P)
        dve.memset(B["eps"][:, :], EPS)

    def groups_of(self, u):
        if u == NT:
            return [(0, PB, P), (PB, 1, DEC)]
        return [(k, min(4, u + 1 - k), P) for k in range(0, u + 1, 4)]

    def gpsimd(self, pool, at, S, B, gate_product):
        tok, ra = B["tok"], B["ra"]
        for t, n in TILES:
            pool.wait_ge(S["tok_ready"], at.next("tok_ready"))
            pool.wait_ge(S["rope"], at.nth("rope", t))
            x = tok[0:n, t, 0:2 * P].rearrange("p (c d) -> p c d", d=DH)
            xc, xs = ra[0:n, 0], ra[0:n, 1]
            pool.tensor_tensor(xc, x[:, :, 0:16], self.cos[0:n, t], ALU.mult)
            pool.tensor_tensor(xs, x[:, :, 0:16], self.sin[0:n, t], ALU.mult).then_inc(S["pool_link"], 1)
            pool.wait_ge(S["pool_link"], at.next("pool_link"))
            pool.tensor_tensor(x[:, :, 0:8], xc[:, :, 0:8], xs[:, :, 8:16], ALU.subtract)
            pool.tensor_tensor(x[:, :, 8:16], xc[:, :, 8:16], xs[:, :, 0:8], ALU.add).then_inc(S["rope"], 1)
        for c in range(3):
            gate_product(c)

    def tensor(self, pe, at, S, B, gate_project):
        sc, pj, acc, wt, p = B["sc"], B["pj"], B["acc"], B["wt"], B["p"]
        ring = [0]

        def score(u, c):
            q0, n, nk = self.UNITS[u]
            if u:
                pe.wait_ge(S["probs"], at.nth("probs", 2 * u + c - 1))
            else:
                pe.wait_ge(S["probs"], at.before("probs"))
            if n < P:
                pe.sem_inc(S["pe_tick"], 1)
            f = slice(c * DH, (c + 1) * DH)
            keys = [([x[f, 0:PAST] for x in B["kpt"]], 0, PAST), ([x[f, 1, SEQ:ROWS] for x in B["qk"]], PAST, DEC)
                    ] if u == NT else [([x[f, 1, k:min(k + 512, nk)] for x in B["qk"]], k, min(512, nk - k))
                                       for k in range(0, nk, 512)]
            for rhs, k, kn in keys:
                last = three(pe, sc[0:n, 2 * c + k // 512, k % 512:k % 512 + kn],
                             [x[f, 0, q0:q0 + n] for x in B["qk"]], rhs, True, True)
            last.then_inc(S["scores"], 1)

        def turn_weights(u):
            q0, n, nk = self.UNITS[u]
            pe.wait_ge(S["weights"], at.nth("weights", u + 1))
            for k0, nb, rows in self.groups_of(u):
                if ring[0] >= 2:
                    pe.wait_ge(S["moved"], at.nth("moved", ring[0] - 1))
                if n < P:
                    pe.sem_inc(S["pe_tick"], 1)
                bank = pj[0:rows, ring[0] % 2, 0:nb * n].rearrange("p (b n) -> p b n", n=n)
                for b in range(nb):
                    k = (k0 + b) * P
                    last = pe.transpose(bank[:, b, :], p[u % 2][0][0:n, k:k + rows], B["ident"][0:n, 0:n])
                last.then_inc(S["w_turned"], 1)
                ring[0] += 1

        def values(c):
            c0, cn = CHUNKS[c]
            if c == 0:
                pe.wait_ge(S["o_ready"], at.before("o_ready"))
            else:
                pe.wait_ge(S["o_ready"], at.nth("o_ready", c))
            pe.wait_ge(S["moved"], at.nth("moved", sum(len(self.groups_of(u)) for u in range({0: 4, 1: 8, 2: 9}[c]))))
            if c == 2:
                for b in range(PB):
                    pe.matmul(acc[:, 0:cn], B["vp"][:, b, :], wt[:, b, 0:cn], start=b == 0, stop=False)
                last = pe.matmul(acc[:, 0:cn], B["tok"][0:DEC, NT, 2 * P:], wt[0:DEC, PB, 0:cn],
                                 start=False, stop=True)
            else:
                blocks = 4 * (c + 1)
                for b in range(blocks):
                    q = max(0, b * P - c0)
                    last = pe.matmul(acc[:, q:], B["tok"][:, b, 2 * P:], wt[:, b, q:],
                                     start=b == 0, stop=b == blocks - 1)
            last.then_inc(S["pv"], 1)

        def variance(c):
            cn = CHUNKS[c][1]
            pe.wait_ge(S["squared"], at.next("squared"))
            if c == 0:
                pe.wait_ge(S["g_raw"], at.all("g_raw"))
            else:
                pe.wait_ge(S["rstd"], at.nth("rstd", c))
            pe.matmul(pj[:, 2, 0:cn], B["mean"][:, :], B["gtmp"][:, 0, 0:cn], start=True, stop=True).then_inc(S["var"], 1)

        for u in range(NT + 1):
            for c in range(2):
                score(u, c)
            if u >= 1:
                turn_weights(u - 1)
                if u - 1 in self.CHUNK_END:
                    values(self.CHUNK_END[u - 1])
            if u in self.GATE_AT:
                gate_project(u - self.GATE_AT[0])
            if u == 7:
                variance(0)
        variance(1)
        turn_weights(NT)
        values(2)
        variance(2)

    def scalar(self, act, at, S, B, next_weights, gate):
        p, sc, wt = B["p"], B["sc"], B["wt"]
        gate_raw, gate_log, gate_sigmoid = gate
        ring = [0]

        def probs(u, c):
            q0, n, nk = self.UNITS[u]
            if u >= 2:
                act.wait_ge(S["w_turned"], at.nth("w_turned", sum(len(self.groups_of(x)) for x in range(u - 1))))
            act.wait_ge(S["neg_max"], at.next("neg_max"))
            act.activation(p[u % 2][c][0:n, 0:nk],
                                  sc[0:n, 2 * c:2 * c + 2, :].rearrange("p a n -> p (a n)")[:, 0:nk],
                                  ACT.Exp, bias=B["nm"][0:n, u % 2, c:c + 1],
                                  accum_out=B["sums"][0:n, u % 2, c:c + 1]).then_inc(S["probs"], 1)

        def move(u):
            q0, n, nk = self.UNITS[u]
            if u in (4, 8):
                act.wait_ge(S["pv"], at.nth("pv", u // 4))
            off = q0 % QC
            for k0, nb, rows in self.groups_of(u):
                act.wait_ge(S["w_turned"], at.next("w_turned"))
                bank = B["pj"][0:rows, ring[0] % 2, 0:nb * n].rearrange("p (b n) -> p b n", n=n)
                act.activation(wt[0:rows, k0:k0 + nb, off:off + n], bank, ACT.Copy).then_inc(S["moved"], 1)
                ring[0] += 1

        def square(c):
            cn = CHUNKS[c][1]
            act.wait_ge(S["pv"], at.next("pv"))
            act.wait_ge(S["g_done"], at.all("g_done"))
            act.activation(B["gtmp"][:, 0, 0:cn], B["acc"][:, 0:cn], ACT.Square).then_inc(S["squared"], 1)

        def norm(c):
            c0, cn = CHUNKS[c]
            act.wait_ge(S["var"], at.next("var"))
            act.wait_ge(S[f"o_stored{c}"], at.before(f"o_stored{c}"))
            r = B["o"][:, c0:c0 + cn]
            act.activation(r, B["pj"][:, 2, 0:cn], ACT.Ln, bias=B["eps"][:, 0:1]).then_inc(S["log"], 1)
            act.wait_ge(S["log"], at.next("log"))
            act.activation(r, r, ACT.Exp, scale=-0.5).then_inc(S["rstd"], 1)

        for u in range(NT + 1):
            for c in range(2):
                probs(u, c)
            if u - 2 in self.GATE_AT:
                gate_sigmoid(u - 2 - self.GATE_AT[0])
            if u - 1 in self.GATE_AT:
                gate_log(u - 1 - self.GATE_AT[0])
            if u >= 1:
                move(u - 1)
            if u in self.GATE_AT:
                gate_raw(u - self.GATE_AT[0])
            if u == 6:
                square(0)
            if u == 7:
                norm(0)
            if u > self.GATE_AT[-1]:
                next_weights(2 * (u - 5))
                next_weights(2 * (u - 5) + 1)
        square(1)
        norm(1)
        move(NT)
        square(2)
        norm(2)

    def vector(self, dve, at, S, B, next_weights, gate):
        sc, p, mx, nm, sums = B["sc"], B["p"], B["mx"], B["nm"], B["sums"]

        def maxima(u, c):
            q0, n, nk = self.UNITS[u]
            dve.wait_ge(S["scores"], at.next("scores"))
            s = sc[0:n, 2 * c:2 * c + 2, :].rearrange("p a n -> p (a n)")[:, 0:nk]
            if u < NT:
                dve.memset(s[0:CHUNK, nk - CHUNK:nk], NEG).then_inc(S["dve_link"], 1)
                dve.wait_ge(S["dve_link"], at.next("dve_link"))
            dve.reduce_max(mx[0:n, u % 2, c:c + 1], s, AX.X).then_inc(S["dve_link"], 1)
            dve.wait_ge(S["dve_link"], at.next("dve_link"))
            dve.tensor_scalar(nm[0:n, u % 2, c:c + 1], mx[0:n, u % 2, c:c + 1], -1.0, None, ALU.mult).then_inc(S["neg_max"], 1)

        def combine(u):
            q0, n, nk = self.UNITS[u]
            dve.wait_ge(S["probs"], at.next("probs"))
            dve.wait_ge(S["probs"], at.next("probs"))
            s, a, b = sums[0:n, u % 2], p[u % 2][0][0:n, 0:nk], p[u % 2][1][0:n, 0:nk]
            dve.reciprocal(s, s).then_inc(S["dve_link"], 1)
            dve.wait_ge(S["dve_link"], at.next("dve_link"))
            dve.tensor_scalar(s[:, 1:2], s[:, 1:2], self.neg_lam[0:n, 0:1], None, ALU.mult).then_inc(S["dve_link"], 1)
            dve.wait_ge(S["dve_link"], at.next("dve_link"))
            dve.tensor_scalar(b, b, s[:, 1:2], None, ALU.mult).then_inc(S["dve_link"], 1)
            dve.wait_ge(S["dve_link"], at.next("dve_link"))
            dve.scalar_tensor_tensor(out=a, in0=a, scalar=s[:, 0:1], in1=b, op0=ALU.mult, op1=ALU.add).then_inc(S["weights"], 1)

        def finish(c):
            c0, cn = CHUNKS[c]
            out = B["o"][:, c0:c0 + cn]
            dve.wait_ge(S["rstd"], at.next("rstd"))
            dve.wait_ge(S["g_done"], at.nth("g_done", c + 1))
            dve.tensor_tensor(out, B["acc"][:, 0:cn], out, ALU.mult).then_inc(S["dve_link"], 1)
            dve.wait_ge(S["dve_link"], at.next("dve_link"))
            dve.scalar_tensor_tensor(out=out, in0=out, scalar=self.gain[:, 0:1],
                                            in1=B["gate"][:, c0:c0 + cn], op0=ALU.mult, op1=ALU.mult).then_inc(S["o_ready"], 1)

        gate_clamp, gate_soft = gate
        for u in range(NT + 1):
            if u >= 1:
                combine(u - 1)
            for c in range(2):
                maxima(u, c)
            if u - 2 in self.GATE_AT:
                gate_soft(u - 2 - self.GATE_AT[0])
            if u - 1 in self.GATE_AT:
                gate_clamp(u - 1 - self.GATE_AT[0])
            if u == 8:
                finish(0)
            if u > self.GATE_AT[-1]:
                next_weights(2 * (u - 5))
                next_weights(2 * (u - 5) + 1)
        combine(NT)
        finish(1)
        finish(2)


class StickBreaking:

    UNITS = [(c, b, hd) for c in range(2) for b in reversed(range(4 * (c + 1))) for hd in range(2)] + [(2, 0, 0)]
    N = len(UNITS)
    SLOTS = 4
    GATE_AT = (1, 5, 9)
    SB = PB + 1
    SN = SB * DEC
    ROWS, PJ_LEFT, G_LEFT = "tok_ready", "pv", "g_raw"
    DIAG = sum(c < 2 and b >= 4 * c for c, b, _ in UNITS)
    TABLE = dict(z=N, clamped=N, exp=N, log=N, soft=N, after=N, a=N, running=24 - 4, r_zero=2, dve_link=DIAG + 5)

    def __init__(self, masks):
        self.masks = masks

    def memory(self, sb):
        return dict(m=[sb(f"m{i}", [P, QC]) for i in range(3)], s=[sb(f"s{i}", [P, QC]) for i in range(4)],
                    a=[sb(f"a{i}", [P, QC]) for i in range(4)], r=sb("r", [P, 2, 2, QC]),
                    rs=sb("rs", [P, 2, PB, DEC]), hide=sb("hide", [P, P], F32R),
                    unit=sb("unit", [P, P], F32R))

    def prepare(self, dve, B):
        dve.tensor_scalar(B["hide"][:, :], self.masks["strict"][:, :], -1.0, -NEG, ALU.add, ALU.mult)
        dve.tensor_copy(B["unit"][:, :], B["ident"][:, :])

    def span(self, s):
        c, b, hd = self.UNITS[s]
        q = max(0, b * P - c * QC)
        return q, QC - q, b >= 4 * c

    def views(self, s, B):
        if self.UNITS[s][0] == 2:
            first = s % self.SLOTS
            assert first + 1 < self.SLOTS
            wide = lambda x: x[:, 0:2 * self.SN].rearrange("p (h n) -> p h n", h=2)
            return B["sc"][:, first:first + 2, 0:self.SN], wide(B["m"][s % 3]), wide(B["s"][s % 4]), wide(B["a"][s % 4])
        q, n, _ = self.span(s)
        return tuple(x[:, q:q + n] for x in (B["sc"][:, s % self.SLOTS, :], B["m"][s % 3], B["s"][s % 4], B["a"][s % 4]))

    def last_of(self, c):
        return max(s for s, x in enumerate(self.UNITS) if x[0] == c)

    def running_before(self, s):
        return sum(self.UNITS[x][0] < 2 and self.UNITS[x][1] > 0 for x in range(s))

    def tensor(self, pe, at, S, B, gate_project):
        sc, acc, qk = B["sc"], B["acc"], B["qk"]
        tri, ones = self.masks["neg_tri"], self.masks["neg_ones"]

        def scores(s):
            c, b, hd = self.UNITS[s]
            slot = sc[:, s % self.SLOTS, :]
            if s >= self.SLOTS:
                pe.wait_ge(S["a"], at.nth("a", s - self.SLOTS + 1 + (c == 2)))
            else:
                pe.wait_ge(S["a"], at.before("a"))
            if c == 2:
                for b in range(self.SB):
                    for hd in range(2):
                        f = slice(hd * DH, (hd + 1) * DH)
                        keys = [x[f, b * P:(b + 1) * P] for x in B["kpt"]] if b < PB else [x[f, 1, SEQ:] for x in qk]
                        last = three(pe, self.views(s, B)[0][:, hd, b * DEC:(b + 1) * DEC], keys,
                                     [x[f, 0, SEQ:ROWS] for x in qk], b == 0, True, skip_group_check=True)
            else:
                q, n, _ = self.span(s)
                f = slice(hd * DH, (hd + 1) * DH)
                c0 = c * QC
                last = three(pe, slot[:, q:], [x[f, 1, b * P:(b + 1) * P] for x in qk],
                             [x[f, 0, c0 + q:c0 + QC] for x in qk], True, True, skip_group_check=True)
            last.then_inc(S["z"], 1)

        def after(s):
            c, b, hd = self.UNITS[s]
            slot, _, sp, _ = self.views(s, B)
            add = dict(start=False, stop=True, skip_group_check=True)
            pe.wait_ge(S["soft"], at.nth("soft", s + 1))
            if c == 2:
                for hd in range(2):
                    pe.matmul(slot[:, hd, PB * DEC:], B["unit"][:, :], B["hide"][:, 0:DEC], **add)
                    pe.matmul(slot[:, hd, 0:PB * DEC], ones[:, :], B["rs"][:, hd].rearrange("p b n -> p (b n)"), **add)
                    last = pe.matmul(slot[:, hd, :], tri[:, :], sp[:, hd, :], **add)
            else:
                q, n, masked = self.span(s)
                if masked:
                    pe.matmul(slot[:, 0:P], B["unit"][:, :], B["hide"][:, :], **add)
                if b < 4 * c + 3:
                    pe.wait_ge(S["running"], at.nth("running", self.running_before(s - 1)))
                    pe.matmul(slot, ones[:, :], B["r"][:, c, hd, q:], **add)
                last = pe.matmul(slot, tri[:, :], sp, **add)
            last.then_inc(S["after"], 1)

        def values(s):
            c, b, hd = self.UNITS[s]
            a = B["a"][s % 4]
            pe.wait_ge(S["a"], at.nth("a", s + 1))
            if s in (0, self.last_of(0) + 1, self.last_of(1) + 1):
                if c == 0:
                    pe.wait_ge(S["o_ready"], at.before("o_ready"))
                else:
                    pe.wait_ge(S["o_ready"], at.nth("o_ready", c))
            if c == 2:
                for b in range(self.SB):
                    for hd in range(2):
                        f = slice(hd * DH, (hd + 1) * DH)
                        v = B["vp"][:, b, f] if b < PB else B["tok"][:, NT, 2 * P + hd * DH:2 * P + (hd + 1) * DH]
                        col = hd * self.SN + b * DEC
                        last = pe.matmul(acc[f, 0:DEC], v, a[:, col:col + DEC], start=b == 0,
                                         stop=b == PB, skip_group_check=True)
            else:
                q = self.span(s)[0]
                f = slice(hd * DH, (hd + 1) * DH)
                last = pe.matmul(acc[f, q:], B["tok"][:, b, 2 * P + hd * DH:2 * P + (hd + 1) * DH], a[:, q:],
                                 start=b == 4 * c + 3, stop=b == 0, skip_group_check=True)
            if s == self.last_of(c):
                last.then_inc(S["pv"], 1)

        for s in range(self.N + 3):
            if s < self.N:
                scores(s)
            if 2 <= s < self.N + 2:
                after(s - 2)
            if s >= 3:
                values(s - 3)
            if s in self.GATE_AT:
                gate_project(self.GATE_AT.index(s))

    def scalar(self, act, at, S, B, next_weights, gate):
        gate_raw, gate_log, gate_sigmoid = gate
        for s in range(self.N + 2):
            if s < self.N:
                m = self.views(s, B)[1]
                act.wait_ge(S["clamped"], at.next("clamped"))
                act.activation(m, m, ACT.Exp).then_inc(S["exp"], 1)
                act.wait_ge(S["exp"], at.next("exp"))
                act.activation(m, m, ACT.Ln, bias=1.0).then_inc(S["log"], 1)
            if s >= 2:
                j = s - 2
                slot, _, _, a = self.views(j, B)
                act.wait_ge(S["after"], at.next("after"))
                act.activation(a, slot, ACT.Exp).then_inc(S["a"], 1)
            if s - 1 in self.GATE_AT:
                gate_raw(self.GATE_AT.index(s - 1))
            if s - 3 in self.GATE_AT:
                gate_log(self.GATE_AT.index(s - 3))
            if s - 5 in self.GATE_AT:
                gate_sigmoid(self.GATE_AT.index(s - 5))
            if 12 <= s < 12 + KT:
                next_weights(s - 12)

    def vector(self, dve, at, S, B, next_weights, gate):
        strict, strict_sample = self.masks["strict"], self.masks["strict_sample"]
        gate_clamp, gate_soft = gate
        dve.wait_ge(S["running"], at.before("running"))
        dve.wait_ge(S["after"], at.before("after"))
        for c in range(2):
            dve.memset(B["r"][:, c, :, :], 0.0).then_inc(S["r_zero"], 1)

        def softplus(s):
            c = self.UNITS[s][0]
            masked = c == 2 or self.span(s)[2]
            slot, m, sp, _ = self.views(s, B)
            dve.wait_ge(S["log"], at.next("log"))
            if s >= 4:
                dve.wait_ge(S["after"], at.nth("after", s - 3))
                dve.wait_ge(S["running"], at.nth("running", self.running_before(s - 3)))
            ins = dve.tensor_tensor(sp, slot, m, ALU.max)
            if not masked:
                ins.then_inc(S["soft"], 1)
            elif c < 2:
                ins.then_inc(S["dve_link"], 1)
                dve.wait_ge(S["dve_link"], at.next("dve_link"))
                dve.tensor_tensor(sp[:, 0:P], sp[:, 0:P], strict[:, :], ALU.mult).then_inc(S["soft"], 1)
            else:
                ins.then_inc(S["dve_link"], 1)
                dve.wait_ge(S["dve_link"], at.next("dve_link"))
                new = sp[:, :, PB * DEC:]
                dve.tensor_tensor(new, new, strict_sample[:, :, :], ALU.mult).then_inc(S["dve_link"], 1)
                dve.wait_ge(S["dve_link"], at.next("dve_link"))
                rs = B["rs"]
                dve.tensor_copy(rs[:, :, PB - 1, :], new).then_inc(S["dve_link"], 1)
                dve.wait_ge(S["dve_link"], at.next("dve_link"))
                for b in reversed(range(PB - 1)):
                    ins = dve.tensor_tensor(rs[:, :, b, :], rs[:, :, b + 1, :], sp[:, :, (b + 1) * DEC:(b + 2) * DEC],
                                            ALU.add)
                    if b:
                        ins.then_inc(S["dve_link"], 1)
                        dve.wait_ge(S["dve_link"], at.next("dve_link"))
                    else:
                        ins.then_inc(S["soft"], 1)

        def finish(c):
            c0, cn = CHUNKS[c]
            dve.wait_ge(S["pv"], at.next("pv"))
            dve.wait_ge(S["g_done"], at.nth("g_done", c + 1))
            dve.wait_ge(S[f"o_stored{c}"], at.before(f"o_stored{c}"))
            dve.tensor_tensor(B["o"][:, c0:c0 + cn], B["acc"][:, 0:cn], B["gate"][:, c0:c0 + cn], ALU.mult).then_inc(S["o_ready"], 1)

        for s in range(self.N + 4):
            if s < self.N:
                slot, m, _, _ = self.views(s, B)
                dve.wait_ge(S["z"], at.next("z"))
                if s >= 3:
                    dve.wait_ge(S["soft"], at.nth("soft", s - 2))
                else:
                    dve.wait_ge(S["soft"], at.before("soft"))
                dve.tensor_scalar(m, slot, SOFT_MAX, None, ALU.min).then_inc(S["clamped"], 1)
            if 1 <= s <= self.N:
                softplus(s - 1)
            for c in range(3):
                if s - 3 == self.last_of(c):
                    finish(c)
            if s - 2 in self.GATE_AT:
                gate_clamp(self.GATE_AT.index(s - 2))
            if s - 4 in self.GATE_AT:
                gate_soft(self.GATE_AT.index(s - 4))
            if 12 <= s < 12 + KT:
                next_weights(s - 12)

    def gpsimd(self, pool, at, S, B, gate_product):
        pool.wait_ge(S["r_zero"], at.all("r_zero"))
        for s, (c, b, hd) in enumerate(self.UNITS):
            if c < 2 and b > 0:
                q = self.span(s)[0]
                pool.wait_ge(S["soft"], at.nth("soft", s + 1))
                pool.wait_ge(S["after"], at.nth("after", s + 1))
                r = B["r"][:, c, hd, q:]
                pool.tensor_tensor(r, r, B["s"][s % 4][:, q:], ALU.add).then_inc(S["running"], 1)
            if s - 5 in self.GATE_AT:
                gate_product(self.GATE_AT.index(s - 5))


def mix_phase(nc, top, name, x_in, x_out, o_dram, p_in, w_out, w_gate, w_proj, ident,
              h, final_gain=None):
    with ExitStack() as ctx:
        sb = lambda n, s, dt=F32: ctx.enter_context(nc.sbuf_tensor(f"{name}_{n}", s, dt))
        pb = lambda n, s: ctx.enter_context(nc.psum_tensor(f"{name}_{n}", s, F32))
        NW = 2 * KT + PT
        w_rest = [sb("w_high", [P, NW - KT, D], F32R), sb("w_low", [P, NW - KT, D], F32R)]

        def w_block(part, k):
            return out_weights(h, part, k) if k < KT else w_rest[part][:, k - KT, :]
        stage = sb("stage", [P, 2, D])
        xt, x1, xo, sig = sb("xt", [P, D]), sb("x1", [P, D]), sb("xo", [P, D]), sb("sig", [P, D])
        pt = sb("pt", [P, PLE])
        if final_gain is not None:
            gb, yo = sb("gb", [P, D]), sb("yo", [P, D])
            ss, rstd, eps = sb("ss", [P, 1]), sb("rstd", [P, 1]), sb("eps", [P, 1])
        ot = sb("ot", [P, KT, P])
        os_ = [sb("o_high", [P, KT, P], F32R), sb("o_low", [P, KT, P], F32R)]
        xs = [sb("x_high", [P, KT, P], F32R), sb("x_low", [P, KT, P], F32R)]
        ps_ = [sb("p_high", [P, PT, P], F32R), sb("p_low", [P, PT, P], F32R)]
        y, xtr, gt, pp = (pb(n, [P, 2, 512]) for n in ("y", "xtr", "gt", "pp"))
        flat = lambda b, n: b[0:n, :, :].rearrange("p a n -> p (a n)")
        per = dict(
            w_even=16, w_odd=16, w_high=NW, w_low=NW, o_loaded=16, x_loaded=16, p_loaded=16, o_high=1,
            o_low=1, y=1, x1=1, turned=1, p_high=1, p_low=1, x_high=1, x_low=1, mixed=1, clamped=1, exp=1,
            log=1, soft=1, sig=1, copied=1,
            x_out=1, stored=16, link=1, gain=16, sum=1, square_log=1, rstd=1, normed=1, fill=1)
        S = semaphores(nc, ctx, name, per)
        block = ctx.enter_context(nc.Block())

        def rounds(eng, tile):
            tile(0, P)
            with eng.Fori(1, NT) as t:
                tile(t, P)
            tile(NT, DEC)

        def done(x, t):
            return (t + 1) * per[x] + CREDIT

        @block.sync
        def _(sp):
            sp.wait_ge(S["fill"], 1 + 1)

            def load_tile(t, n):
                sp.wait_ge(S["o_low"], done("o_low", t - 1))
                rows = bass.ds(t * P, n)
                sp.dma_start(ot[:, :, 0:n], o_dram[:, :, rows].rearrange("k p n -> p k n")).then_inc(S["o_loaded"], 16)
                sp.wait_ge(S["turned"], done("turned", t - 1))
                sp.dma_start(pt[0:n, :], p_in[rows, :]).then_inc(S["p_loaded"], 16)
                sp.dma_start(xt[0:n, :], x_in[rows, :]).then_inc(S["x_loaded"], 16)

            blocks = [m[k * P:(k + 1) * P, :] for m, count in ((w_out, KT), (w_gate, KT), (w_proj, PT))
                      for k in range(count)]
            load_tile(0, P)
            if final_gain is not None:
                sp.dma_start(gb[:, :], final_gain.to_broadcast([P, D])).then_inc(S["gain"], 16)
            for k, src in enumerate(blocks):
                if k >= 2:
                    sp.wait_ge(S["w_low"], k - 1 + 1)
                sp.dma_start(stage[:, k % 2, :], src).then_inc(S["w_odd" if k % 2 else "w_even"], 16)
            with sp.Fori(1, NT) as t:
                load_tile(t, P)
            load_tile(NT, DEC)

        @block.scalar
        def _(act):
            act.preload_act_table_set("natural_log_exp_and_others")
            act.wait_ge(S["fill"], 1 + 1)

            def o_high(t, n):
                act.wait_ge(S["o_loaded"], done("o_loaded", t))
                act.wait_ge(S["y"], done("y", t - 1))
                act.activation(os_[0][:, :, 0:n], ot[:, :, 0:n], ACT.Copy).then_inc(S["o_high"], 1)

            def sigmoid(t, n):
                v = sig[0:n, :]
                act.wait_ge(S["clamped"], done("clamped", t))
                act.activation(v, v, ACT.Exp, scale=-1.0).then_inc(S["exp"], 1)
                act.wait_ge(S["exp"], done("exp", t))
                act.activation(v, v, ACT.Ln, bias=1.0).then_inc(S["log"], 1)
                act.wait_ge(S["soft"], done("soft", t))
                act.activation(v, v, ACT.Exp, scale=-1.0).then_inc(S["sig"], 1)

            def send(t, n):
                act.wait_ge(S["x_out"], done("x_out", t))
                act.dma_start(x_out[bass.ds(t * P, n), :], xo[0:n, :]).then_inc(S["stored"], 16)

            def statistics(t, n):
                act.wait_ge(S["x_out"], done("x_out", t))
                act.wait_ge(S["stored"], done("stored", t - 1))
                act.activation(yo[0:n, :], xo[0:n, :], ACT.Square, accum_out=ss[0:n, :]).then_inc(S["sum"], 1)
                act.wait_ge(S["sum"], done("sum", t))
                act.activation(ss[0:n, :], ss[0:n, :], ACT.Ln, scale=1.0 / D,
                               bias=eps[0:n, 0:1]).then_inc(S["square_log"], 1)
                act.wait_ge(S["square_log"], done("square_log", t))
                act.activation(rstd[0:n, :], ss[0:n, :], ACT.Exp, scale=-0.5).then_inc(S["rstd"], 1)

            def send_normed(t, n):
                act.wait_ge(S["normed"], done("normed", t))
                act.dma_start(x_out[bass.ds(t * P, n), :], yo[0:n, :]).then_inc(S["stored"], 16)

            def tile(t, n, first=False, last=False):
                if not last:
                    o_high(t + 1, DEC if isinstance(t, int) and t == NT - 1 else P)
                act.wait_ge(S["turned"], done("turned", t))
                act.activation(ps_[0][:, :, 0:n], y[:, 0, 0:2 * P].rearrange("p (k n) -> p k n", n=P)[:, :, 0:n],
                               ACT.Copy).then_inc(S["p_high"], 1)
                act.activation(xs[0][:, :, 0:n], xtr[:, :, :].rearrange("p a (k n) -> p (a k) n", n=P)[:, :, 0:n],
                               ACT.Copy).then_inc(S["x_high"], 1)
                if not first:
                    sigmoid(t - 1, P)
                    if final_gain is None:
                        send(t - 1, P)
                    else:
                        statistics(t - 1, P)
                        send_normed(t - 1, P)
                act.wait_ge(S["x1"], done("x1", t))
                if final_gain is None:
                    act.wait_ge(S["stored"], done("stored", t - 1))
                act.activation(xo[0:n, :], x1[0:n, :], ACT.Copy).then_inc(S["copied"], 1)

            o_high(0, P)
            for k in range(NW):
                act.wait_ge(S["w_odd" if k % 2 else "w_even"], 16 * (k // 2 + 1) + 1)
                act.activation(w_block(0, k), stage[:, k % 2, :], ACT.Copy).then_inc(S["w_high"], 1)
            tile(0, P, first=True)
            with act.Fori(1, NT - 1) as t:
                tile(t, P)
            tile(NT - 1, P)
            tile(NT, DEC, last=True)
            sigmoid(NT, DEC)
            if final_gain is None:
                send(NT, DEC)
            else:
                statistics(NT, DEC)
                send_normed(NT, DEC)
            act.wait_ge(S["stored"], done("stored", NT))

        @block.vector
        def _(dve):
            start_credits(dve, S)
            if final_gain is not None:
                dve.memset(eps[:, :], EPS)
            dve.drain().then_inc(S["fill"], 1)

            def o_low(t, n):
                dve.wait_ge(S["o_high"], done("o_high", t))
                dve.tensor_tensor(os_[1][:, :, 0:n], ot[:, :, 0:n], os_[0][:, :, 0:n].bitcast(F32),
                                  ALU.subtract).then_inc(S["o_low"], 1)

            def residual(t, n):
                dve.wait_ge(S["y"], done("y", t))
                dve.wait_ge(S["x_loaded"], done("x_loaded", t))
                dve.wait_ge(S["copied"], done("copied", t - 1))
                dve.tensor_tensor(x1[0:n, :], xt[0:n, :], flat(y, n), ALU.add).then_inc(S["x1"], 1)

            def finish(t, n):
                at = Count(per, t)
                v = sig[0:n, :]
                dve.wait_ge(S["mixed"], done("mixed", t))
                dve.wait_ge(S["x_out"], done("x_out", t - 1))
                dve.tensor_scalar(v, flat(gt, n), -SOFT_MAX, None, ALU.max).then_inc(S["clamped"], 1)
                dve.wait_ge(S["log"], done("log", t))
                dve.scalar_tensor_tensor(out=v, in0=flat(gt, n), scalar=-1.0, in1=v, op0=ALU.mult,
                                         op1=ALU.max).then_inc(S["soft"], 1)
                dve.wait_ge(S["sig"], done("sig", t))
                dve.tensor_tensor(v, flat(pp, n), v, ALU.mult).then_inc(S["link"], 1)
                dve.wait_ge(S["link"], at.next("link"))
                dve.wait_ge(S["copied"], done("copied", t))
                dve.tensor_tensor(xo[0:n, :], xo[0:n, :], v, ALU.add).then_inc(S["x_out"], 1)
                if final_gain is not None:
                    dve.wait_ge(S["rstd"], done("rstd", t))
                    dve.wait_ge(S["gain"], 16 + 1)
                    dve.scalar_tensor_tensor(out=yo[0:n, :], in0=xo[0:n, :], scalar=rstd[0:n, 0:1], in1=gb[0:n, :],
                                             op0=ALU.mult, op1=ALU.mult).then_inc(S["normed"], 1)

            def x_low(t, n):
                dve.wait_ge(S["p_high"], done("p_high", t))
                dve.tensor_tensor(ps_[1][:, :, 0:n], y[:, 0, 0:2 * P].rearrange("p (k n) -> p k n", n=P)[:, :, 0:n],
                                  ps_[0][:, :, 0:n].bitcast(F32), ALU.subtract).then_inc(S["p_low"], 1)
                dve.wait_ge(S["x_high"], done("x_high", t))
                dve.tensor_tensor(xs[1][:, :, 0:n], xtr[:, :, :].rearrange("p a (k n) -> p (a k) n", n=P)[:, :, 0:n],
                                  xs[0][:, :, 0:n].bitcast(F32), ALU.subtract).then_inc(S["x_low"], 1)

            def tile(t, n, first=False, last=False):
                residual(t, n)
                if not last:
                    o_low(t + 1, DEC if isinstance(t, int) and t == NT - 1 else P)
                x_low(t, n)
                if not first:
                    finish(t - 1, P)

            o_low(0, P)
            for k in range(NW):
                dve.wait_ge(S["w_high"], k + 1 + 1)
                dve.tensor_tensor(w_block(1, k), stage[:, k % 2, :], w_block(0, k).bitcast(F32),
                                  ALU.subtract).then_inc(S["w_low"], 1)
            tile(0, P, first=True)
            with dve.Fori(1, NT - 1) as t:
                tile(t, P)
            tile(NT - 1, P)
            tile(NT, DEC, last=True)
            finish(NT, DEC)

        @block.tensor
        def _(pe):
            def product(out, n, parts, first_block, blocks):
                for half in range(2):
                    for k in range(blocks):
                        last = three(pe, out[0:n, half, :], [x[:, k, 0:n] for x in parts],
                                     [w_block(part, first_block + k)[:, half * 512:(half + 1) * 512]
                                      for part in range(2)],
                                     k == 0, k == blocks - 1)
                return last

            def out_product(t, n):
                pe.wait_ge(S["o_low"], done("o_low", t))
                pe.wait_ge(S["p_low"], done("p_low", t - 1))
                product(y, n, os_, 0, KT).then_inc(S["y"], 1)

            def mix(t, n):
                pe.wait_ge(S["x_low"], done("x_low", t))
                pe.wait_ge(S["x_out"], done("x_out", t - 1))
                product(pp, n, ps_, 2 * KT, PT)
                product(gt, n, xs, KT, KT).then_inc(S["mixed"], 1)

            def turn(t, n):
                pe.wait_ge(S["x1"], done("x1", t))
                pe.wait_ge(S["p_loaded"], done("p_loaded", t))
                for k in range(KT):
                    pe.transpose(xtr[:, k // 4, k % 4 * P:k % 4 * P + n], x1[0:n, k * P:(k + 1) * P], ident[0:n, 0:n])
                for k in range(PT):
                    last = pe.transpose(y[:, 0, k * P:k * P + n], pt[0:n, k * P:(k + 1) * P], ident[0:n, 0:n])
                last.then_inc(S["turned"], 1)

            pe.wait_ge(S["w_low"], KT + 1)
            out_product(0, P)
            turn(0, P)
            pe.wait_ge(S["w_low"], NW + 1)
            with pe.Fori(1, NT) as t:
                out_product(t, P)
                mix(t - 1, P)
                turn(t, P)
            out_product(NT, DEC)
            mix(NT - 1, P)
            turn(NT, DEC)
            mix(NT, DEC)


def start_phase(nc, top, tables, lams, sub_gain, neg_lam, gain):
    lam_init = 0.8 - 0.6 * math.exp(-0.3 * 0)
    with ExitStack() as ctx:
        sb = lambda n, s: ctx.enter_context(nc.sbuf_tensor(f"lam_{n}", s, F32))
        rows, prod, dots = sb("rows", [P, 4, DH]), sb("prod", [P, 2, DH]), sb("dots", [P, 2])
        loaded, step, es, placed = (top.enter_context(nc.semaphore(f"lam_{n}"))
                                    for n in ("loaded", "step", "exp", "placed"))
        block = ctx.enter_context(nc.Block())

        @block.sync
        def _(sp):
            for n, row in enumerate(lams):
                sp.dma_start(rows[:, n, :], row.to_broadcast([P, DH])).then_inc(loaded, 16)
            sp.dma_start(gain[:, :], sub_gain.rearrange("o p -> p o")).then_inc(loaded, 16)

        @block.gpsimd
        def _(pool):
            for dst, src in tables:
                pool.dma_start(dst, src).then_inc(placed, 16)
            pool.wait_ge(placed, 16 * len(tables))

        @block.scalar
        def _(act):
            act.preload_act_table_set("natural_log_exp_and_others")
            act.wait_ge(step, 2)
            act.activation(dots[:, :], dots[:, :], ACT.Exp).then_inc(es, 1)

        @block.vector
        def _(dve):
            dve.wait_ge(loaded, 80)
            dve.tensor_scalar(gain[:, :], gain[:, :], 1.0 - lam_init, None, ALU.mult)
            dve.tensor_tensor(prod[:, :, :], rows[:, 0::2, :], rows[:, 1::2, :], ALU.mult).then_inc(step, 1)
            dve.wait_ge(step, 1)
            dve.reduce_sum(dots[:, :], prod[:, :, :], AX.X).then_inc(step, 1)
            dve.wait_ge(es, 1)
            dve.tensor_scalar(neg_lam[:, :], dots[:, 1:2], dots[:, 0:1], -lam_init, ALU.subtract, ALU.add)


def build(nc, A, out):
    y, ak, av, bk, bv = out
    top = ExitStack()
    with top:
        internal = lambda n, s: nc.dram_tensor(n, s, F32, kind="Internal").ap()
        x_mid = internal("x_mid", (ROWS, D))
        o_dram = internal("o_t", (GROUPS, P, ROWS))
        ident = top.enter_context(nc.sbuf_tensor("ident", [P, P], F32))
        masks = {n: top.enter_context(nc.sbuf_tensor(n, s, F32)) for n, s in
                 (("neg_tri", [P, P]), ("neg_ones", [P, P]), ("strict", [P, P]), ("strict_sample", [P, 2, DEC]))}
        h = [top.enter_context(nc.sbuf_tensor(f"h_{n}", [P, KT, ROWS], F32R)) for n in ("high", "low")]

        with ExitStack() as a:
            sb = lambda n, s: a.enter_context(nc.sbuf_tensor(n, s, F32))
            cos, sin = sb("cos", [P, NT + 1, 4, 16]), sb("sin", [P, NT + 1, 4, 16])
            neg_lam, gain = sb("neg_lam", [P, 1]), sb("sub_gain", [P, 1])
            tables = [(ident[:, :], A["c_ident"]), (cos[:, :, :, :], A["c_cos"]), (sin[:, :, :, :], A["c_sin"])]
            tables += [(m[:], A[f"c_{n}"]) for n, m in masks.items()]
            start_phase(nc, top, tables, [A[f"a_lam_{n}"] for n in ("q1", "k1", "q2", "k2")], A["a_subln_g"],
                        neg_lam, gain)
            norm_phase(nc, top, "norm_a", A["x"], A["a_norm_g"], ident, h)
            attention_layer(nc, top, "la", h, A["a_w_in"], A["cache_a_k"], A["cache_a_v"], ak, av, o_dram,
                            dict(ident=ident), DifferentialAttention(neg_lam, gain, cos, sin))
        mix_phase(nc, top, "mix_a", A["x"], x_mid, o_dram, A["p"][0], A["a_w_out"], A["ple_w_gate"][0],
                  A["ple_w_proj"][0], ident, h)
        norm_phase(nc, top, "norm_b", x_mid, A["b_norm_g"], ident, h)
        attention_layer(nc, top, "lb", h, A["b_w_in"], A["cache_b_k"], A["cache_b_v"], bk, bv, o_dram,
                        dict(ident=ident), StickBreaking(masks))
        mix_phase(nc, top, "mix_b", x_mid, y, o_dram, A["p"][1], A["b_w_out"], A["ple_w_gate"][1],
                  A["ple_w_proj"][1], ident, h, final_gain=A["final_norm_g"])


def constants():
    half, theta = DH // 8, 500000.0
    inv = np.float32(theta) ** (-np.arange(half, dtype=np.float32) * np.float32(2.0) / np.float32(DH // 4))
    pos = np.zeros(PADDED, np.float32)
    pos[:SEQ] = np.arange(SEQ)
    pos[SEQ:ROWS] = PAST + np.arange(DEC)
    ang = (pos[:, None] * inv[None, :]).astype(np.float32)
    wide = lambda a: np.ascontiguousarray(
        np.tile(a.astype(np.float32), (1, 8)).reshape(NT + 1, P, 4, 16).transpose(1, 0, 2, 3))
    i = np.arange(P)
    strict = (i[:, None] < i[None, :]).astype(np.float32)
    return {"c_cos": wide(np.cos(ang)), "c_sin": wide(np.sin(ang)), "c_ident": np.eye(P, dtype=np.float32),
            "c_neg_tri": -(i[:, None] >= i[None, :]).astype(np.float32),
            "c_neg_ones": np.full((P, P), -1.0, np.float32), "c_strict": strict,
            "c_strict_sample": np.ascontiguousarray(np.tile(strict[:, None, :DEC], (1, 2, 1)))}


def kernel(**inputs):
    import concourse.bacc as bacc
    from concourse.bass_utils import run_bass_kernel_spmd

    a = {k: np.asarray(v) for k, v in inputs.items()}
    by_group = lambda w: w.reshape(D, 4, GROUPS, P).transpose(2, 0, 1, 3).reshape(GROUPS, D, 4 * P)
    arrays = {
        "x": np.concatenate([a["x_prompt"][0], a["x_sample"][0]]),
        "p": np.concatenate([a["p_prompt"][:, 0], a["p_sample"][:, 0]], axis=1),
        "a_w_in": by_group(a["a_w_in"][0]), "b_w_in": by_group(a["b_w_in"][0]),
        "a_w_out": a["a_w_out"][0], "b_w_out": a["b_w_out"][0],
        "ple_w_gate": a["ple_w_gate"], "ple_w_proj": a["ple_w_proj"],
        "a_norm_g": a["a_norm_g"], "b_norm_g": a["b_norm_g"], "a_subln_g": a["a_subln_g"],
        "final_norm_g": a["final_norm_g"].reshape(1, D),
        **{f"a_lam_{n}": a[f"a_lam_{n}"] for n in ("q1", "k1", "q2", "k2")},
        **{n: a[n].reshape(PAST, D) for n in ("cache_a_k", "cache_a_v", "cache_b_k", "cache_b_v")},
        **constants(),
    }
    nc = bacc.Bacc("TRN2", target_bir_lowering=False, num_devices=1)
    arrays = {k: np.ascontiguousarray(v) for k, v in arrays.items()}
    A = {k: nc.dram_tensor(f"in_{k}", v.shape, F32, kind="ExternalInput").ap() for k, v in arrays.items()}
    names = ["y", "ak", "av", "bk", "bv"]
    out = [nc.dram_tensor(f"out_{n}", (ROWS, D), F32, kind="ExternalOutput").ap() for n in names]
    build(nc, A, out)
    r = run_bass_kernel_spmd(nc, [{f"in_{k}": v for k, v in arrays.items()}], core_ids=[0]).results[0]
    y, ak, av, bk, bv = (r[f"out_{n}"] for n in names)
    p_, s_ = slice(0, SEQ), slice(SEQ, ROWS)
    shape = {"ak": (8, 2, DH), "av": (8, 2 * DH), "bk": (16, DH), "bv": (16, DH)}
    cut = lambda arr, n, rows: arr[rows].reshape(1, 1, -1, *shape[n])
    return (y[p_].reshape(1, SEQ, D), y[s_].reshape(1, DEC, D),
            cut(ak, "ak", p_), cut(av, "av", p_), cut(bk, "bk", p_), cut(bv, "bv", p_),
            cut(ak, "ak", s_), cut(av, "av", s_), cut(bk, "bk", s_), cut(bv, "bv", s_))
```

```python
import math
from contextlib import ExitStack

import numpy as np

import concourse.bass as bass
from concourse import mybir

F32 = mybir.dt.float32
F32R = mybir.dt.float32r
ACT = mybir.ActivationFunctionType
ALU = mybir.AluOpType
AX = mybir.AxisListType

P = 128
D = 1024
KT = D // P
SEQ, DEC, PAST = 1024, 32, 512
ROWS = SEQ + DEC
NT = SEQ // P
PADDED = SEQ + P
GROUPS = D // P
DH = 64
STAGES = 4
PB = PAST // P
PLE = 256
PT = PLE // P
CHUNK = 64
EPS = 1e-6
QC = 512
NEG = -1e30
SOFT_MAX = 40.0
TURN_BANKS = 3
CHUNKS = [(0, QC), (QC, QC), (SEQ, DEC)]
TILES = [(t, P) for t in range(NT)] + [(NT, DEC)]


OUT_SLOTS = STAGES * QC // D
CREDIT = 1


class Count:

    def __init__(self, per, r):
        self.per, self.r, self.seen = per, r, {}

    def nth(self, x, k):
        return self.r * self.per[x] + k + CREDIT

    def before(self, x):
        return self.nth(x, 0)

    def all(self, x):
        return self.nth(x, self.per[x])

    def next(self, x):
        self.seen[x] = self.seen.get(x, 0) + 1
        return self.nth(x, self.seen[x])


def semaphores(nc, ctx, name, per):
    made = {x: nc.alloc_semaphore(f"{name}_{x}") for x in per}
    sems = list(made.values())

    def give_back():
        nc.clear_and_free_semaphores(sems)
        nc.all_engine_barrier()
    ctx.callback(give_back)
    return made


def start_credits(eng, S):
    for sem in S.values():
        eng.sem_inc(sem, CREDIT)


def three(pe, out, a, b, start, stop, **kw):
    pairs = [(a[0], b[0]), (a[1], b[0]), (a[0], b[1])]
    for n, (x, y) in enumerate(pairs):
        last = pe.matmul(out, x, y, start=start and n == 0, stop=stop and n == 2, **kw)
    return last


def out_weights(h, part, k):
    return h[part][:, :, :].rearrange("p k n -> p (k n)")[:, k * D:(k + 1) * D]


def norm_phase(nc, top, name, x_in, gain, ident, h, w_in, stage):
    with ExitStack() as ctx:
        sb = lambda n, s, dt=F32: ctx.enter_context(nc.sbuf_tensor(f"{name}_{n}", s, dt))
        xt = sb("xt", [P, 2, D])
        hn = sb("hn", [P, 2, D])
        sq = sb("sq", [P, D])
        ss = sb("ss", [P, 2])
        rstd = sb("rstd", [P, 2])
        eps = sb("eps", [P, 1])
        gb = sb("gb", [P, D])
        ps = ctx.enter_context(nc.psum_tensor(f"{name}_ps", [P, 2, KT, P], F32))
        per = {"gain": 16, "x_even": 16, "x_odd": 16, "sum": 2, "log": 2, "rstd": 2, "h": 2,
            "turned": 2, "high": 2, "low": 2, "staged": 16, "fill": 1}
        S = semaphores(nc, ctx, name, per)
        loaded = ("x_even", "x_odd")
        block = ctx.enter_context(nc.Block())

        def after_first(t):
            return not isinstance(t, int) or t > 0

        def rounds(eng, front, back=None):
            def pair(i, last):
                for u in range(2):
                    front(Count(per, i + u), 2 * i + u + 1, 1 - u, DEC if last and u else P)
                    if back:
                        back(Count(per, i), 2 * i + u, u, P)
            front(Count(per, 0), 0, 0, P)
            with eng.Fori(0, NT // 2 - 1) as i:
                pair(i, False)
            pair(NT // 2 - 1, True)
            if back:
                back(Count(per, NT // 2), NT, 0, DEC)

        @block.sync
        def _(sp):
            sp.dma_start(gb[:, :], gain.to_broadcast([P, D])).then_inc(S["gain"], 16)

            def load(at, t, u, n):
                if after_first(t):
                    sp.wait_ge(S["h"], at.nth("h", u - 1))
                sp.dma_start(xt[0:n, u, :], x_in[bass.ds(t * P, n), :]).then_inc(S[loaded[u]], 16)
            rounds(sp, load)
            sp.dma_start(stage[:, :, :], w_in[0, 0:STAGES * P, :].rearrange("(k p) n -> p k n", p=P)
                         ).then_inc(S["staged"], 16)
            sp.wait_ge(S["staged"], 16 + 1)

        @block.scalar
        def _(act):
            act.preload_act_table_set("natural_log_exp_and_others")
            act.wait_ge(S["fill"], 1 + 1)

            def statistics(at, t, u, n):
                act.wait_ge(S[loaded[u]], at.nth(loaded[u], 16))
                act.activation(sq[0:n, :], xt[0:n, u, :], ACT.Square,
                               accum_out=ss[0:n, u:u + 1]).then_inc(S["sum"], 1)
                act.wait_ge(S["sum"], at.nth("sum", u + 1))
                act.activation(ss[0:n, u:u + 1], ss[0:n, u:u + 1], ACT.Ln, scale=1.0 / D,
                               bias=eps[0:n, 0:1]).then_inc(S["log"], 1)
                act.wait_ge(S["log"], at.nth("log", u + 1))
                act.activation(rstd[0:n, u:u + 1], ss[0:n, u:u + 1], ACT.Exp,
                               scale=-0.5).then_inc(S["rstd"], 1)

            def high(at, t, u, n):
                act.wait_ge(S["turned"], at.nth("turned", u + 1))
                act.activation(h[0][:, :, bass.ds(t * P, n)], ps[:, u, :, 0:n], ACT.Copy).then_inc(S["high"], 1)
            rounds(act, statistics, high)

        @block.vector
        def _(dve):
            start_credits(dve, S)
            dve.memset(eps[:, :], EPS)
            dve.drain().then_inc(S["fill"], 1)

            def scale(at, t, u, n):
                dve.wait_ge(S["rstd"], at.nth("rstd", u + 1))
                if after_first(t):
                    dve.wait_ge(S["low"], at.nth("low", u - 1))
                dve.scalar_tensor_tensor(out=hn[0:n, u, :], in0=xt[0:n, u, :], scalar=rstd[0:n, u:u + 1],
                                         in1=gb[0:n, :], op0=ALU.mult, op1=ALU.mult).then_inc(S["h"], 1)

            def low(at, t, u, n):
                dve.wait_ge(S["high"], at.nth("high", u + 1))
                cols = bass.ds(t * P, n)
                dve.tensor_tensor(h[1][:, :, cols], ps[:, u, :, 0:n], h[0][:, :, cols].bitcast(F32),
                                  ALU.subtract).then_inc(S["low"], 1)
            dve.wait_ge(S["gain"], 16 + 1)
            rounds(dve, scale, low)

        @block.tensor
        def _(pe):
            def turn(at, t, u, n):
                pe.wait_ge(S["h"], at.nth("h", u + 1))
                if after_first(t):
                    pe.wait_ge(S["low"], at.nth("low", u - 1))
                for k in range(KT):
                    last = pe.transpose(ps[:, u, k, 0:n], hn[0:n, u, k * P:(k + 1) * P], ident[0:n, 0:n])
                last.then_inc(S["turned"], 1)
            rounds(pe, turn)


def attention_layer(nc, top, name, h, w_in, k_past, v_past, k_out, v_out, o_dram, w_out, consts, stage, core):
    ident = consts["ident"]
    with ExitStack() as ctx:
        sb = lambda n, s, dt=F32: ctx.enter_context(nc.sbuf_tensor(f"{name}_{n}", s, dt))
        pb = lambda n, s: ctx.enter_context(nc.psum_tensor(f"{name}_{n}", s, F32))
        w = [sb("w_high", [P, KT, QC], F32R), sb("w_low", [P, KT, QC], F32R)]
        tok = sb("tok", [P, NT + 1, 3 * P])
        qk = [sb("qk_high", [P, 2, PADDED], F32R), sb("qk_low", [P, 2, PADDED], F32R)]
        kp = sb("kp", [P, PB, P])
        vp = sb("vp", [P, PB, P])
        kpt = [sb("kpt_high", [P, PAST], F32R), sb("kpt_low", [P, PAST], F32R)]
        gate = sb("gate", [P, ROWS])
        gtmp = sb("gtmp", [P, 2, QC])
        o = sb("o", [P, ROWS])
        pj = pb("pj", [P, 3, 512])
        acc = pb("acc", [P, 512])
        sc = pb("sc", [P, 4, 512])
        table = dict(past=32, w_high=KT, w_low=KT, tok_ready=9, pj_tok=9, turned=10, turned_high=10,
                     turned_low=10, tok_stored=64, g_ready=3, g_raw=3, g_clamped=3, g_exp=3, g_log=3,
                     g_soft=3, g_sig=3, g_done=3, pv=3,
                     o_ready=3, pe_tick=0, fill=1)
        table.update({f"w_loaded{s}": 16 * KT // STAGES for s in range(STAGES)})
        table.update({f"o_stored{c}": 16 for c in range(3)})
        table.update(out_high=0, out_low=0, **{f"out_loaded{k}": 0 for k in range(KT)})
        table.update(core.TABLE)
        S = semaphores(nc, ctx, name, table)
        rows_ready = core.ROWS
        B = dict(tok=tok, qk=qk, kpt=kpt, vp=vp, gate=gate, gtmp=gtmp, o=o, pj=pj, acc=acc, sc=sc,
                 ident=ident, **core.memory(sb))
        block = ctx.enter_context(nc.Block())

        def groups(eng, body):
            with eng.Fori(0, GROUPS - 1) as r:
                body(r, True)
            body(GROUPS - 1, False)

        def load_w(sp, g, k):
            sp.dma_start(stage[:, k % STAGES, :], w_in[bass.ds(g, 1), k * P:(k + 1) * P, :]
                         .rearrange("o p n -> p (o n)")).then_inc(S[f"w_loaded{k % STAGES}"], 16)

        def out_raw(k):
            slot = k % OUT_SLOTS
            return stage[:, :, :].rearrange("p s n -> p (s n)")[:, slot * D:(slot + 1) * D]

        def split_w_high(act, g, k):
            act.wait_ge(S[f"w_loaded{k % STAGES}"], Count(table, g).nth(f"w_loaded{k % STAGES}", 16 * (k // STAGES + 1)))
            act.activation(w[0][:, k, :], stage[:, k % STAGES, :], ACT.Copy).then_inc(S["w_high"], 1)

        def split_w_low(dve, g, k):
            dve.wait_ge(S["w_high"], Count(table, g).nth("w_high", k + 1))
            dve.tensor_tensor(w[1][:, k, :], stage[:, k % STAGES, :], w[0][:, k, :].bitcast(F32),
                              ALU.subtract).then_inc(S["w_low"], 1)

        @block.sync
        def _(sp):
            sp.wait_ge(S["fill"], 1 + 1)
            for k in range(STAGES, KT):
                sp.wait_ge(S["w_low"], k - STAGES + 1 + 1)
                load_w(sp, 0, k)

            def body(r, more):
                at = Count(table, r)
                sp.wait_ge(S["pv"], at.before("pv"))
                sp.wait_ge(S["turned_high"], at.before("turned_high"))
                for buf, past in ((kp, k_past), (vp, v_past)):
                    sp.dma_start(buf[:, :, :], past[:, bass.ds(r * P, P)].rearrange("(b p) f -> p b f", p=P)
                                 ).then_inc(S["past"], 16)
                if more:
                    for k in range(KT):
                        sp.wait_ge(S["w_low"], Count(table, r + 1).nth("w_low", k - STAGES + 1))
                        if k == STAGES:
                            send_rows(r, at)
                        load_w(sp, r + 1, k)
                else:
                    for k in range(KT):
                        if k == 0:
                            sp.wait_ge(S["w_low"], at.all("w_low"))
                        if k == OUT_SLOTS:
                            send_rows(r, at)
                        if k >= OUT_SLOTS:
                            sp.wait_ge(S["out_low"], k - OUT_SLOTS + 1 + 1)
                        sp.dma_start(out_raw(k), w_out[k * P:(k + 1) * P, :]).then_inc(S[f"out_loaded{k}"], 16)
                for c, (c0, cn) in enumerate(CHUNKS):
                    sp.wait_ge(S["o_ready"], at.next("o_ready"))
                    sp.dma_start(o_dram[bass.ds(r, 1), :, c0:c0 + cn].rearrange("o p n -> p (o n)"),
                                 o[:, c0:c0 + cn]).then_inc(S[f"o_stored{c}"], 16)

            def send_rows(r, at):
                sp.wait_ge(S[rows_ready], at.nth(rows_ready, 9))
                for n, out in ((1, k_out), (2, v_out)):
                    cols = slice(n * P, (n + 1) * P)
                    sp.dma_start(out[0:SEQ, bass.ds(r * P, P)].rearrange("(t p) f -> p t f", p=P),
                                 tok[:, 0:NT, cols]).then_inc(S["tok_stored"], 16)
                    sp.dma_start(out[SEQ:ROWS, bass.ds(r * P, P)],
                                 tok[0:DEC, NT, cols]).then_inc(S["tok_stored"], 16)
            groups(sp, body)
            sp.wait_ge(S["tok_stored"], 64 * GROUPS + 1)
            for c in range(3):
                sp.wait_ge(S[f"o_stored{c}"], 16 * GROUPS + 1)

        def turned_bank(n):
            return (acc[:, :], sc[:, 3, :], sc[:, 1, :])[n % TURN_BANKS]

        def pair_of(n):
            return turned_bank(n)[:, 0:2 * P].rearrange("p (a n) -> p a n", a=2)

        @block.scalar
        def _(act):
            act.preload_act_table_set("natural_log_exp_and_others")
            act.wait_ge(S["fill"], 1 + 1)
            for k in range(KT):
                split_w_high(act, 0, k)

            def body(r, more):
                at = Count(table, r)
                act.wait_ge(S["tok_stored"], at.before("tok_stored"))
                act.wait_ge(S["pv"], at.before("pv"))

                def turned_high(n):
                    act.wait_ge(S["turned"], at.next("turned"))
                    if n <= NT:
                        t, m = TILES[n]
                        out, src = qk[0][:, :, t * P:t * P + m], pair_of(n)[:, :, 0:m]
                    else:
                        out, src = kpt[0][:, :], turned_bank(n)
                    act.activation(out, src, ACT.Copy).then_inc(S["turned_high"], 1)

                def gate_raw(c):
                    c0, cn = CHUNKS[c]
                    act.wait_ge(S["g_ready"], at.next("g_ready"))
                    act.wait_ge(S["o_ready"], at.before("o_ready"))
                    act.activation(gate[:, c0:c0 + cn], pj[:, 2, 0:cn], ACT.Copy).then_inc(S["g_raw"], 1)

                def gate_log(c):
                    g = gtmp[:, c % 2, 0:CHUNKS[c][1]]
                    act.wait_ge(S["g_clamped"], at.next("g_clamped"))
                    act.activation(g, g, ACT.Exp, scale=-1.0).then_inc(S["g_exp"], 1)
                    act.wait_ge(S["g_exp"], at.next("g_exp"))
                    act.activation(g, g, ACT.Ln, bias=1.0).then_inc(S["g_log"], 1)

                def gate_sigmoid(c):
                    g = gtmp[:, c % 2, 0:CHUNKS[c][1]]
                    act.wait_ge(S["g_soft"], at.next("g_soft"))
                    act.activation(g, g, ACT.Exp, scale=-1.0).then_inc(S["g_sig"], 1)

                for t, n in TILES:
                    act.wait_ge(S["pj_tok"], at.next("pj_tok"))
                    act.activation(tok[0:n, t, 0:P], pj[0:n, t % 2, 0:P], ACT.Copy, scale=DH ** -0.5)
                    act.activation(tok[0:n, t, P:], pj[0:n, t % 2, P:3 * P], ACT.Copy).then_inc(S["tok_ready"], 1)
                    if t >= 2:
                        turned_high(t - 2)
                turned_high(NT - 1)
                gate_raw(0)
                turned_high(NT)
                turned_high(NT + 1)

                def next_weights(k):
                    if more:
                        if k == 0:
                            act.wait_ge(S["g_ready"], at.all("g_ready"))
                        split_w_high(act, r + 1, k)
                    else:
                        if k == 0:
                            act.wait_ge(S["g_ready"], at.all("g_ready"))
                        act.wait_ge(S[f"out_loaded{k}"], 16 + 1)
                        act.activation(out_weights(h, 0, k), out_raw(k), ACT.Copy).then_inc(S["out_high"], 1)
                core.scalar(act, at, S, B, next_weights, (gate_raw, gate_log, gate_sigmoid))
            groups(act, body)

        @block.vector
        def _(dve):
            start_credits(dve, S)
            for s in range(STAGES):
                dve.sem_inc(S[f"w_loaded{s}"], 16)
            dve.memset(qk[0][:, :, ROWS:].bitcast(F32), 0.0)
            dve.memset(qk[1][:, :, ROWS:].bitcast(F32), 0.0)
            for q in range(DEC, P, DEC):
                dve.memset(tok[q:q + DEC, NT, :], 0.0)
            core.prepare(dve, B)
            dve.drain().then_inc(S["fill"], 1)
            for k in range(KT):
                split_w_low(dve, 0, k)

            def body(r, more):
                at = Count(table, r)

                def turned_low(n):
                    dve.wait_ge(S["turned_high"], at.next("turned_high"))
                    if n <= NT:
                        t, m = TILES[n]
                        cols = slice(t * P, t * P + m)
                        out, sub, src = qk[1][:, :, cols], qk[0][:, :, cols], pair_of(n)[:, :, 0:m]
                    else:
                        out, sub, src = kpt[1][:, :], kpt[0][:, :], turned_bank(n)
                    dve.tensor_tensor(out, src, sub.bitcast(F32), ALU.subtract).then_inc(S["turned_low"], 1)

                def gate_clamp(c):
                    c0, cn = CHUNKS[c]
                    dve.wait_ge(S["g_raw"], at.next("g_raw"))
                    if c == 2:
                        dve.wait_ge(S["g_done"], at.nth("g_done", 1))
                    dve.tensor_scalar(gtmp[:, c % 2, 0:cn], gate[:, c0:c0 + cn], -SOFT_MAX, None,
                                      ALU.max).then_inc(S["g_clamped"], 1)

                def gate_soft(c):
                    c0, cn = CHUNKS[c]
                    g = gtmp[:, c % 2, 0:cn]
                    dve.wait_ge(S["g_log"], at.next("g_log"))
                    dve.scalar_tensor_tensor(out=g, in0=gate[:, c0:c0 + cn], scalar=-1.0, in1=g, op0=ALU.mult,
                                             op1=ALU.max).then_inc(S["g_soft"], 1)

                for k in range(NT + 2):
                    turned_low(k)

                def next_weights(k):
                    if more:
                        split_w_low(dve, r + 1, k)
                    else:
                        dve.wait_ge(S["out_high"], k + 1 + 1)
                        dve.tensor_tensor(out_weights(h, 1, k), out_raw(k), out_weights(h, 0, k).bitcast(F32),
                                          ALU.subtract).then_inc(S["out_low"], 1)
                core.vector(dve, at, S, B, next_weights, (gate_clamp, gate_soft))
            groups(dve, body)

        @block.gpsimd
        def _(pool):
            pool.wait_ge(S["fill"], 1 + 1)

            def body(r, more):
                at = Count(table, r)

                def gate_product(c):
                    c0, cn = CHUNKS[c]
                    g = gate[:, c0:c0 + cn]
                    pool.wait_ge(S["g_sig"], at.next("g_sig"))
                    pool.tensor_tensor(g, g, gtmp[:, c % 2, 0:cn], ALU.mult).then_inc(S["g_done"], 1)
                core.gpsimd(pool, at, S, B, gate_product)
            groups(pool, body)

        @block.tensor
        def _(pe):
            pe.wait_ge(S["fill"], 1 + 1)

            def body(r, more):
                at = Count(table, r)
                pe.wait_ge(S["w_low"], at.all("w_low"))
                pe.wait_ge(S[core.PJ_LEFT], at.before(core.PJ_LEFT))

                def project(t, n):
                    pe.wait_ge(S["tok_ready"], at.nth("tok_ready", t - 1))
                    rows = slice(t * P, t * P + n)
                    for k in range(KT):
                        last = three(pe, pj[0:n, t % 2, 0:3 * P], [x[:, k, rows] for x in h],
                                     [x[:, k, 0:3 * P] for x in w], k == 0, k == KT - 1)
                    last.then_inc(S["pj_tok"], 1)

                def turn(n):
                    if n == 0:
                        pe.wait_ge(S["o_ready"], at.before("o_ready"))
                    if n >= TURN_BANKS:
                        pe.wait_ge(S["turned_low"], at.nth("turned_low", n - TURN_BANKS + 1))
                    bank = turned_bank(n)
                    if n <= NT:
                        pe.wait_ge(S[rows_ready], at.nth(rows_ready, n + 1))
                        t, m = TILES[n]
                        if m < P:
                            pe.sem_inc(S["pe_tick"], 1)
                        for a in range(2):
                            last = pe.transpose(bank[:, a * P:a * P + m], tok[0:m, t, a * P:(a + 1) * P],
                                                ident[0:m, 0:m])
                    else:
                        pe.wait_ge(S["past"], at.nth("past", 32))
                        for b in range(PB):
                            last = pe.transpose(bank[:, b * P:(b + 1) * P], kp[:, b, :], ident[:, :])
                    last.then_inc(S["turned"], 1)

                for t, n in TILES:
                    project(t, n)
                    if t >= 2:
                        turn(t - 2)
                def gate_project(c):
                    c0, cn = CHUNKS[c]
                    if c == 0:
                        pe.wait_ge(S[core.G_LEFT], at.before(core.G_LEFT))
                    else:
                        pe.wait_ge(S["g_raw"], at.nth("g_raw", c))
                    for k in range(KT):
                        last = three(pe, pj[:, 2, 0:cn], [x[:, k, 3 * P:] for x in w],
                                     [x[:, k, c0:c0 + cn] for x in h], k == 0, k == KT - 1)
                    last.then_inc(S["g_ready"], 1)
                turn(NT - 1)
                gate_project(0)
                turn(NT)
                turn(NT + 1)
                pe.wait_ge(S["tok_ready"], at.all("tok_ready"))
                core.tensor(pe, at, S, B, gate_project)
            groups(pe, body)


class DifferentialAttention:

    UNITS = [(qb * P, P, (qb + 1) * P) for qb in range(NT)] + [(SEQ, DEC, PAST + DEC)]
    CHUNK_END = {3: 0, 7: 1, 8: 2}
    GATE_AT = (0, 3, 4)
    ROWS, PJ_LEFT, G_LEFT = "rope", "moved", "rstd"
    TABLE = dict(rope=9, pool_link=9, scores=18, neg_max=18, probs=18, weights=9, w_turned=14, moved=14,
                 squared=3, var=3, log=3, rstd=3, dve_link=34 + 27 + 3)

    def __init__(self, lam, gain, cos, sin):
        self.neg_lam, self.gain, self.cos, self.sin = lam, gain, cos, sin

    def memory(self, sb):
        return dict(p=([sb(f"p{u}0", [P, SEQ]) for u in range(3)], [sb(f"p{u}1", [P, SEQ]) for u in range(2)]),
                    wt=sb("wt", [P, NT, QC]), wt_sample=sb("wt_sample", [P, PB + 1, DEC]), mean=sb("mean", [P, P]), eps=sb("eps", [P, 1]),
                    mx=sb("mx", [P, 2, 2]), nm=sb("nm", [P, 2, 2]), sums=sb("sums", [P, 2, 2]),
                    ra=sb("ra", [P, 2, 4, 16]))

    def prepare(self, dve, B):
        dve.memset(B["mean"][:, :], 1.0 / P)
        dve.memset(B["eps"][:, :], EPS)

    def groups_of(self, u):
        if u == NT:
            return [(0, PB, P), (PB, 1, DEC)]
        return [(k, min(4, u + 1 - k), P) for k in range(0, u + 1, 4)]

    def scores_of(self, u, c, B):
        q0, n, nk = self.UNITS[u]
        first = self.bank_of(u) * 512
        return B["sc"][0:n, 2 * c:2 * c + 2, :].rearrange("p a n -> p (a n)")[:, first:first + nk]

    @staticmethod
    def bank_of(u):
        return u % 2 if u < 4 else 0

    @staticmethod
    def sums_bank(c, B):
        return B["sc"][:, 0, :] if c == 2 else B["acc"][:, :]

    @staticmethod
    def var_bank(c, B):
        return B["sc"][:, 1, :] if c == 2 else B["pj"][:, 2, :]

    def gpsimd(self, pool, at, S, B, gate_product):
        tok, ra = B["tok"], B["ra"]
        for t, n in TILES:
            pool.wait_ge(S["tok_ready"], at.next("tok_ready"))
            pool.wait_ge(S["rope"], at.nth("rope", t))
            x = tok[0:n, t, 0:2 * P].rearrange("p (c d) -> p c d", d=DH)
            xc, xs = ra[0:n, 0], ra[0:n, 1]
            pool.tensor_tensor(xc, x[:, :, 0:16], self.cos[0:n, t], ALU.mult)
            pool.tensor_tensor(xs, x[:, :, 0:16], self.sin[0:n, t], ALU.mult).then_inc(S["pool_link"], 1)
            pool.wait_ge(S["pool_link"], at.next("pool_link"))
            pool.tensor_tensor(x[:, :, 0:8], xc[:, :, 0:8], xs[:, :, 8:16], ALU.subtract)
            pool.tensor_tensor(x[:, :, 8:16], xc[:, :, 8:16], xs[:, :, 0:8], ALU.add).then_inc(S["rope"], 1)
        for c in range(3):
            gate_product(c)

    def tensor(self, pe, at, S, B, gate_project):
        sc, pj, acc, wt, p = B["sc"], B["pj"], B["acc"], B["wt"], B["p"]
        ring = [0]

        def score(u, c):
            q0, n, nk = self.UNITS[u]
            if u >= 4:
                pe.wait_ge(S["probs"], at.nth("probs", 2 * (u - 1) + c + 1))
            elif u >= 2:
                pe.wait_ge(S["probs"], at.nth("probs", 2 * (u - 2) + c + 1))
            else:
                pe.wait_ge(S["probs"], at.before("probs"))
                pe.wait_ge(S["turned_low"], at.nth("turned_low", NT + 1 if u else 1))
            if n < P:
                pe.sem_inc(S["pe_tick"], 1)
            f = slice(c * DH, (c + 1) * DH)
            keys = [([x[f, 0:PAST] for x in B["kpt"]], 0, PAST), ([x[f, 1, SEQ:ROWS] for x in B["qk"]], PAST, DEC)
                    ] if u == NT else [([x[f, 1, k:min(k + 512, nk)] for x in B["qk"]], k, min(512, nk - k))
                                       for k in range(0, nk, 512)]
            for rhs, k, kn in keys:
                last = three(pe, sc[0:n, 2 * c + self.bank_of(u) + k // 512, k % 512:k % 512 + kn],
                             [x[f, 0, q0:q0 + n] for x in B["qk"]], rhs, True, True)
            last.then_inc(S["scores"], 1)

        def turn_weights(u):
            q0, n, nk = self.UNITS[u]
            pe.wait_ge(S["weights"], at.nth("weights", u + 1))
            for k0, nb, rows in self.groups_of(u):
                if ring[0] >= 2:
                    pe.wait_ge(S["moved"], at.nth("moved", ring[0] - 1))
                if n < P:
                    pe.sem_inc(S["pe_tick"], 1)
                bank = pj[0:rows, ring[0] % 2, 0:nb * n].rearrange("p (b n) -> p b n", n=n)
                for b in range(nb):
                    k = (k0 + b) * P
                    last = pe.transpose(bank[:, b, :], p[0][u % 3][0:n, k:k + rows], B["ident"][0:n, 0:n])
                last.then_inc(S["w_turned"], 1)
                ring[0] += 1

        def values(c):
            c0, cn = CHUNKS[c]
            if c == 0:
                pe.wait_ge(S["turned_low"], at.all("turned_low"))
                pe.wait_ge(S["o_ready"], at.before("o_ready"))
            elif c == 1:
                pe.wait_ge(S["o_ready"], at.nth("o_ready", 1))
            else:
                pe.wait_ge(S["probs"], at.all("probs"))
            pe.wait_ge(S["moved"], at.nth("moved", sum(len(self.groups_of(u)) for u in range({0: 4, 1: 8, 2: 9}[c]))))
            out = self.sums_bank(c, B)
            if c == 2:
                for b in range(PB):
                    pe.matmul(out[:, 0:cn], B["vp"][:, b, :], B["wt_sample"][:, b, :], start=b == 0, stop=False)
                last = pe.matmul(out[:, 0:cn], B["tok"][0:DEC, NT, 2 * P:], B["wt_sample"][0:DEC, PB, :],
                                 start=False, stop=True)
            else:
                blocks = 4 * (c + 1)
                for b in range(blocks):
                    q = max(0, b * P - c0)
                    last = pe.matmul(out[:, q:], B["tok"][:, b, 2 * P:], wt[:, b, q:],
                                     start=b == 0, stop=b == blocks - 1)
            last.then_inc(S["pv"], 1)

        def variance(c):
            cn = CHUNKS[c][1]
            pe.wait_ge(S["squared"], at.next("squared"))
            if c == 0:
                pe.wait_ge(S["g_raw"], at.all("g_raw"))
            elif c == 1:
                pe.wait_ge(S["rstd"], at.nth("rstd", 1))
            pe.matmul(self.var_bank(c, B)[:, 0:cn], B["mean"][:, :], B["gtmp"][:, c % 2, 0:cn], start=True,
                      stop=True).then_inc(S["var"], 1)

        for u in range(NT + 1):
            for c in range(2):
                score(u, c)
            if u - 3 in self.CHUNK_END:
                values(self.CHUNK_END[u - 3])
            if u >= 2:
                turn_weights(u - 2)
            if u in self.GATE_AT[1:]:
                gate_project(self.GATE_AT.index(u))
            if u == 7:
                variance(0)
        turn_weights(NT - 1)
        values(1)
        turn_weights(NT)
        values(2)
        variance(1)
        variance(2)

    def scalar(self, act, at, S, B, next_weights, gate):
        p, sc, wt = B["p"], B["sc"], B["wt"]
        gate_raw, gate_log, gate_sigmoid = gate
        ring = [0]

        def probs(u, c):
            q0, n, nk = self.UNITS[u]
            if u >= 3:
                act.wait_ge(S["w_turned"], at.nth("w_turned", sum(len(self.groups_of(x)) for x in range(u - 2))))
            act.wait_ge(S["neg_max"], at.next("neg_max"))
            act.activation(p[c][u % (3 - c)][0:n, 0:nk], self.scores_of(u, c, B),
                                  ACT.Exp, bias=B["nm"][0:n, u % 2, c:c + 1],
                                  accum_out=B["sums"][0:n, u % 2, c:c + 1]).then_inc(S["probs"], 1)

        def move(u):
            q0, n, nk = self.UNITS[u]
            if u == 4:
                act.wait_ge(S["pv"], at.nth("pv", 1))
            off = q0 % QC
            for k0, nb, rows in self.groups_of(u):
                act.wait_ge(S["w_turned"], at.next("w_turned"))
                bank = B["pj"][0:rows, ring[0] % 2, 0:nb * n].rearrange("p (b n) -> p b n", n=n)
                out = B["wt_sample"][0:rows, k0:k0 + nb, :] if u == NT else wt[0:rows, k0:k0 + nb, off:off + n]
                act.activation(out, bank, ACT.Copy).then_inc(S["moved"], 1)
                ring[0] += 1

        def square(c):
            cn = CHUNKS[c][1]
            act.wait_ge(S["pv"], at.next("pv"))
            act.wait_ge(S["g_done"], at.all("g_done"))
            act.activation(B["gtmp"][:, c % 2, 0:cn], self.sums_bank(c, B)[:, 0:cn], ACT.Square).then_inc(S["squared"], 1)

        def norm(c):
            c0, cn = CHUNKS[c]
            act.wait_ge(S["var"], at.next("var"))
            act.wait_ge(S[f"o_stored{c}"], at.before(f"o_stored{c}"))
            r = B["o"][:, c0:c0 + cn]
            act.activation(r, self.var_bank(c, B)[:, 0:cn], ACT.Ln, bias=B["eps"][:, 0:1]).then_inc(S["log"], 1)
            act.wait_ge(S["log"], at.next("log"))
            act.activation(r, r, ACT.Exp, scale=-0.5).then_inc(S["rstd"], 1)

        for u in range(NT + 1):
            if u == NT:
                move(u - 2)
                move(u - 1)
            for c in range(2):
                probs(u, c)
            if 2 <= u < NT:
                move(u - 2)
            if u - 2 in self.GATE_AT:
                gate_sigmoid(self.GATE_AT.index(u - 2))
            if u - 1 in self.GATE_AT:
                gate_log(self.GATE_AT.index(u - 1))
            if u in self.GATE_AT[1:]:
                gate_raw(self.GATE_AT.index(u))
            if u in (5, 6):
                next_weights(2 * (u - 5))
                next_weights(2 * (u - 5) + 1)
            if u == NT:
                for k in range(4, KT):
                    next_weights(k)
            if u == 6:
                square(0)
            if u == 7:
                norm(0)
        square(1)
        move(NT)
        square(2)
        norm(1)
        norm(2)

    def vector(self, dve, at, S, B, next_weights, gate):
        sc, p, mx, nm, sums = B["sc"], B["p"], B["mx"], B["nm"], B["sums"]

        def maxima(u, c):
            q0, n, nk = self.UNITS[u]
            dve.wait_ge(S["scores"], at.next("scores"))
            s = self.scores_of(u, c, B)
            if u < NT:
                dve.memset(s[0:CHUNK, nk - CHUNK:nk], NEG).then_inc(S["dve_link"], 1)
                dve.wait_ge(S["dve_link"], at.next("dve_link"))
            dve.reduce_max(mx[0:n, u % 2, c:c + 1], s, AX.X).then_inc(S["dve_link"], 1)
            dve.wait_ge(S["dve_link"], at.next("dve_link"))
            dve.tensor_scalar(nm[0:n, u % 2, c:c + 1], mx[0:n, u % 2, c:c + 1], -1.0, None, ALU.mult).then_inc(S["neg_max"], 1)

        def combine(u):
            q0, n, nk = self.UNITS[u]
            dve.wait_ge(S["probs"], at.next("probs"))
            dve.wait_ge(S["probs"], at.next("probs"))
            s, a, b = sums[0:n, u % 2], p[0][u % 3][0:n, 0:nk], p[1][u % 2][0:n, 0:nk]
            dve.reciprocal(s, s).then_inc(S["dve_link"], 1)
            dve.wait_ge(S["dve_link"], at.next("dve_link"))
            dve.tensor_scalar(s[:, 1:2], s[:, 1:2], self.neg_lam[0:n, 0:1], None, ALU.mult).then_inc(S["dve_link"], 1)
            dve.wait_ge(S["dve_link"], at.next("dve_link"))
            dve.tensor_scalar(b, b, s[:, 1:2], None, ALU.mult).then_inc(S["dve_link"], 1)
            dve.wait_ge(S["dve_link"], at.next("dve_link"))
            dve.scalar_tensor_tensor(out=a, in0=a, scalar=s[:, 0:1], in1=b, op0=ALU.mult, op1=ALU.add).then_inc(S["weights"], 1)

        def finish(c):
            c0, cn = CHUNKS[c]
            out = B["o"][:, c0:c0 + cn]
            dve.wait_ge(S["rstd"], at.next("rstd"))
            dve.wait_ge(S["g_done"], at.nth("g_done", c + 1))
            dve.tensor_tensor(out, self.sums_bank(c, B)[:, 0:cn], out, ALU.mult).then_inc(S["dve_link"], 1)
            dve.wait_ge(S["dve_link"], at.next("dve_link"))
            dve.scalar_tensor_tensor(out=out, in0=out, scalar=self.gain[:, 0:1],
                                            in1=B["gate"][:, c0:c0 + cn], op0=ALU.mult, op1=ALU.mult).then_inc(S["o_ready"], 1)

        gate_clamp, gate_soft = gate
        for u in range(NT + 1):
            if u == NT:
                combine(u - 1)
                finish(0)
            for c in range(2):
                maxima(u, c)
            if 1 <= u < NT:
                combine(u - 1)
            if u - 2 in self.GATE_AT:
                gate_soft(self.GATE_AT.index(u - 2))
            if u - 1 in self.GATE_AT:
                gate_clamp(self.GATE_AT.index(u - 1))
            if u == 6:
                next_weights(0)
                next_weights(1)
        for k in range(2, 6):
            next_weights(k)
        combine(NT)
        next_weights(KT - 2)
        next_weights(KT - 1)
        finish(1)
        finish(2)


class StickBreaking:

    UNITS = [(c, b, hd) for c in range(2) for b in reversed(range(4 * (c + 1))) for hd in range(2)] + [(2, 0, 0)]
    N = len(UNITS)
    SLOTS = 4
    GATE_AT = (-2, 1, 5)
    WEIGHTS_AT = range(7, 7 + 2 * KT, 2)
    SB = PB + 1
    SN = SB * DEC
    ROWS, PJ_LEFT, G_LEFT = "tok_ready", "pv", "g_raw"
    DIAG = sum(c < 2 and b >= 4 * c for c, b, _ in UNITS)
    TABLE = dict(z=N, clamped=N, exp=N, log=N, soft=N, after=N, a=N, running=24 - 4, r_zero=2, dve_link=DIAG + 5)

    def __init__(self, masks):
        self.masks = masks

    def memory(self, sb):
        return dict(m=[sb(f"m{i}", [P, QC]) for i in range(3)], s=[sb(f"s{i}", [P, QC]) for i in range(4)],
                    a=[sb(f"a{i}", [P, QC]) for i in range(4)], r=sb("r", [P, 2, 2, QC]),
                    rs=sb("rs", [P, 2, PB, DEC]), hide=sb("hide", [P, P], F32R),
                    unit=sb("unit", [P, P], F32R))

    def prepare(self, dve, B):
        dve.tensor_scalar(B["hide"][:, :], self.masks["strict"][:, :], -1.0, -NEG, ALU.add, ALU.mult)
        dve.tensor_copy(B["unit"][:, :], B["ident"][:, :])

    def span(self, s):
        c, b, hd = self.UNITS[s]
        q = max(0, b * P - c * QC)
        return q, QC - q, b >= 4 * c

    def views(self, s, B):
        if self.UNITS[s][0] == 2:
            first = s % self.SLOTS
            assert first + 1 < self.SLOTS
            wide = lambda x: x[:, 0:2 * self.SN].rearrange("p (h n) -> p h n", h=2)
            return B["sc"][:, first:first + 2, 0:self.SN], wide(B["m"][s % 3]), wide(B["s"][s % 4]), wide(B["a"][s % 4])
        q, n, _ = self.span(s)
        return tuple(x[:, q:q + n] for x in (B["sc"][:, s % self.SLOTS, :], B["m"][s % 3], B["s"][s % 4], B["a"][s % 4]))

    def last_of(self, c):
        return max(s for s, x in enumerate(self.UNITS) if x[0] == c)

    def running_before(self, s):
        return sum(self.UNITS[x][0] < 2 and self.UNITS[x][1] > 0 for x in range(s))

    def tensor(self, pe, at, S, B, gate_project):
        sc, acc, qk = B["sc"], B["acc"], B["qk"]
        tri, ones = self.masks["neg_tri"], self.masks["neg_ones"]

        def scores(s):
            c, b, hd = self.UNITS[s]
            slot = sc[:, s % self.SLOTS, :]
            if s >= self.SLOTS:
                pe.wait_ge(S["a"], at.nth("a", s - self.SLOTS + 1 + (c == 2)))
            else:
                pe.wait_ge(S["a"], at.before("a"))
                pe.wait_ge(S["turned_low"], at.nth("turned_low", NT + 1 if s else 4))
            if c == 2:
                for b in range(self.SB):
                    for hd in range(2):
                        f = slice(hd * DH, (hd + 1) * DH)
                        keys = [x[f, b * P:(b + 1) * P] for x in B["kpt"]] if b < PB else [x[f, 1, SEQ:] for x in qk]
                        last = three(pe, self.views(s, B)[0][:, hd, b * DEC:(b + 1) * DEC], keys,
                                     [x[f, 0, SEQ:ROWS] for x in qk], b == 0, True, skip_group_check=True)
            else:
                q, n, _ = self.span(s)
                f = slice(hd * DH, (hd + 1) * DH)
                c0 = c * QC
                last = three(pe, slot[:, q:], [x[f, 1, b * P:(b + 1) * P] for x in qk],
                             [x[f, 0, c0 + q:c0 + QC] for x in qk], True, True, skip_group_check=True)
            last.then_inc(S["z"], 1)

        def after(s):
            c, b, hd = self.UNITS[s]
            slot, _, sp, _ = self.views(s, B)
            add = dict(start=False, stop=True, skip_group_check=True)
            pe.wait_ge(S["soft"], at.nth("soft", s + 1))
            if c == 2:
                for hd in range(2):
                    pe.matmul(slot[:, hd, PB * DEC:], B["unit"][:, :], B["hide"][:, 0:DEC], **add)
                    pe.matmul(slot[:, hd, 0:PB * DEC], ones[:, :], B["rs"][:, hd].rearrange("p b n -> p (b n)"), **add)
                    last = pe.matmul(slot[:, hd, :], tri[:, :], sp[:, hd, :], **add)
            else:
                q, n, masked = self.span(s)
                if masked:
                    pe.matmul(slot[:, 0:P], B["unit"][:, :], B["hide"][:, :], **add)
                if b < 4 * c + 3:
                    pe.wait_ge(S["running"], at.nth("running", self.running_before(s - 1)))
                    pe.matmul(slot, ones[:, :], B["r"][:, c, hd, q:], **add)
                last = pe.matmul(slot, tri[:, :], sp, **add)
            last.then_inc(S["after"], 1)

        def values(s):
            c, b, hd = self.UNITS[s]
            a = B["a"][s % 4]
            pe.wait_ge(S["a"], at.nth("a", s + 1))
            if s in (0, self.last_of(0) + 1, self.last_of(1) + 1):
                if c == 0:
                    pe.wait_ge(S["turned_low"], at.all("turned_low"))
                    pe.wait_ge(S["o_ready"], at.before("o_ready"))
                else:
                    pe.wait_ge(S["o_ready"], at.nth("o_ready", c))
            if c == 2:
                for b in range(self.SB):
                    for hd in range(2):
                        f = slice(hd * DH, (hd + 1) * DH)
                        v = B["vp"][:, b, f] if b < PB else B["tok"][:, NT, 2 * P + hd * DH:2 * P + (hd + 1) * DH]
                        col = hd * self.SN + b * DEC
                        last = pe.matmul(acc[f, 0:DEC], v, a[:, col:col + DEC], start=b == 0,
                                         stop=b == PB, skip_group_check=True)
            else:
                q = self.span(s)[0]
                f = slice(hd * DH, (hd + 1) * DH)
                last = pe.matmul(acc[f, q:], B["tok"][:, b, 2 * P + hd * DH:2 * P + (hd + 1) * DH], a[:, q:],
                                 start=b == 4 * c + 3, stop=b == 0, skip_group_check=True)
            if s == self.last_of(c):
                last.then_inc(S["pv"], 1)

        for s in range(self.N + 3):
            if s < self.N:
                scores(s)
            if 2 <= s < self.N + 2:
                after(s - 2)
            if s >= 3:
                values(s - 3)
            if s in self.GATE_AT:
                gate_project(self.GATE_AT.index(s))

    def scalar(self, act, at, S, B, next_weights, gate):
        gate_raw, gate_log, gate_sigmoid = gate
        for s in range(self.N + 2):
            if s < self.N:
                m = self.views(s, B)[1]
                act.wait_ge(S["clamped"], at.next("clamped"))
                act.activation(m, m, ACT.Exp).then_inc(S["exp"], 1)
                act.wait_ge(S["exp"], at.next("exp"))
                act.activation(m, m, ACT.Ln, bias=1.0).then_inc(S["log"], 1)
            if s >= 2:
                j = s - 2
                slot, _, _, a = self.views(j, B)
                act.wait_ge(S["after"], at.next("after"))
                act.activation(a, slot, ACT.Exp).then_inc(S["a"], 1)
            if s - 1 in self.GATE_AT:
                gate_raw(self.GATE_AT.index(s - 1))
            if s - 3 in self.GATE_AT:
                gate_log(self.GATE_AT.index(s - 3))
            if s - 5 in self.GATE_AT:
                gate_sigmoid(self.GATE_AT.index(s - 5))
            if s in self.WEIGHTS_AT:
                next_weights(self.WEIGHTS_AT.index(s))

    def vector(self, dve, at, S, B, next_weights, gate):
        strict, strict_sample = self.masks["strict"], self.masks["strict_sample"]
        gate_clamp, gate_soft = gate
        dve.wait_ge(S["running"], at.before("running"))
        dve.wait_ge(S["after"], at.before("after"))
        for c in range(2):
            dve.memset(B["r"][:, c, :, :], 0.0).then_inc(S["r_zero"], 1)

        def softplus(s):
            c = self.UNITS[s][0]
            masked = c == 2 or self.span(s)[2]
            slot, m, sp, _ = self.views(s, B)
            dve.wait_ge(S["log"], at.next("log"))
            if s >= 4:
                dve.wait_ge(S["after"], at.nth("after", s - 3))
                dve.wait_ge(S["running"], at.nth("running", self.running_before(s - 3)))
            ins = dve.tensor_tensor(sp, slot, m, ALU.max)
            if not masked:
                ins.then_inc(S["soft"], 1)
            elif c < 2:
                ins.then_inc(S["dve_link"], 1)
                dve.wait_ge(S["dve_link"], at.next("dve_link"))
                dve.tensor_tensor(sp[:, 0:P], sp[:, 0:P], strict[:, :], ALU.mult).then_inc(S["soft"], 1)
            else:
                ins.then_inc(S["dve_link"], 1)
                dve.wait_ge(S["dve_link"], at.next("dve_link"))
                new = sp[:, :, PB * DEC:]
                dve.tensor_tensor(new, new, strict_sample[:, :, :], ALU.mult).then_inc(S["dve_link"], 1)
                dve.wait_ge(S["dve_link"], at.next("dve_link"))
                rs = B["rs"]
                dve.tensor_copy(rs[:, :, PB - 1, :], new).then_inc(S["dve_link"], 1)
                dve.wait_ge(S["dve_link"], at.next("dve_link"))
                for b in reversed(range(PB - 1)):
                    ins = dve.tensor_tensor(rs[:, :, b, :], rs[:, :, b + 1, :], sp[:, :, (b + 1) * DEC:(b + 2) * DEC],
                                            ALU.add)
                    if b:
                        ins.then_inc(S["dve_link"], 1)
                        dve.wait_ge(S["dve_link"], at.next("dve_link"))
                    else:
                        ins.then_inc(S["soft"], 1)

        def finish(c):
            c0, cn = CHUNKS[c]
            dve.wait_ge(S["pv"], at.next("pv"))
            dve.wait_ge(S["g_done"], at.nth("g_done", c + 1))
            dve.wait_ge(S[f"o_stored{c}"], at.before(f"o_stored{c}"))
            dve.tensor_tensor(B["o"][:, c0:c0 + cn], B["acc"][:, 0:cn], B["gate"][:, c0:c0 + cn], ALU.mult).then_inc(S["o_ready"], 1)

        for s in range(self.N + 4):
            if s < self.N:
                slot, m, _, _ = self.views(s, B)
                dve.wait_ge(S["z"], at.next("z"))
                if s >= 3:
                    dve.wait_ge(S["soft"], at.nth("soft", s - 2))
                else:
                    dve.wait_ge(S["soft"], at.before("soft"))
                dve.tensor_scalar(m, slot, SOFT_MAX, None, ALU.min).then_inc(S["clamped"], 1)
            if 1 <= s <= self.N:
                softplus(s - 1)
            for c in range(3):
                if s - 3 == self.last_of(c):
                    finish(c)
            if s - 2 in self.GATE_AT:
                gate_clamp(self.GATE_AT.index(s - 2))
            if s - 4 in self.GATE_AT:
                gate_soft(self.GATE_AT.index(s - 4))
            if s - 1 in self.WEIGHTS_AT:
                next_weights(self.WEIGHTS_AT.index(s - 1))

    def gpsimd(self, pool, at, S, B, gate_product):
        pool.wait_ge(S["r_zero"], at.all("r_zero"))
        for s, (c, b, hd) in enumerate(self.UNITS):
            if c < 2 and b > 0:
                q = self.span(s)[0]
                pool.wait_ge(S["soft"], at.nth("soft", s + 1))
                pool.wait_ge(S["after"], at.nth("after", s + 1))
                r = B["r"][:, c, hd, q:]
                pool.tensor_tensor(r, r, B["s"][s % 4][:, q:], ALU.add).then_inc(S["running"], 1)
            if s - 5 in self.GATE_AT:
                gate_product(self.GATE_AT.index(s - 5))


def mix_phase(nc, top, name, x_in, x_out, o_dram, p_in, w_gate, w_proj, ident, h,
              final_gain=None):
    with ExitStack() as ctx:
        sb = lambda n, s, dt=F32: ctx.enter_context(nc.sbuf_tensor(f"{name}_{n}", s, dt))
        pb = lambda n, s: ctx.enter_context(nc.psum_tensor(f"{name}_{n}", s, F32))
        NW = PT + KT
        TILE_0_AT = 3
        w = [sb("w_high", [P, NW, D], F32R), sb("w_low", [P, NW, D], F32R)]
        stage = sb("stage", [P, 2, D])
        xt, x1, xo, sig = sb("xt", [P, D]), sb("x1", [P, D]), sb("xo", [P, D]), sb("sig", [P, D])
        pt = sb("pt", [P, PLE])
        if final_gain is not None:
            gb, yo = sb("gb", [P, D]), sb("yo", [P, D])
            ss, rstd, eps = sb("ss", [P, 1]), sb("rstd", [P, 1]), sb("eps", [P, 1])
        ot = sb("ot", [P, KT, P])
        os_ = [sb("o_high", [P, KT, P], F32R), sb("o_low", [P, KT, P], F32R)]
        xs = [sb("x_high", [P, KT, P], F32R), sb("x_low", [P, KT, P], F32R)]
        ps_ = [sb("p_high", [P, PT, P], F32R), sb("p_low", [P, PT, P], F32R)]
        y, xtr, gt, pp = (pb(n, [P, 2, 512]) for n in ("y", "xtr", "gt", "pp"))
        flat = lambda b, n: b[0:n, :, :].rearrange("p a n -> p (a n)")
        per = dict(
            w_even=16, w_odd=16, w_high=NW, w_low=NW, o_loaded=16, x_loaded=16, p_loaded=16, o_high=1,
            o_low=1, y=1, x1=1, p_turned=1, turned=1, p_high=1, p_low=1, x_high=1, x_low=1, mixed=1, clamped=1, exp=1,
            log=1, soft=1, sig=1, copied=1,
            x_out=1, stored=16, link=1, gain=16, sum=1, square_log=1, rstd=1, normed=1, fill=1)
        S = semaphores(nc, ctx, name, per)
        block = ctx.enter_context(nc.Block())

        def rounds(eng, tile):
            tile(0, P)
            with eng.Fori(1, NT) as t:
                tile(t, P)
            tile(NT, DEC)

        def done(x, t):
            return (t + 1) * per[x] + CREDIT

        @block.sync
        def _(sp):
            sp.wait_ge(S["fill"], 1 + 1)

            def load_o(t, n):
                sp.wait_ge(S["o_low"], done("o_low", t - 1))
                rows = bass.ds(t * P, n)
                sp.dma_start(ot[:, :, 0:n], o_dram[:, :, rows].rearrange("k p n -> p k n")).then_inc(S["o_loaded"], 16)

            def load_x(t, n):
                rows = bass.ds(t * P, n)
                sp.wait_ge(S["turned"], done("turned", t - 1))
                sp.dma_start(pt[0:n, :], p_in[rows, :]).then_inc(S["p_loaded"], 16)
                sp.dma_start(xt[0:n, :], x_in[rows, :]).then_inc(S["x_loaded"], 16)

            blocks = [m[k * P:(k + 1) * P, :] for m, count in ((w_proj, PT), (w_gate, KT))
                      for k in range(count)]
            load_o(0, P)
            load_x(0, P)
            if final_gain is not None:
                sp.dma_start(gb[:, :], final_gain.to_broadcast([P, D])).then_inc(S["gain"], 16)
            for k, src in enumerate(blocks):
                if k >= 2:
                    sp.wait_ge(S["w_low"], k - 1 + 1)
                sp.dma_start(stage[:, k % 2, :], src).then_inc(S["w_odd" if k % 2 else "w_even"], 16)
                if k == TILE_0_AT:
                    load_o(1, P)
                if k == 2 * TILE_0_AT:
                    load_x(1, P)
            with sp.Fori(2, NT) as t:
                load_o(t, P)
                load_x(t, P)
            load_o(NT, DEC)
            load_x(NT, DEC)

        @block.scalar
        def _(act):
            act.preload_act_table_set("natural_log_exp_and_others")
            act.wait_ge(S["fill"], 1 + 1)

            def o_high(t, n):
                act.wait_ge(S["o_loaded"], done("o_loaded", t))
                act.wait_ge(S["y"], done("y", t - 1))
                act.activation(os_[0][:, :, 0:n], ot[:, :, 0:n], ACT.Copy).then_inc(S["o_high"], 1)

            def sigmoid(t, n):
                v = sig[0:n, :]
                act.wait_ge(S["clamped"], done("clamped", t))
                act.activation(v, v, ACT.Exp, scale=-1.0).then_inc(S["exp"], 1)
                act.wait_ge(S["exp"], done("exp", t))
                act.activation(v, v, ACT.Ln, bias=1.0).then_inc(S["log"], 1)
                act.wait_ge(S["soft"], done("soft", t))
                act.activation(v, v, ACT.Exp, scale=-1.0).then_inc(S["sig"], 1)

            def send(t, n):
                act.wait_ge(S["x_out"], done("x_out", t))
                act.dma_start(x_out[bass.ds(t * P, n), :], xo[0:n, :]).then_inc(S["stored"], 16)

            def statistics(t, n):
                act.wait_ge(S["x_out"], done("x_out", t))
                act.wait_ge(S["stored"], done("stored", t - 1))
                act.activation(yo[0:n, :], xo[0:n, :], ACT.Square, accum_out=ss[0:n, :]).then_inc(S["sum"], 1)
                act.wait_ge(S["sum"], done("sum", t))
                act.activation(ss[0:n, :], ss[0:n, :], ACT.Ln, scale=1.0 / D,
                               bias=eps[0:n, 0:1]).then_inc(S["square_log"], 1)
                act.wait_ge(S["square_log"], done("square_log", t))
                act.activation(rstd[0:n, :], ss[0:n, :], ACT.Exp, scale=-0.5).then_inc(S["rstd"], 1)

            def send_normed(t, n):
                act.wait_ge(S["normed"], done("normed", t))
                act.dma_start(x_out[bass.ds(t * P, n), :], yo[0:n, :]).then_inc(S["stored"], 16)

            def tile(t, n, first=False, last=False):
                if not last:
                    o_high(t + 1, DEC if isinstance(t, int) and t == NT - 1 else P)
                act.wait_ge(S["p_turned"], done("p_turned", t))
                act.activation(ps_[0][:, :, 0:n], y[:, 0, 0:2 * P].rearrange("p (k n) -> p k n", n=P)[:, :, 0:n],
                               ACT.Copy).then_inc(S["p_high"], 1)
                act.wait_ge(S["turned"], done("turned", t))
                act.activation(xs[0][:, :, 0:n], xtr[:, :, :].rearrange("p a (k n) -> p (a k) n", n=P)[:, :, 0:n],
                               ACT.Copy).then_inc(S["x_high"], 1)
                if not first:
                    sigmoid(t - 1, P)
                    if final_gain is None:
                        send(t - 1, P)
                    else:
                        statistics(t - 1, P)
                        send_normed(t - 1, P)
                act.wait_ge(S["x1"], done("x1", t))
                if final_gain is None:
                    act.wait_ge(S["stored"], done("stored", t - 1))
                act.activation(xo[0:n, :], x1[0:n, :], ACT.Copy).then_inc(S["copied"], 1)

            o_high(0, P)
            for k in range(NW):
                act.wait_ge(S["w_odd" if k % 2 else "w_even"], 16 * (k // 2 + 1) + 1)
                act.activation(w[0][:, k, :], stage[:, k % 2, :], ACT.Copy).then_inc(S["w_high"], 1)
                if k == TILE_0_AT:
                    tile(0, P, first=True)
            with act.Fori(1, NT - 1) as t:
                tile(t, P)
            tile(NT - 1, P)
            tile(NT, DEC, last=True)
            sigmoid(NT, DEC)
            if final_gain is None:
                send(NT, DEC)
            else:
                statistics(NT, DEC)
                send_normed(NT, DEC)
            act.wait_ge(S["stored"], done("stored", NT))

        @block.vector
        def _(dve):
            start_credits(dve, S)
            if final_gain is not None:
                dve.memset(eps[:, :], EPS)
            dve.drain().then_inc(S["fill"], 1)

            def o_low(t, n):
                dve.wait_ge(S["o_high"], done("o_high", t))
                dve.tensor_tensor(os_[1][:, :, 0:n], ot[:, :, 0:n], os_[0][:, :, 0:n].bitcast(F32),
                                  ALU.subtract).then_inc(S["o_low"], 1)

            def residual(t, n):
                dve.wait_ge(S["y"], done("y", t))
                dve.wait_ge(S["x_loaded"], done("x_loaded", t))
                dve.wait_ge(S["copied"], done("copied", t - 1))
                dve.tensor_tensor(x1[0:n, :], xt[0:n, :], flat(y, n), ALU.add).then_inc(S["x1"], 1)

            def finish(t, n):
                at = Count(per, t)
                v = sig[0:n, :]
                dve.wait_ge(S["mixed"], done("mixed", t))
                dve.wait_ge(S["x_out"], done("x_out", t - 1))
                dve.tensor_scalar(v, flat(gt, n), -SOFT_MAX, None, ALU.max).then_inc(S["clamped"], 1)
                dve.wait_ge(S["log"], done("log", t))
                dve.scalar_tensor_tensor(out=v, in0=flat(gt, n), scalar=-1.0, in1=v, op0=ALU.mult,
                                         op1=ALU.max).then_inc(S["soft"], 1)
                dve.wait_ge(S["sig"], done("sig", t))
                dve.tensor_tensor(v, flat(pp, n), v, ALU.mult).then_inc(S["link"], 1)
                dve.wait_ge(S["link"], at.next("link"))
                dve.wait_ge(S["copied"], done("copied", t))
                dve.tensor_tensor(xo[0:n, :], xo[0:n, :], v, ALU.add).then_inc(S["x_out"], 1)
                if final_gain is not None:
                    dve.wait_ge(S["rstd"], done("rstd", t))
                    dve.wait_ge(S["gain"], 16 + 1)
                    dve.scalar_tensor_tensor(out=yo[0:n, :], in0=xo[0:n, :], scalar=rstd[0:n, 0:1], in1=gb[0:n, :],
                                             op0=ALU.mult, op1=ALU.mult).then_inc(S["normed"], 1)

            def x_low(t, n):
                dve.wait_ge(S["p_high"], done("p_high", t))
                dve.tensor_tensor(ps_[1][:, :, 0:n], y[:, 0, 0:2 * P].rearrange("p (k n) -> p k n", n=P)[:, :, 0:n],
                                  ps_[0][:, :, 0:n].bitcast(F32), ALU.subtract).then_inc(S["p_low"], 1)
                dve.wait_ge(S["x_high"], done("x_high", t))
                dve.tensor_tensor(xs[1][:, :, 0:n], xtr[:, :, :].rearrange("p a (k n) -> p (a k) n", n=P)[:, :, 0:n],
                                  xs[0][:, :, 0:n].bitcast(F32), ALU.subtract).then_inc(S["x_low"], 1)

            def tile(t, n, first=False, last=False):
                residual(t, n)
                if not last:
                    o_low(t + 1, DEC if isinstance(t, int) and t == NT - 1 else P)
                x_low(t, n)
                if not first:
                    finish(t - 1, P)

            o_low(0, P)
            for k in range(NW):
                dve.wait_ge(S["w_high"], k + 1 + 1)
                dve.tensor_tensor(w[1][:, k, :], stage[:, k % 2, :], w[0][:, k, :].bitcast(F32),
                                  ALU.subtract).then_inc(S["w_low"], 1)
                if k == TILE_0_AT:
                    tile(0, P, first=True)
            with dve.Fori(1, NT - 1) as t:
                tile(t, P)
            tile(NT - 1, P)
            tile(NT, DEC, last=True)
            finish(NT, DEC)

        @block.tensor
        def _(pe):
            def product(out, n, parts, weights, blocks, split_first=None):
                for half in range(2):
                    for k in range(blocks):
                        if split_first is not None and half == 0:
                            pe.wait_ge(S["w_low"], split_first + k + 1 + 1)
                        last = three(pe, out[0:n, half, :], [x[:, k, 0:n] for x in parts],
                                     [weights(part, k)[:, half * 512:(half + 1) * 512] for part in range(2)],
                                     k == 0, k == blocks - 1)
                return last

            w_proj_block = lambda part, k: w[part][:, k, :]
            w_gate_block = lambda part, k: w[part][:, PT + k, :]

            def out_product(t, n):
                pe.wait_ge(S["o_low"], done("o_low", t))
                pe.wait_ge(S["p_low"], done("p_low", t - 1))
                product(y, n, os_, lambda part, k: out_weights(h, part, k), KT).then_inc(S["y"], 1)

            def mix(t, n, first=False):
                pe.wait_ge(S["x_low"], done("x_low", t))
                pe.wait_ge(S["x_out"], done("x_out", t - 1))
                product(pp, n, ps_, w_proj_block, PT, 0 if first else None)
                product(gt, n, xs, w_gate_block, KT, PT if first else None).then_inc(S["mixed"], 1)

            def turn(t, n):
                pe.wait_ge(S["x1"], done("x1", t))
                pe.wait_ge(S["p_loaded"], done("p_loaded", t))
                for k in range(PT):
                    last = pe.transpose(y[:, 0, k * P:k * P + n], pt[0:n, k * P:(k + 1) * P], ident[0:n, 0:n])
                last.then_inc(S["p_turned"], 1)
                for k in range(KT):
                    last = pe.transpose(xtr[:, k // 4, k % 4 * P:k % 4 * P + n], x1[0:n, k * P:(k + 1) * P],
                                        ident[0:n, 0:n])
                last.then_inc(S["turned"], 1)

            out_product(0, P)
            turn(0, P)
            out_product(1, P)
            mix(0, P, first=True)
            turn(1, P)
            with pe.Fori(2, NT) as t:
                out_product(t, P)
                mix(t - 1, P)
                turn(t, P)
            out_product(NT, DEC)
            mix(NT - 1, P)
            turn(NT, DEC)
            mix(NT, DEC)


def start_phase(nc, top, tables, lams, sub_gain, neg_lam, gain):
    lam_init = 0.8 - 0.6 * math.exp(-0.3 * 0)
    with ExitStack() as ctx:
        sb = lambda n, s: ctx.enter_context(nc.sbuf_tensor(f"lam_{n}", s, F32))
        rows, prod, dots = sb("rows", [P, 4, DH]), sb("prod", [P, 2, DH]), sb("dots", [P, 2])
        loaded, step, es, placed = (top.enter_context(nc.semaphore(f"lam_{n}"))
                                    for n in ("loaded", "step", "exp", "placed"))
        block = ctx.enter_context(nc.Block())

        @block.sync
        def _(sp):
            for n, row in enumerate(lams):
                sp.dma_start(rows[:, n, :], row.to_broadcast([P, DH])).then_inc(loaded, 16)
            sp.dma_start(gain[:, :], sub_gain.rearrange("o p -> p o")).then_inc(loaded, 16)
            for dst, src in tables:
                sp.dma_start(dst, src).then_inc(placed, 16)
            sp.wait_ge(placed, 16 * len(tables))

        @block.scalar
        def _(act):
            act.preload_act_table_set("natural_log_exp_and_others")
            act.wait_ge(step, 2)
            act.activation(dots[:, :], dots[:, :], ACT.Exp).then_inc(es, 1)

        @block.vector
        def _(dve):
            dve.wait_ge(loaded, 80)
            dve.tensor_scalar(gain[:, :], gain[:, :], 1.0 - lam_init, None, ALU.mult)
            dve.tensor_tensor(prod[:, :, :], rows[:, 0::2, :], rows[:, 1::2, :], ALU.mult).then_inc(step, 1)
            dve.wait_ge(step, 1)
            dve.reduce_sum(dots[:, :], prod[:, :, :], AX.X).then_inc(step, 1)
            dve.wait_ge(es, 1)
            dve.tensor_scalar(neg_lam[:, :], dots[:, 1:2], dots[:, 0:1], -lam_init, ALU.subtract, ALU.add)


def build(nc, A, out):
    y, ak, av, bk, bv = out
    top = ExitStack()
    with top:
        internal = lambda n, s: nc.dram_tensor(n, s, F32, kind="Internal").ap()
        x_mid = internal("x_mid", (ROWS, D))
        o_dram = internal("o_t", (GROUPS, P, ROWS))
        ident = top.enter_context(nc.sbuf_tensor("ident", [P, P], F32))
        masks = {n: top.enter_context(nc.sbuf_tensor(n, s, F32)) for n, s in
                 (("neg_tri", [P, P]), ("neg_ones", [P, P]), ("strict", [P, P]), ("strict_sample", [P, 2, DEC]))}
        h = [top.enter_context(nc.sbuf_tensor(f"h_{n}", [P, KT, ROWS], F32R)) for n in ("high", "low")]

        with ExitStack() as a:
            sb = lambda n, s: a.enter_context(nc.sbuf_tensor(n, s, F32))
            cos, sin = sb("cos", [P, NT + 1, 4, 16]), sb("sin", [P, NT + 1, 4, 16])
            neg_lam, gain = sb("neg_lam", [P, 1]), sb("sub_gain", [P, 1])
            tables = [(ident[:, :], A["c_ident"]), (cos[:, :, :, :], A["c_cos"]), (sin[:, :, :, :], A["c_sin"])]
            tables += [(m[:], A[f"c_{n}"]) for n, m in masks.items()]
            start_phase(nc, top, tables, [A[f"a_lam_{n}"] for n in ("q1", "k1", "q2", "k2")], A["a_subln_g"],
                        neg_lam, gain)
            stage = sb("stage_a", [P, STAGES, QC])
            norm_phase(nc, top, "norm_a", A["x"], A["a_norm_g"], ident, h, A["a_w_in"], stage)
            attention_layer(nc, top, "la", h, A["a_w_in"], A["cache_a_k"], A["cache_a_v"], ak, av, o_dram, A["a_w_out"],
                            dict(ident=ident), stage, DifferentialAttention(neg_lam, gain, cos, sin))
        mix_phase(nc, top, "mix_a", A["x"], x_mid, o_dram, A["p"][0], A["ple_w_gate"][0],
                  A["ple_w_proj"][0], ident, h)
        with ExitStack() as b:
            stage = b.enter_context(nc.sbuf_tensor("stage_b", [P, STAGES, QC], F32))
            norm_phase(nc, top, "norm_b", x_mid, A["b_norm_g"], ident, h, A["b_w_in"], stage)
            attention_layer(nc, top, "lb", h, A["b_w_in"], A["cache_b_k"], A["cache_b_v"], bk, bv, o_dram,
                            A["b_w_out"], dict(ident=ident), stage, StickBreaking(masks))
        mix_phase(nc, top, "mix_b", x_mid, y, o_dram, A["p"][1], A["ple_w_gate"][1],
                  A["ple_w_proj"][1], ident, h, final_gain=A["final_norm_g"])


def constants():
    half, theta = DH // 8, 500000.0
    inv = np.float32(theta) ** (-np.arange(half, dtype=np.float32) * np.float32(2.0) / np.float32(DH // 4))
    pos = np.zeros(PADDED, np.float32)
    pos[:SEQ] = np.arange(SEQ)
    pos[SEQ:ROWS] = PAST + np.arange(DEC)
    ang = (pos[:, None] * inv[None, :]).astype(np.float32)
    wide = lambda a: np.ascontiguousarray(
        np.tile(a.astype(np.float32), (1, 8)).reshape(NT + 1, P, 4, 16).transpose(1, 0, 2, 3))
    i = np.arange(P)
    strict = (i[:, None] < i[None, :]).astype(np.float32)
    return {"c_cos": wide(np.cos(ang)), "c_sin": wide(np.sin(ang)), "c_ident": np.eye(P, dtype=np.float32),
            "c_neg_tri": -(i[:, None] >= i[None, :]).astype(np.float32),
            "c_neg_ones": np.full((P, P), -1.0, np.float32), "c_strict": strict,
            "c_strict_sample": np.ascontiguousarray(np.tile(strict[:, None, :DEC], (1, 2, 1)))}


def kernel(**inputs):
    import concourse.bacc as bacc
    from concourse.bass_utils import run_bass_kernel_spmd

    a = {k: np.asarray(v) for k, v in inputs.items()}
    by_group = lambda w: w.reshape(D, 4, GROUPS, P).transpose(2, 0, 1, 3).reshape(GROUPS, D, 4 * P)
    arrays = {
        "x": np.concatenate([a["x_prompt"][0], a["x_sample"][0]]),
        "p": np.concatenate([a["p_prompt"][:, 0], a["p_sample"][:, 0]], axis=1),
        "a_w_in": by_group(a["a_w_in"][0]), "b_w_in": by_group(a["b_w_in"][0]),
        "a_w_out": a["a_w_out"][0], "b_w_out": a["b_w_out"][0],
        "ple_w_gate": a["ple_w_gate"], "ple_w_proj": a["ple_w_proj"],
        "a_norm_g": a["a_norm_g"], "b_norm_g": a["b_norm_g"], "a_subln_g": a["a_subln_g"],
        "final_norm_g": a["final_norm_g"].reshape(1, D),
        **{f"a_lam_{n}": a[f"a_lam_{n}"] for n in ("q1", "k1", "q2", "k2")},
        **{n: a[n].reshape(PAST, D) for n in ("cache_a_k", "cache_a_v", "cache_b_k", "cache_b_v")},
        **constants(),
    }
    nc = bacc.Bacc("TRN2", target_bir_lowering=False, num_devices=1)
    arrays = {k: np.ascontiguousarray(v) for k, v in arrays.items()}
    A = {k: nc.dram_tensor(f"in_{k}", v.shape, F32, kind="ExternalInput").ap() for k, v in arrays.items()}
    names = ["y", "ak", "av", "bk", "bv"]
    out = [nc.dram_tensor(f"out_{n}", (ROWS, D), F32, kind="ExternalOutput").ap() for n in names]
    build(nc, A, out)
    r = run_bass_kernel_spmd(nc, [{f"in_{k}": v for k, v in arrays.items()}], core_ids=[0]).results[0]
    y, ak, av, bk, bv = (r[f"out_{n}"] for n in names)
    p_, s_ = slice(0, SEQ), slice(SEQ, ROWS)
    shape = {"ak": (8, 2, DH), "av": (8, 2 * DH), "bk": (16, DH), "bv": (16, DH)}
    cut = lambda arr, n, rows: arr[rows].reshape(1, 1, -1, *shape[n])
    return (y[p_].reshape(1, SEQ, D), y[s_].reshape(1, DEC, D),
            cut(ak, "ak", p_), cut(av, "av", p_), cut(bk, "bk", p_), cut(bv, "bv", p_),
            cut(ak, "ak", s_), cut(av, "av", s_), cut(bk, "bk", s_), cut(bv, "bv", s_))
```
